# Optimizing a Trainium2 kernel written in Bass

```python
import math
import numpy as np
import jax
import jax.numpy as jnp
from jax import lax

D_MODEL = 1024
BATCH = 1
SEQ = 512
DEPTH = 2
DEC_BATCH = 8
DEC_SEQ = 4
PAST_LEN = 4096
PAGE_SIZE = 128

MIX_WIDTH = D_MODEL
GROUP_WIDTH = MIX_WIDTH // 4
CONV_CH = GROUP_WIDTH
CONV_WIDTH = 31
POOL_CH = GROUP_WIDTH
POOL_WINDOWS = (2, 4, 8, 16)
POOL_GROUP = POOL_CH // len(POOL_WINDOWS)
POOL_BUF = max(POOL_WINDOWS) - 1
ATT_HEADS = 4
ATT_KV_HEADS = 2
ATT_GROUP = ATT_HEADS // ATT_KV_HEADS
HEAD_DIM = GROUP_WIDTH // ATT_HEADS
ATT_SCALE = HEAD_DIM ** -0.5
CMP_BLOCK = 32
CMP_STRIDE = 16
SEL_BLOCK = 64
SEL_TOPN = 16
WINDOW = 512
SEL_QBLOCK = 16
WIN_QBLOCK = 128
N_BUCKETS = 32
MAX_DISTANCE = 128
GDN_HEADS = 4
GDN_DK = GROUP_WIDTH // GDN_HEADS
GDN_DV = GROUP_WIDTH // GDN_HEADS
GDN_QKV = GDN_HEADS * (2 * GDN_DK + GDN_DV)
GDN_CONV = 4
GDN_CHUNK = 64
D_FF = 4 * D_MODEL
DN_ALPHA = (2 * DEPTH) ** 0.25
DN_BETA = (8 * DEPTH) ** -0.25
LN_EPS = 1e-5
NEG = -1e30
FORCE = 1e4
SPLITS = (2 * CONV_CH, POOL_CH, ATT_HEADS * HEAD_DIM, 6 * ATT_KV_HEADS * HEAD_DIM, 3 * ATT_HEADS,
          GDN_QKV, GDN_HEADS * GDN_DV, GDN_HEADS, GDN_HEADS)
IN_WIDTH = sum(SPLITS)
F32 = jnp.float32

kernel_name = 'hymba_conv_pool_nsa_gdn_decoder_step'

def split_cols(h, sizes):
    out, start = [], 0
    for s in sizes:
        out.append(h[..., start:start + s])
        start += s
    return out

def layer_norm(x, g, b):
    xf = x.astype(F32)
    mu = xf.mean(-1, keepdims=True)
    var = jnp.square(xf - mu).mean(-1, keepdims=True)
    return ((xf - mu) * lax.rsqrt(var + LN_EPS) * g + b).astype(x.dtype)

def rms_norm(x, g):
    xf = x.astype(F32)
    return xf * lax.rsqrt(jnp.square(xf).mean(-1, keepdims=True) + LN_EPS) * g

def l2_normalize(x):
    return x * lax.rsqrt(jnp.sum(jnp.square(x), -1, keepdims=True) + 1e-6)

def masked_softmax(s, mask):
    s = jnp.where(mask, s.astype(F32), NEG)
    e = jnp.where(mask, jnp.exp(s - s.max(-1, keepdims=True)), 0.0)
    return e / jnp.maximum(e.sum(-1, keepdims=True), 1e-30)

def causal_dwconv(u, w):
    return lax.conv_general_dilated(u, w[:, None, :].astype(u.dtype), (1,), 'VALID',
                                    dimension_numbers=('NWC', 'WIO', 'NWC'),
                                    feature_group_count=u.shape[-1])

def t5_bucket(d):
    d = jnp.maximum(d, 0)
    exact = N_BUCKETS // 2
    logd = jnp.log(jnp.maximum(d, 1).astype(F32) / exact) / math.log(MAX_DISTANCE / exact)
    large = jnp.minimum(exact + (logd * (N_BUCKETS - exact)).astype(jnp.int32), N_BUCKETS - 1)
    return jnp.where(d < exact, d, large)

def head_bias(rel_bias, d):
    b = rel_bias[t5_bucket(d)].astype(F32)
    return jnp.moveaxis(b, -1, 0).reshape((ATT_KV_HEADS, ATT_GROUP) + d.shape)

def conformer_conv(h, buf, dw, dw_b, ln_g, ln_b, pw):
    u = h[..., :CONV_CH] * jax.nn.sigmoid(h[..., CONV_CH:])
    full = jnp.concatenate([buf.astype(u.dtype), u], axis=1)
    y = causal_dwconv(full, dw) + dw_b
    y = jax.nn.silu(layer_norm(y, ln_g, ln_b))
    return y @ pw, full[:, -(CONV_WIDTH - 1):]

def pool_mixer(h, buf, offset, pool_w, pool_scale):
    B, T, C = h.shape
    u = jnp.concatenate([buf.astype(h.dtype), h], axis=1)
    uf = u.astype(F32)
    cs = jnp.concatenate([jnp.zeros((B, 1, C), F32), jnp.cumsum(uf, axis=1)], axis=1)
    hi = cs[:, POOL_BUF + 1:POOL_BUF + 1 + T]
    pos = offset + jnp.arange(T)
    parts = []
    for gi, w in enumerate(POOL_WINDOWS):
        sl = slice(gi * POOL_GROUP, (gi + 1) * POOL_GROUP)
        lo = cs[:, POOL_BUF + 1 - w:POOL_BUF + 1 - w + T, sl]
        cnt = jnp.minimum(pos + 1, w).astype(F32)[None, :, None]
        parts.append((hi[..., sl] - lo) / cnt - uf[:, POOL_BUF:, sl])
    d = jnp.stack(parts, axis=2)
    y = jnp.einsum('btgc,gcd->btgd', d, pool_w.astype(F32)).reshape(B, T, C) * pool_scale
    return y, u[:, -POOL_BUF:]

def compress_blocks(kseq, pe, w1, w2):
    B, L, KH, HD = kseq.shape
    nc = -(-L // CMP_STRIDE)
    kp = jnp.pad(kseq, ((0, 0), (0, nc * CMP_STRIDE - L), (0, 0), (0, 0)))
    ch = kp.reshape(B, nc, CMP_STRIDE, KH, HD).transpose(0, 1, 3, 2, 4).reshape(B, nc, KH, CMP_STRIDE * HD)
    half = CMP_STRIDE * HD
    ha = ch @ w1[:half]
    hb = ch @ w1[half:]
    h = ha[:, :-1] + hb[:, 1:] + pe.reshape(-1) @ w1
    return jax.nn.silu(h) @ w2

def nsa_selected(qg, k_sel, v_sel, top_idx, top_ok, qpos, rel_bias):
    B, T, KH, G, HD = qg.shape
    L = k_sel.shape[1]
    n_sel = -(-L // SEL_BLOCK)
    padw = ((0, 0), (0, n_sel * SEL_BLOCK - L), (0, 0), (0, 0))
    kt = jnp.pad(k_sel, padw).transpose(0, 2, 1, 3)
    vt = jnp.pad(v_sel, padw).transpose(0, 2, 1, 3)
    n = top_idx.shape[-1]
    qb = math.gcd(T, SEL_QBLOCK)
    nb = T // qb
    bi = jnp.arange(B)[:, None, None, None]
    hi = jnp.arange(KH)[None, :, None, None]
    bias_tab = rel_bias.reshape(N_BUCKETS, KH, G)

    def block(args):
        q_b, idx, ok, pb = args
        tok = (idx[..., None] * SEL_BLOCK + jnp.arange(SEL_BLOCK)).reshape(B, KH, qb, n * SEL_BLOCK)
        okt = jnp.repeat(ok, SEL_BLOCK, axis=-1)
        kg = kt[bi, hi, tok]
        vg = vt[bi, hi, tok]
        d = pb[None, None, :, None] - tok
        mask = okt & (d >= 0)
        bias = jnp.moveaxis(bias_tab[t5_bucket(d), hi].astype(F32), -1, 2)
        s = jnp.einsum('bqkgd,bkqmd->bkgqm', q_b, kg).astype(F32) * ATT_SCALE + bias
        p = masked_softmax(s, mask[:, :, None])
        return jnp.einsum('bkgqm,bkqmd->bqkgd', p, vg.astype(F32))

    xs = (qg.reshape(B, nb, qb, KH, G, HD).swapaxes(0, 1),
          jnp.moveaxis(top_idx.reshape(B, KH, nb, qb, n), 2, 0),
          jnp.moveaxis(top_ok.reshape(B, KH, nb, qb, n), 2, 0),
          qpos.reshape(nb, qb))
    o = lax.map(block, xs)
    return o.swapaxes(0, 1).reshape(B, T, KH, G, HD)

def nsa_window(qg, kw_all, key_pos0, qpos, rel_bias):
    B, T, KH, G, HD = qg.shape
    Lk = kw_all.shape[1]
    Pw = Lk - T
    qb = math.gcd(T, WIN_QBLOCK)
    nb = T // qb
    band = WINDOW - 1 + qb
    kw_pad = jnp.pad(kw_all, ((0, 0), (WINDOW - 1, 0), (0, 0), (0, 0), (0, 0)))
    kpos = key_pos0 - (WINDOW - 1) + jnp.arange(Lk + WINDOW - 1)
    real = jnp.arange(Lk + WINDOW - 1) >= WINDOW - 1

    def block(args):
        q_b, start, pb = args
        kv = lax.dynamic_slice_in_dim(kw_pad, start, band, axis=1)
        kp = lax.dynamic_slice_in_dim(kpos, start, band)
        rl = lax.dynamic_slice_in_dim(real, start, band)
        d = pb[:, None] - kp[None, :]
        mask = rl[None, :] & (d >= 0) & (d < WINDOW)
        s = jnp.einsum('bqkgd,bmkd->bkgqm', q_b, kv[:, :, 0]).astype(F32) * ATT_SCALE + head_bias(rel_bias, d)
        p = masked_softmax(s, mask)
        return jnp.einsum('bkgqm,bmkd->bqkgd', p, kv[:, :, 1].astype(F32))

    xs = (qg.reshape(B, nb, qb, KH, G, HD).swapaxes(0, 1), Pw + jnp.arange(nb) * qb, qpos.reshape(nb, qb))
    o = lax.map(block, xs)
    return o.swapaxes(0, 1).reshape(B, T, KH, G, HD)

def nsa_mixer(q, kv_new, gate_logits, past, win_buf, cmp_pe, cmp_w1, cmp_w2, rel_bias):
    B, T = q.shape[:2]
    offset = past[0].shape[1]
    L = offset + T
    qpos = offset + jnp.arange(T)
    qg = q.reshape(B, T, ATT_KV_HEADS, ATT_GROUP, HEAD_DIM)
    k_cmp, v_cmp, k_sel, v_sel = [jnp.concatenate([past[c].astype(kv_new.dtype), kv_new[:, :, c]], axis=1)
                                  for c in range(4)]
    kc = compress_blocks(k_cmp, cmp_pe[0], cmp_w1[0], cmp_w2[0])
    vc = compress_blocks(v_cmp, cmp_pe[1], cmp_w1[1], cmp_w2[1])
    cmp_start = jnp.arange(kc.shape[1]) * CMP_STRIDE
    d_cmp = qpos[:, None] - (cmp_start + CMP_BLOCK - 1)[None, :]
    s = jnp.einsum('btkgd,bnkd->bkgtn', qg, kc).astype(F32) * ATT_SCALE + head_bias(rel_bias, d_cmp)
    p_cmp = masked_softmax(s, d_cmp >= 0)
    o_cmp = jnp.einsum('bkgtn,bnkd->btkgd', p_cmp, vc.astype(F32))
    n_sel = -(-L // SEL_BLOCK)
    sel_start = jnp.arange(n_sel) * SEL_BLOCK
    cover = ((cmp_start[:, None] < sel_start[None, :] + SEL_BLOCK)
             & (cmp_start[:, None] + CMP_BLOCK > sel_start[None, :])).astype(F32)
    imp = jnp.einsum('bkgtn,nj->bktj', p_cmp, cover)
    cur = (qpos // SEL_BLOCK)[:, None]
    j = jnp.arange(n_sel)[None, :]
    forced = (j == 0) | (j == cur) | (j == cur - 1)
    avail = sel_start[None, :] <= qpos[:, None]
    score = jnp.where(avail, imp + jnp.where(forced, FORCE, 0.0), NEG)
    top_val, top_idx = lax.top_k(score, min(SEL_TOPN, n_sel))
    top_ok = top_val > 0.5 * NEG
    o_sel = nsa_selected(qg, k_sel, v_sel, top_idx, top_ok, qpos, rel_bias)
    kw_all = jnp.concatenate([win_buf.astype(kv_new.dtype), kv_new[:, :, 4:]], axis=1)
    o_win = nsa_window(qg, kw_all, offset - win_buf.shape[1], qpos, rel_bias)
    gates = jax.nn.sigmoid(gate_logits.astype(F32)).reshape(B, T, 3, ATT_KV_HEADS, ATT_GROUP, 1)
    o = gates[:, :, 0] * o_cmp + gates[:, :, 1] * o_sel + gates[:, :, 2] * o_win
    return o.reshape(B, T, ATT_HEADS * HEAD_DIM), kw_all[:, -min(WINDOW, kw_all.shape[1]):]

def chunk_gated_delta(q, k, v, g, beta, S0):
    B, T, H, dk = q.shape
    dv = v.shape[-1]
    C = min(GDN_CHUNK, T)
    n = -(-T // C)
    pad = n * C - T

    def prep(a):
        a = jnp.pad(a, ((0, 0), (0, pad)) + ((0, 0),) * (a.ndim - 2))
        return jnp.moveaxis(a.reshape((B, n, C) + a.shape[2:]), (1, 3), (0, 2))

    qc, kc, vc, gc, bc = prep(q), prep(k), prep(v), prep(g), prep(beta)
    gcum = jnp.cumsum(gc, axis=-1)
    incl = jnp.tril(jnp.ones((C, C), bool))
    strict = jnp.tril(jnp.ones((C, C), bool), -1)
    decay = jnp.exp(jnp.where(incl, gcum[..., :, None] - gcum[..., None, :], NEG))
    kb = kc * bc[..., None]
    lower = jnp.where(strict, jnp.einsum('...id,...jd->...ij', kb, kc) * decay, 0.0)
    A = lower + jnp.eye(C, dtype=F32)
    u_val = lax.linalg.triangular_solve(A, vc * bc[..., None], left_side=True, lower=True, unit_diagonal=True)
    w_dec = lax.linalg.triangular_solve(A, kb * jnp.exp(gcum)[..., None], left_side=True, lower=True,
                                        unit_diagonal=True)
    qk = jnp.einsum('...id,...jd->...ij', qc, kc) * decay

    def step(S, xs):
        qi, ki, ui, wi, qki, gi = xs
        vnew = ui - wi @ S
        o = (qi * jnp.exp(gi)[..., None]) @ S + qki @ vnew
        g_last = gi[..., -1:]
        S = S * jnp.exp(g_last)[..., None] + jnp.einsum('bhcd,bhce->bhde', ki * jnp.exp(g_last - gi)[..., None], vnew)
        return S, o

    S, o = lax.scan(step, S0, (qc, kc, u_val, w_dec, qk, gcum))
    o = jnp.moveaxis(o, (0, 2), (1, 3)).reshape(B, n * C, H, dv)[:, :T]
    return o, S

def gdn_mixer(qkv, z, a, b, conv_buf, S0, conv_w, a_log, dt_bias, norm_g):
    B, T = qkv.shape[:2]
    u = jnp.concatenate([conv_buf.astype(qkv.dtype), qkv], axis=1)
    c = jax.nn.silu(causal_dwconv(u, conv_w).astype(F32))
    q, k, v = split_cols(c, (GDN_HEADS * GDN_DK, GDN_HEADS * GDN_DK, GDN_HEADS * GDN_DV))
    q = l2_normalize(q.reshape(B, T, GDN_HEADS, GDN_DK)) * GDN_DK ** -0.5
    k = l2_normalize(k.reshape(B, T, GDN_HEADS, GDN_DK))
    v = v.reshape(B, T, GDN_HEADS, GDN_DV)
    g = -jnp.exp(a_log.astype(F32)) * jax.nn.softplus(a.astype(F32) + dt_bias)
    beta = jax.nn.sigmoid(b.astype(F32))
    o, S = chunk_gated_delta(q, k, v, g, beta, S0.astype(F32))
    o = rms_norm(o, norm_g) * jax.nn.silu(z.astype(F32)).reshape(B, T, GDN_HEADS, GDN_DV)
    return o.reshape(B, T, GDN_HEADS * GDN_DV), u[:, -(GDN_CONV - 1):], S

def decoder_layer(x, past, win_buf, conv_buf, pool_buf, gdn_buf, gdn_S,
                  w_in, conv_dw, conv_dw_b, conv_ln_g, conv_ln_b, conv_pw, pool_w, pool_scale,
                  cmp_pe, cmp_w1, cmp_w2, gdn_conv_w, gdn_a_log, gdn_dt_bias, gdn_norm_g,
                  w_out, ln1_g, ln1_b, w_up, w_down, ln2_g, ln2_b, rel_bias):
    B, T, _ = x.shape
    offset = past[0].shape[1]
    h = x @ w_in
    h_conv, h_pool, a_q, a_kv, a_gate, d_qkv, d_z, d_a, d_b = split_cols(h, SPLITS)
    y_conv, conv_new = conformer_conv(h_conv, conv_buf, conv_dw, conv_dw_b, conv_ln_g, conv_ln_b, conv_pw)
    y_pool, pool_new = pool_mixer(h_pool, pool_buf, offset, pool_w, pool_scale)
    kv_new = a_kv.reshape(B, T, 6, ATT_KV_HEADS, HEAD_DIM)
    y_att, win_new = nsa_mixer(a_q, kv_new, a_gate, past, win_buf, cmp_pe, cmp_w1, cmp_w2, rel_bias)
    y_gdn, gdn_buf_new, S_new = gdn_mixer(d_qkv, d_z, d_a, d_b, gdn_buf, gdn_S, gdn_conv_w, gdn_a_log,
                                          gdn_dt_bias, gdn_norm_g)
    mix = jnp.concatenate([y_conv.astype(F32), y_pool, y_att, y_gdn], axis=-1).astype(x.dtype) @ w_out
    x1 = layer_norm(DN_ALPHA * x + mix, ln1_g, ln1_b)
    f = jnp.square(jax.nn.relu(x1 @ w_up)) @ w_down
    x2 = layer_norm(DN_ALPHA * x1 + f, ln2_g, ln2_b)
    return x2, kv_new[:, :, :4], win_new, conv_new, pool_new, gdn_buf_new, S_new

def setup_inputs(seed: int = 0) -> dict:
    key = jax.random.key(seed)
    ks = list(jax.random.split(key, 40))

    def nrm(i, shape, scale):
        return jax.random.normal(ks[i], shape, F32) * scale

    n_pages = PAST_LEN // PAGE_SIZE
    n_pool = (DEC_BATCH * n_pages * 5) // 4
    wbuf = min(WINDOW, PAST_LEN)
    page_table = jax.random.permutation(ks[8], n_pool)[:DEC_BATCH * n_pages].astype(jnp.int32).reshape(DEC_BATCH, n_pages)
    dt = jnp.exp(jax.random.uniform(ks[21], (DEPTH, GDN_HEADS), F32, math.log(1e-3), math.log(1e-1)))
    return {
        'x_prompt': nrm(0, (BATCH, SEQ, D_MODEL), 1.0),
        'x_sample': nrm(1, (DEC_BATCH, DEC_SEQ, D_MODEL), 1.0),
        'cache_nsa_kv': nrm(2, (DEPTH, n_pool, PAGE_SIZE, 4, ATT_KV_HEADS, HEAD_DIM), 1.0),
        'cache_win_kv': nrm(3, (DEPTH, DEC_BATCH, wbuf, 2, ATT_KV_HEADS, HEAD_DIM), 1.0),
        'state_conv': nrm(4, (DEPTH, DEC_BATCH, CONV_WIDTH - 1, CONV_CH), 0.5),
        'state_pool': nrm(5, (DEPTH, DEC_BATCH, POOL_BUF, POOL_CH), 1.0),
        'state_gdn_conv': nrm(6, (DEPTH, DEC_BATCH, GDN_CONV - 1, GDN_QKV), 1.0),
        'state_gdn': nrm(7, (DEPTH, DEC_BATCH, GDN_HEADS, GDN_DK, GDN_DV), 0.1),
        'page_table': page_table,
        'w_in': nrm(9, (DEPTH, D_MODEL, IN_WIDTH), D_MODEL ** -0.5),
        'conv_dw': nrm(10, (DEPTH, CONV_WIDTH, CONV_CH), CONV_WIDTH ** -0.5),
        'conv_dw_b': nrm(11, (DEPTH, CONV_CH), 0.02),
        'conv_ln_g': 1.0 + nrm(12, (DEPTH, CONV_CH), 0.05),
        'conv_ln_b': nrm(13, (DEPTH, CONV_CH), 0.02),
        'conv_pw': nrm(14, (DEPTH, CONV_CH, CONV_CH), CONV_CH ** -0.5),
        'pool_w': nrm(15, (DEPTH, len(POOL_WINDOWS), POOL_GROUP, POOL_GROUP), POOL_GROUP ** -0.5),
        'pool_scale': 1.0 + nrm(16, (DEPTH, POOL_CH), 0.1),
        'cmp_pe': nrm(17, (DEPTH, 2, CMP_BLOCK, HEAD_DIM), 0.1),
        'cmp_w1': nrm(18, (DEPTH, 2, CMP_BLOCK * HEAD_DIM, HEAD_DIM), (CMP_BLOCK * HEAD_DIM) ** -0.5),
        'cmp_w2': nrm(19, (DEPTH, 2, HEAD_DIM, HEAD_DIM), HEAD_DIM ** -0.5),
        'gdn_conv_w': nrm(20, (DEPTH, GDN_CONV, GDN_QKV), GDN_CONV ** -0.5),
        'gdn_a_log': jnp.log(jax.random.uniform(ks[22], (DEPTH, GDN_HEADS), F32, 1.0, 16.0)),
        'gdn_dt_bias': dt + jnp.log(-jnp.expm1(-dt)),
        'gdn_norm_g': 1.0 + nrm(23, (DEPTH, GDN_DV), 0.05),
        'w_out': nrm(24, (DEPTH, MIX_WIDTH, D_MODEL), MIX_WIDTH ** -0.5 * DN_BETA),
        'ln1_g': 1.0 + nrm(25, (DEPTH, D_MODEL), 0.05),
        'ln1_b': nrm(26, (DEPTH, D_MODEL), 0.02),
        'w_up': nrm(27, (DEPTH, D_MODEL, D_FF), D_MODEL ** -0.5),
        'w_down': nrm(28, (DEPTH, D_FF, D_MODEL), D_FF ** -0.5 * DN_BETA),
        'ln2_g': 1.0 + nrm(29, (DEPTH, D_MODEL), 0.05),
        'ln2_b': nrm(30, (DEPTH, D_MODEL), 0.02),
        'rel_bias': nrm(31, (N_BUCKETS, ATT_HEADS), 0.5),
    }

def reference(x_prompt, x_sample, cache_nsa_kv, cache_win_kv, state_conv, state_pool, state_gdn_conv, state_gdn,
              page_table, w_in, conv_dw, conv_dw_b, conv_ln_g, conv_ln_b, conv_pw, pool_w, pool_scale,
              cmp_pe, cmp_w1, cmp_w2, gdn_conv_w, gdn_a_log, gdn_dt_bias, gdn_norm_g,
              w_out, ln1_g, ln1_b, w_up, w_down, ln2_g, ln2_b, rel_bias):
    per_layer = (w_in, conv_dw, conv_dw_b, conv_ln_g, conv_ln_b, conv_pw, pool_w, pool_scale,
                 cmp_pe, cmp_w1, cmp_w2, gdn_conv_w, gdn_a_log, gdn_dt_bias, gdn_norm_g,
                 w_out, ln1_g, ln1_b, w_up, w_down, ln2_g, ln2_b)
    bp, dtp = x_prompt.shape[0], x_prompt.dtype
    db = x_sample.shape[0]
    n_pages = page_table.shape[1]
    page = cache_nsa_kv.shape[2]
    yp, ys = x_prompt, x_sample
    new_p = [[] for _ in range(6)]
    new_s = [[] for _ in range(6)]
    for l in range(DEPTH):
        lw = [w[l] for w in per_layer] + [rel_bias]
        past_p = tuple(jnp.zeros((bp, 0, ATT_KV_HEADS, HEAD_DIM), dtp) for _ in range(4))
        yp, *st_p = decoder_layer(
            yp, past_p, jnp.zeros((bp, 0, 2, ATT_KV_HEADS, HEAD_DIM), dtp),
            jnp.zeros((bp, CONV_WIDTH - 1, CONV_CH), dtp), jnp.zeros((bp, POOL_BUF, POOL_CH), dtp),
            jnp.zeros((bp, GDN_CONV - 1, GDN_QKV), dtp), jnp.zeros((bp, GDN_HEADS, GDN_DK, GDN_DV), F32), *lw)
        past_s = tuple(jnp.take(cache_nsa_kv[l, :, :, c], page_table, axis=0).reshape(
            db, n_pages * page, ATT_KV_HEADS, HEAD_DIM) for c in range(4))
        ys, *st_s = decoder_layer(ys, past_s, cache_win_kv[l], state_conv[l], state_pool[l],
                                  state_gdn_conv[l], state_gdn[l], *lw)
        for lst, arr in zip(new_p, st_p):
            lst.append(arr)
        for lst, arr in zip(new_s, st_s):
            lst.append(arr)
    p_nsa = jnp.stack(new_p[0]).reshape(DEPTH, -1, page, 4, ATT_KV_HEADS, HEAD_DIM)
    p_win, p_conv, p_pool, p_gconv, p_gdn = [jnp.stack(a) for a in new_p[1:]]
    s_nsa, s_win, s_conv, s_pool, s_gconv, s_gdn = [jnp.stack(a) for a in new_s]
    return (yp, ys, p_nsa, p_win, p_conv, p_pool, p_gconv, p_gdn, s_nsa, s_win, s_conv, s_pool, s_gconv, s_gdn)


_drawn_inputs = setup_inputs


def setup_inputs(seed=0):
    import zlib

    import numpy as np

    out = dict(_drawn_inputs(seed))
    spreads = {}
    factors = {'cache_nsa_kv': 6.062,
     'conv_dw_b': 8.0,
     'conv_ln_g': 6.416,
     'conv_ln_b': 8.0,
     'cmp_pe': 8.0,
     'gdn_norm_g': 6.833,
     'rel_bias': 3.358}
    for name, (base, spread) in spreads.items():
        noise = np.random.default_rng([zlib.crc32(name.encode()), seed]).standard_normal(out[name].shape)
        drawn = base * np.exp(spread * noise) if base else spread * noise
        out[name] = jnp.asarray(drawn.astype(out[name].dtype))
    for name, factor in factors.items():
        out[name] = (out[name] * factor).astype(out[name].dtype)
    return out
```

```python
from contextlib import ExitStack, contextmanager

import numpy as np

import concourse.bass as bass
from concourse import mybir

F32 = mybir.dt.float32
I32 = mybir.dt.int32
ALU = mybir.AluOpType
ACT = mybir.ActivationFunctionType
AX = mybir.AxisListType
ds = bass.ds

P = 128
DEPTH, D, SEQ, NB, NT = 2, 1024, 512, 8, 4
PAST, PAGE = 4096, 128
NS = NB * NT
TOK = SEQ + NS
HALF = TOK // 2
KT = D // P
QT = SEQ // P
HD, HEADS, KVH, GRP = 64, 4, 2, 2
DFF = 4 * D
CW, PBUF, GC = 31, 15, 4
IN_W = 2836
NCH = PAST // 16
NCB = NCH - 1
NPG = PAST // PAGE
NBLK = PAST // 64
ALPHA = (2 * DEPTH) ** 0.25
NEG = -1e30
STRIP = 896
LINE = 1024
T_CONV, T_GLU, T_POOL, T_Q, T_KV, T_GDN, T_Z, T_MISC = 0, 2, 4, 6, 8, 14, 20, 22
N_IN = 23
M_GATE, M_A, M_B, M_W = 0, 32, 64, 96


def bucket(d):
    d = np.maximum(np.asarray(d), 0)
    log = np.log(np.maximum(d, 1).astype(np.float32) / np.float32(16)) / np.float32(np.log(128 / 16))
    large = np.minimum(16 + (log * np.float32(16)).astype(np.int32), 31)
    return np.where(d < 16, d, large)


def one_hot(d, base=None):
    d = np.asarray(d)
    e = np.zeros((33, d.size), np.float32)
    for j, x in enumerate(d.ravel()):
        if x < 0:
            e[32, j] = 1
        else:
            e[int(bucket(x)), j] += 1
            if base is not None:
                e[base, j] -= 1
    return e


def constant_tables():
    i = np.arange(P)
    s = np.arange(NS)
    row = np.arange(P)
    rb, rh, rt = row // 16, row // 4 % 4, row % 4
    t = {}
    t["ident"] = np.eye(P)
    t["mean_d"] = np.full((P, P), 1 / D)
    t["mean_c"] = np.full((P, P), 1 / 256)
    t["ones"] = np.ones((P, P))
    t["upto"] = i[:, None] <= i[None, :]
    t["after"] = np.where(i[None, :] >= i[:, None], 0, NEG)
    for l in range(7):
        w = 2 << l
        same = i[:, None] // w == i[None, :] // w
        t[f"level{l}"] = same & (i[:, None] % w < w // 2) & (i[None, :] % w >= w // 2)
    sb = s // NT
    same = sb[:, None] == sb[None, :]
    t["s_ones"] = same
    t["s_upto"] = same & (s[:, None] <= s[None, :])
    t["s_after"] = np.where(same & (s[None, :] >= s[:, None]), 0, NEG)
    t["s_batch"] = sb[:, None] == np.arange(NB)[None, :]
    t["s_row"] = (sb[:, None] == rb[None, :]) & (s[:, None] % NT == rt[None, :])
    inv = np.zeros((P, 2, 16))
    wcol = np.zeros((P, 2))
    for c in range(2):
        for q in range(2):
            w = (2, 4, 8, 16)[2 * c + q]
            inv[64 * q:64 * q + 64, c] = 1 / np.minimum(np.arange(16) + 1, w)
            wcol[64 * q:64 * q + 64, c] = 1 / w
    t["pool_first"] = inv.reshape(P, 32)
    t["pool_inv"] = wcol
    t["eps"] = np.tile(np.array([1e-5, 1e-6]), (P, 1))
    t["line"] = one_hot(511 - np.arange(LINE))
    e = np.zeros((33, NT, 416), np.float32)
    for q in range(NT):
        e[:, q, 0:128] = one_hot(128 + q - np.arange(128), 31)
        e[:, q, 128:160] = one_hot(q - np.arange(NS) % NT)
        e[:, q, 160:415] = one_hot(PAST + q - 16 * np.arange(NCB) - 31)
        e[31, q, 415] = 1
    t["s_line"] = e.reshape(33, -1)
    t["other_b"] = np.where(rb[:, None] == sb[None, :], 0, NEG)
    t["win_old"] = np.where(np.arange(NT)[None, :] > rt[:, None], 0, NEG)
    t["pair"] = (rb[:, None] == rb[None, :]) & (rt[:, None] == rt[None, :]) & (rh[:, None] // 2 == rh[None, :] // 2)
    t["row_head"] = rh[:, None] == np.arange(HEADS)[None, :]
    force = np.zeros(NBLK + 1)
    force[[0, NBLK - 1, NBLK]] = 1e4
    t["force"] = np.tile(force, (P, 1))
    return {k: np.asarray(v, np.float32) for k, v in t.items()}


def pack_tables():
    t = constant_tables()
    for k in ("line", "s_line"):
        t[k] = t.pop(k)
    where, n = {}, 0
    for k, v in t.items():
        where[k] = (n, v.shape[0], v.shape[1])
        n += v.shape[1]
    out = np.zeros((P, n), np.float32)
    for k, v in t.items():
        out[:v.shape[0], where[k][0]:where[k][0] + v.shape[1]] = v
    return out, where


class Named:

    def __init__(self, table):
        self.table = table

    def __getattr__(self, name):
        return self.table[name]


POOL = []


@contextmanager
def stage(nc, label, *names):
    while len(POOL) < len(names):
        POOL.append(nc.alloc_semaphore(f"stage_sem{len(POOL)}"))
    used = POOL[:len(names)]
    nums = [x.num for x in used]
    assert nums == list(range(nums[0], nums[0] + len(nums)))
    with nc.Block() as block:
        yield block, Named(dict(zip(names, used)))
    nc.all_engine_barrier(sems_to_clear=range(nums[0], nums[-1] + 1))


class Serial:

    def __init__(self, eng, own):
        self.eng, self.own, self.count = eng, own, {}

    def __call__(self, ins, signal=None):
        sem = self.own if signal is None else signal
        self.count[sem.num] = self.count.get(sem.num, 0) + 1
        ins.then_inc(sem, 1)
        self.eng.wait_ge(sem, self.count[sem.num])


def bc(ap, n):
    ap = ap.unsqueeze(len(ap.shape))
    return ap.broadcast_to(list(ap.shape[:-1]) + [n])


def bc_mid(ap, n):
    ap = ap.unsqueeze(1)
    return ap.broadcast_to([ap.shape[0], n] + list(ap.shape[2:]))


def halves(ap):
    return ap.rearrange("p (h n) -> p h n", h=2)


def build(nc, io, where):
    POOL.clear()
    with ExitStack() as top:
        def sb(name, shape, dt=F32, ctx=top):
            return ctx.enter_context(nc.sbuf_tensor(name, shape, dt))

        S = Named(dict(nc=nc, io=io, where=where, sb=sb))
        S.xT = sb("xT", [P, KT, TOK])
        S.yT = sb("yT", [P, KT, TOK])
        S.cst = sb("cst", [P, where["line"][0]])
        S.C = {k: S.cst[0:r, o:o + n] for k, (o, r, n) in where.items() if k not in ("line", "s_line")}
        S.sbias = sb("sbias", [P, 416])
        S.pages = sb("pages", [1, NB * NPG], I32)
        S.psum = top.enter_context(nc.psum_tensor("psum", [P, 8, 512], F32))
        load_inputs(S)
        with ExitStack() as c:
            bias_tables(S, c)
        with nc.Fori(0, DEPTH) as l:
            with ExitStack() as mix:
                S.HT = sb("HT", [P, N_IN - 6, TOK], ctx=mix)
                S.misc_n = sb("misc_n", [P, QT + 1, M_W], ctx=mix)
                S.gates = sb("gates", [P, QT + 1, 12], ctx=mix)
                with ExitStack() as c:
                    S.HC = sb("HC", [P, 6, TOK], ctx=c)
                    project_in(S, l, c)
                    conv_and_pool(S, l, c)
                with ExitStack() as att:
                    compression_weights(S, l, att)
                    with ExitStack() as c:
                        prompt_attention(S, l, c)
                    with ExitStack() as c:
                        sample_scores(S, l, c)
                        sample_attention(S, l, c)
                with ExitStack() as c:
                    gated_delta(S, l, c)
            with ExitStack() as c:
                project_out(S, l, c)
            with ExitStack() as c:
                feed_forward(S, l, c)
        store_outputs(S)


def load_inputs(S):
    nc, io = S.nc, S.io
    with ExitStack() as c:
        xn = S.sb("xn", [P, QT + 1, D], ctx=c)
        with stage(nc, "in", "loaded", "turned", "copied") as (block, s):
            @block.sync
            def _(sp):
                sp.dma_start(S.cst[:, :], io.cst[:, 0:S.where["line"][0]]).then_inc(s.loaded, 16)
                sp.dma_start(S.pages[:, :], io.page_table.rearrange("(a b) j -> a (b j)", a=1)).then_inc(s.loaded, 16)
                sp.dma_start(xn[:, 0:QT, :], io.x_prompt.rearrange("a (q p) n -> p (a q) n", p=P)).then_inc(s.loaded, 16)
                sp.dma_start(xn[0:NS, QT, :], io.x_sample.rearrange("b t n -> (b t) n")).then_inc(s.loaded, 16)

            @block.tensor
            def _(pe):
                pe.wait_ge(s.loaded, 64)
                for q in range(QT + 1):
                    n = P if q < QT else NS
                    if q >= 2:
                        pe.wait_ge(s.copied, q - 1)
                    for k in range(KT):
                        last = pe.transpose(S.psum[:, 2 * (q % 2) + k // 4, (k % 4) * P:(k % 4) * P + n],
                                            xn[0:n, q, k * P:(k + 1) * P], S.C["ident"][0:n, 0:n])
                    last.then_inc(s.turned, 1)

            @block.vector
            def _(dve):
                for q in range(QT + 1):
                    n = P if q < QT else NS
                    dve.wait_ge(s.turned, q + 1)
                    src = S.psum[:, 2 * (q % 2):2 * (q % 2) + 2, :].rearrange("p b (k n) -> p (b k) n", n=P)
                    dve.tensor_copy(S.xT[:, :, q * P:q * P + n], src[:, :, 0:n]).then_inc(s.copied, 1)


def bias_tables(S, ctx):
    nc, io, sb = S.nc, S.io, S.sb
    line = sb("line", [33, LINE], ctx=ctx)
    sline = sb("sline", [33, NT, 416], ctx=ctx)
    rel = sb("rel", [33, HEADS], ctx=ctx)
    relp = sb("relp", [33, HEADS, P], ctx=ctx)
    rels = sb("rels", [33, NT, P], ctx=ctx)
    rows = sb("rows", [P, HEADS, LINE], ctx=ctx)
    w = S.where
    with stage(nc, "bias", "loaded", "mask", "spread", "product", "copied", "stored") as (block, s):
        @block.sync
        def _(sp):
            sp.dma_start(line[:, :], io.cst[0:33, w["line"][0]:w["line"][0] + LINE]).then_inc(s.loaded, 16)
            sp.dma_start(sline[:, :, :], io.cst[0:33, w["s_line"][0]:w["s_line"][0] + NT * 416]
                         .rearrange("p (t n) -> p t n", t=NT)).then_inc(s.loaded, 16)
            sp.dma_start(rel[0:32, :], io.rel_bias).then_inc(s.loaded, 16)
            sp.wait_ge(s.copied, 2 * HEADS)
            sp.dma_start(io.line_dram.rearrange("h p n -> p h n"), rows[:, :, :]).then_inc(s.stored, 16)
            sp.wait_ge(s.stored, 16)

        @block.vector
        def _(dve):
            step = Serial(dve, s.spread)
            dve.memset(rel[32:33, :], NEG).then_inc(s.mask, 1)
            step(dve.memset(rels[:, :, :], 0.0))
            dve.wait_ge(s.mask, 1)
            dve.wait_ge(s.loaded, 48)
            step(dve.tensor_copy(relp[:, :, :], bc(rel[:, :], P)))
            for t in range(NT):
                dst = rels[:, t, :].rearrange("k (b h q) -> k b h q", b=NB, h=HEADS)[:, :, :, t]
                step(dve.tensor_copy(dst, bc_mid(rel[:, :], NB)))
            for h in range(HEADS):
                for j in range(2):
                    n = 2 * h + j
                    dve.wait_ge(s.product, n + 1)
                    dve.tensor_copy(rows[:, h, j * 512:(j + 1) * 512], S.psum[:, n % 4, :]).then_inc(s.copied, 1)
            dve.wait_ge(s.product, 2 * HEADS + 1)
            dve.tensor_copy(S.sbias[:, :], S.psum[:, 4, 0:416]).then_inc(s.copied, 1)
            dve.wait_ge(s.copied, 2 * HEADS + 1)
            dve.tensor_tensor(S.sbias[:, 128:160], S.sbias[:, 128:160], S.C["other_b"], ALU.add).then_inc(s.copied, 1)

        @block.tensor
        def _(pe):
            pe.wait_ge(s.spread, 2 + NT)
            for h in range(HEADS):
                for j in range(2):
                    n = 2 * h + j
                    if n >= 4:
                        pe.wait_ge(s.copied, n - 3)
                    pe.matmul(S.psum[:, n % 4, :], relp[:, h, :], line[:, j * 512:(j + 1) * 512],
                              start=True, stop=True).then_inc(s.product, 1)
            for t in range(NT):
                last = pe.matmul(S.psum[:, 4, 0:416], rels[:, t, :], sline[:, t, :], start=(t == 0), stop=(t == NT - 1))
            last.then_inc(s.product, 1)


def dense(S, label, weights, kt, moving, lhsT, n_tiles, evac_act, evac_dve, beside=None):
    nc, psum = S.nc, S.psum
    slots, per, load, n_dmas = weights
    n_groups = -(-n_tiles // per)
    names = [f"loaded{i}" for i in range(slots)]
    with stage(nc, label, "product", "taken_dve", "taken_act", "rect_dve", "rect_act", "beside", *names) as (block, s):
        loaded = [s.table[n] for n in names]

        @block.sync
        def _(sp):
            for g in range(n_groups):
                if g >= slots:
                    sp.wait_ge(s.product, per * (g - slots + 1))
                load(sp, g, g % slots, loaded[g % slots])

        @block.tensor
        def _(pe):
            arrived = [0] * slots
            for t in range(n_tiles):
                g = t // per
                if t % per == 0:
                    arrived[g % slots] += 16 * n_dmas(g)
                    pe.wait_ge(loaded[g % slots], arrived[g % slots])
                if t >= 4:
                    if evac_act is None:
                        pe.wait_ge(s.taken_dve, t - 3)
                    else:
                        pe.wait_ge(s.taken_act if t % 2 else s.taken_dve, (t - 4) // 2 + 1)
                for k in range(kt):
                    w = lhsT(t, k)
                    for h in range(2):
                        last = pe.matmul(psum[0:w.shape[1], 2 * (t % 4) + h, 0:HALF], w,
                                         moving(k)[:, h * HALF:(h + 1) * HALF], start=(k == 0), stop=(k == kt - 1))
                last.then_inc(s.product, 1)

        def tile_of(t):
            return psum[:, 2 * (t % 4):2 * (t % 4) + 2, 0:HALF]

        @block.vector
        def _(dve):
            for t in range(0, n_tiles, 1 if evac_act is None else 2):
                dve.wait_ge(s.product, t + 1)
                evac_dve(dve, t, tile_of(t), s).then_inc(s.taken_dve, 1)

        @block.scalar
        def _(act):
            n_beside = beside(act, s.beside) if beside else 0
            for t in range(1, n_tiles, 2) if evac_act else ():
                act.wait_ge(s.product, t + 1)
                evac_act(act, t, tile_of(t), s).then_inc(s.taken_act, 1)
            if n_beside:
                act.wait_ge(s.beside, 16 * n_beside)


def layer(ap, l):
    dims = " ".join(f"d{i}" for i in range(len(ap.shape) - 2))
    return ap[ds(l, 1)].rearrange(f"a b {dims} -> (a b) {dims}")


def project_in(S, l, ctx):
    nc, io, sb = S.nc, S.io, S.sb
    ring = sb("w_ring", [P, 3, KT, 256], ctx=ctx)
    misc = sb("w_misc", [P, KT, M_W], ctx=ctx)
    w_in = layer(io.w_in, l).rearrange("(k p) n -> p k n", p=P)
    start = [0, 256, 512, 768, 1024, 1280, 1536, 1804, 2060, 2316, 2572]

    with stage(nc, "misc", "zero", "loaded") as (block, s):
        @block.gpsimd
        def _(pool):
            pool.memset(misc[:, :, :], 0.0).then_inc(s.zero, 1)

        @block.scalar
        def _(act):
            act.wait_ge(s.zero, 1)
            act.dma_start(misc[:, :, M_GATE:M_GATE + 12], w_in[:, :, 1792:1804]).then_inc(s.loaded, 16)
            act.dma_start(misc[:, :, M_A:M_A + 4], w_in[:, :, 2828:2832]).then_inc(s.loaded, 16)
            act.dma_start(misc[:, :, M_B:M_B + 4], w_in[:, :, 2832:2836]).then_inc(s.loaded, 16)
            act.wait_ge(s.loaded, 48)

    def load(sp, g, slot, sem):
        if g == 3:
            for grp in range(GRP):
                for kh in range(KVH):
                    c = 768 + (kh * GRP + grp) * HD
                    sp.dma_start(ring[:, slot, :, (grp * KVH + kh) * HD:(grp * KVH + kh + 1) * HD],
                                 w_in[:, :, c:c + HD]).then_inc(sem, 16)
        elif g < 11:
            sp.dma_start(ring[:, slot, :, :], w_in[:, :, start[g]:start[g] + 256]).then_inc(sem, 16)

    def lhsT(t, k):
        if t == T_MISC:
            return misc[:, k, :]
        return ring[:, (t // 2) % 3, k, (t % 2) * P:(t % 2) * P + P]

    def dest(t):
        return S.HC[:, t, :] if t < 6 else S.HT[:, t - 6, :]

    def evac_act(act, t, src, s):
        if t == T_Q + 1:
            return act.mul(halves(dest(t)), src, HD ** -0.5)
        return act.copy(halves(dest(t)), src)

    def evac_dve(dve, t, src, s):
        if t == T_Q:
            return dve.tensor_scalar(halves(dest(t)), src, HD ** -0.5, None, ALU.mult)
        if t == T_MISC:
            return dve.tensor_copy(halves(dest(t)[0:M_W]), src[0:M_W])
        return dve.tensor_copy(halves(dest(t)), src)

    def keep_window(act, sem):
        for b in range(NB):
            act.dma_start(layer(io.sample_win, l)[b, 0:512 - NT].rearrange("w c k d -> w (c k d)"),
                          layer(io.cache_win_kv, l)[b, NT:].rearrange("w c k d -> w (c k d)")).then_inc(sem, 16)
        return NB

    dense(S, "proj", (3, 2, load, lambda g: 4 if g == 3 else (0 if g == 11 else 1)), KT, lambda k: S.xT[:, k, :],
          lhsT, N_IN, evac_act, evac_dve, beside=keep_window)


def conv_and_pool(S, l, ctx):
    nc, io, sb, psum, C, HC = S.nc, S.io, S.sb, S.psum, S.C, S.HC
    vrow = sb("vrow", [35, 256], ctx=ctx)
    cols = sb("cols", [P, 2, 35], ctx=ctx)
    conv_st = sb("conv_st", [120, 2, 256], ctx=ctx)
    pool_st = sb("pool_st", [120, 256], ctx=ctx)
    u = sb("u", [P, 2, CW - 1 + SEQ], ctx=ctx)
    us = sb("us", [P, 2, NB, CW - 1 + NT], ctx=ctx)
    v = sb("v", [P, 2, PBUF + SEQ], ctx=ctx)
    vs = sb("vs", [P, 2, NB, PBUF + NT], ctx=ctx)
    poolw = sb("poolw", [P, 2, P], ctx=ctx)
    pw = sb("pw", [P, 2, 256], ctx=ctx)
    with stage(nc, "glu", "loaded", "linear", "zero", "turned", "sigmoid", "placed", "copied", "moved") as (block, s):
        @block.sync
        def _(sp):
            sp.dma_start(vrow[0:CW, :], layer(io.conv_dw, l)).then_inc(s.loaded, 16)
            for i, a in enumerate((io.conv_dw_b, io.conv_ln_g, io.conv_ln_b, io.pool_scale)):
                sp.dma_start(vrow[CW + i:CW + i + 1, :], a[ds(l, 1)]).then_inc(s.loaded, 16)
            sp.dma_start(conv_st[:, :, :], layer(io.state_conv, l).rearrange("(h b) w c -> (b w) h c", h=2)).then_inc(s.loaded, 16)
            sp.dma_start(pool_st[:, :], layer(io.state_pool, l).rearrange("b w c -> (b w) c")).then_inc(s.loaded, 16)
            sp.dma_start(pw[:, :, :], layer(io.conv_pw, l).rearrange("(k p) n -> p k n", p=P)).then_inc(s.loaded, 16)
            sp.wait_ge(s.zero, 3)
            for g in range(4):
                r = 64 * (g % 2)
                sp.dma_start(poolw[r:r + 64, g // 2, r:r + 64], layer(io.pool_w, l)[g]).then_inc(s.linear, 16)
            sp.wait_ge(s.linear, 16 * 4)

        @block.gpsimd
        def _(pool):
            pool.memset(u[:, :, 0:CW - 1], 0.0).then_inc(s.zero, 1)
            pool.memset(v[:, :, 0:PBUF], 0.0).then_inc(s.zero, 1)
            pool.memset(poolw[:, :, :], 0.0).then_inc(s.zero, 1)
            pool.tensor_copy(v[:, :, PBUF:], HC[:, 4:6, 0:SEQ]).then_inc(s.moved, 1)
            for c in range(2):
                pool.tensor_copy(vs[:, c, :, PBUF:], HC[:, 4 + c, SEQ:].rearrange("p (b t) -> p b t", b=NB)).then_inc(s.moved, 1)

        @block.tensor
        def _(pe):
            pe.wait_ge(s.loaded, 16 * 8)
            for c in range(2):
                f = slice(c * P, c * P + P)
                pe.transpose(psum[:, c, 0:35], vrow[:, f], C["ident"][0:35, 0:35]).then_inc(s.turned, 1)
                pe.transpose(psum[:, 2 + c, 0:120], pool_st[:, f], C["ident"][0:120, 0:120]).then_inc(s.turned, 1)
                for h in range(2):
                    pe.transpose(psum[:, 4 + 2 * c + h, 0:120], conv_st[:, h, f], C["ident"][0:120, 0:120]).then_inc(s.turned, 1)

        @block.scalar
        def _(act):
            act.activation(HC[:, 2:4, :], HC[:, 2:4, :], ACT.Sigmoid).then_inc(s.sigmoid, 1)
            for c in range(2):
                act.wait_ge(s.turned, 4 * c + 4)
                act.copy(cols[:, c, :], psum[:, c, 0:35]).then_inc(s.copied, 1)
                act.copy(vs[:, c, :, 0:PBUF], psum[:, 2 + c, 0:120].rearrange("p (b w) -> p b w", b=NB)).then_inc(s.copied, 1)
                for h in range(2):
                    act.copy(us[:, c, 4 * h:4 * h + 4, 0:CW - 1],
                             psum[:, 4 + 2 * c + h, 0:120].rearrange("p (b w) -> p b w", b=4)).then_inc(s.copied, 1)

        @block.vector
        def _(dve):
            dve.wait_ge(s.sigmoid, 1)
            dve.tensor_tensor(u[:, :, CW - 1:], HC[:, 0:2, 0:SEQ], HC[:, 2:4, 0:SEQ], ALU.mult).then_inc(s.placed, 1)
            for c in range(2):
                dve.tensor_tensor(us[:, c, :, CW - 1:], HC[:, c, SEQ:].rearrange("p (b t) -> p b t", b=NB),
                                  HC[:, 2 + c, SEQ:].rearrange("p (b t) -> p b t", b=NB), ALU.mult).then_inc(s.placed, 1)

    pack = sb("pack", [P, 2, 3 * 120], ctx=ctx)
    nat = sb("nat", [120, 5, 256], ctx=ctx)
    acc = sb("acc", [P, 2, TOK], ctx=ctx)
    sq = sb("sq", [P, 2, TOK], ctx=ctx)
    rstd = sb("rstd", [P, TOK], ctx=ctx)
    sums = [sb(f"sum{w}", [P, 2, PBUF + SEQ], ctx=ctx) for w in (2, 4, 8, 16)]
    sums_s = [sb(f"sums{w}", [P, 2, NB, PBUF + NT], ctx=ctx) for w in (2, 4, 8, 16)]
    pd = sb("pd", [P, 2, TOK], ctx=ctx)
    names = ("packed", "turned", "copied", "stored", "taps", "conv", "mean", "centred", "squared", "var", "ln", "rstd",
             "normed", "swish", "pooled", "psteps", "linear", "scaled", "pointwise", "out", "dsteps")
    with stage(nc, "conv", *names) as (block, s):
        @block.gpsimd
        def _(pool):
            for c in range(2):
                for h in range(2):
                    pool.tensor_copy(pack[:, c, h * 120:h * 120 + 120].rearrange("p (b w) -> p b w", b=4),
                                     us[:, c, 4 * h:4 * h + 4, NT:]).then_inc(s.packed, 1)
                pool.tensor_copy(pack[:, c, 240:360].rearrange("p (b w) -> p b w", b=NB), vs[:, c, :, NT:]).then_inc(s.packed, 1)
            step = Serial(pool, s.psteps)
            a, b = v, vs
            for i, w in enumerate((2, 4, 8, 16)):
                h = w // 2
                step(pool.tensor_tensor(sums[i][:, :, w - 1:], a[:, :, w - 1:], a[:, :, w - 1 - h:PBUF + SEQ - h], ALU.add))
                for c in range(2):
                    step(pool.tensor_tensor(sums_s[i][:, c, :, w - 1:], b[:, c, :, w - 1:], b[:, c, :, w - 1 - h:PBUF + NT - h], ALU.add))
                a, b = sums[i], sums_s[i]
            for i in range(4):
                c, r = i // 2, slice(64 * (i % 2), 64 * (i % 2) + 64)
                inv = C["pool_inv"][r, c:c + 1]
                pool.tensor_scalar(pd[r, c, 16:SEQ], sums[i][r, c, PBUF + 16:], inv, None, ALU.mult)
                pool.tensor_tensor(pd[r, c, 0:16], sums[i][r, c, PBUF:PBUF + 16], C["pool_first"][r, 16 * c:16 * c + 16], ALU.mult)
                step(pool.tensor_scalar(pd[r, c, SEQ:].rearrange("p (b t) -> p b t", b=NB), sums_s[i][r, c, :, PBUF:], inv, None, ALU.mult))
            pool.tensor_tensor(pd[:, :, :], pd[:, :, :], HC[:, 4:6, :], ALU.subtract).then_inc(s.pooled, 1)

        @block.vector
        def _(dve):
            def tap(n, w, c, out, src):
                if n >= 4:
                    dve.wait_ge(s.taps, n - 3)
                if w == 0:
                    dve.tensor_scalar(out, src, cols[:, c, 0:1], cols[:, c, 31:32], ALU.mult, ALU.add).then_inc(s.taps, 1)
                else:
                    dve.scalar_tensor_tensor(out, src, cols[:, c, w:w + 1], out, ALU.mult, ALU.add).then_inc(s.taps, 1)

            for w in range(CW):
                for c in range(2):
                    tap(4 * w + 2 * c, w, c, acc[:, c, 0:SEQ], u[:, c, w:w + SEQ])
                    tap(4 * w + 2 * c + 1, w, c, acc[:, c, SEQ:].rearrange("p (b t) -> p b t", b=NB), us[:, c, :, w:w + NT])
            dve.wait_ge(s.mean, 1)
            for c in range(2):
                dve.tensor_tensor(halves(acc[:, c, :]), halves(acc[:, c, :]), psum[:, 6:8, 0:HALF], ALU.subtract).then_inc(s.centred, 1)
            dve.wait_ge(s.rstd, 1)
            for c in range(2):
                dve.wait_ge(s.centred, 2)
                dve.tensor_tensor(acc[:, c, :], acc[:, c, :], rstd[:, :], ALU.mult).then_inc(s.normed, 1)
            for c in range(2):
                dve.wait_ge(s.pointwise, c + 1)
                dve.tensor_copy(halves(S.yT[:, c, :]), psum[:, 2 * c:2 * c + 2, 0:HALF]).then_inc(s.out, 1)

        @block.tensor
        def _(pe):
            pe.wait_ge(s.packed, 6)
            for c in range(2):
                srcs = (u[:, c, SEQ:], v[:, c, SEQ:], pack[:, c, 0:120], pack[:, c, 120:240], pack[:, c, 240:360])
                for j, src in enumerate(srcs):
                    pe.transpose(psum[0:src.shape[1], j, c * P:c * P + P], src, C["ident"]).then_inc(s.turned, 1)
            pe.wait_ge(s.taps, 4 * CW)
            for h in range(2):
                for c in range(2):
                    last = pe.matmul(psum[:, 6 + h, 0:HALF], C["mean_c"], acc[:, c, h * HALF:(h + 1) * HALF], start=(c == 0), stop=(c == 1))
            last.then_inc(s.mean, 1)
            pe.wait_ge(s.pooled, 1)
            pe.wait_ge(s.copied, 5)
            for c in range(2):
                for h in range(2):
                    last = pe.matmul(psum[:, 2 * c + h, 0:HALF], poolw[:, c, :], pd[:, c, h * HALF:(h + 1) * HALF], start=True, stop=True)
                last.then_inc(s.linear, 1)
            pe.wait_ge(s.squared, 1)
            for h in range(2):
                for c in range(2):
                    last = pe.matmul(psum[:, 6 + h, 0:HALF], C["mean_c"], sq[:, c, h * HALF:(h + 1) * HALF], start=(c == 0), stop=(c == 1))
            last.then_inc(s.var, 1)
            pe.wait_ge(s.swish, 2)
            pe.wait_ge(s.scaled, 2)
            for c in range(2):
                for k in range(2):
                    for h in range(2):
                        last = pe.matmul(psum[:, 2 * c + h, 0:HALF], pw[:, k, c * P:c * P + P], acc[:, k, h * HALF:(h + 1) * HALF],
                                         start=(k == 0), stop=(k == 1))
                last.then_inc(s.pointwise, 1)

        @block.scalar
        def _(act):
            act.wait_ge(s.turned, 10)
            for j, n in enumerate((CW - 1, PBUF, 120, 120, 120)):
                act.copy(nat[0:n, j, :], psum[0:n, j, 0:256]).then_inc(s.copied, 1)
            for c in range(2):
                act.wait_ge(s.linear, c + 1)
                act.mul(halves(S.yT[:, 2 + c, :]), psum[:, 2 * c:2 * c + 2, 0:HALF], cols[:, c, 34:35]).then_inc(s.scaled, 1)
            act.wait_ge(s.centred, 2)
            act.activation(sq[:, :, :], acc[:, :, :], ACT.Square).then_inc(s.squared, 1)
            act.wait_ge(s.var, 1)
            act.activation(halves(rstd[:, :]), psum[:, 6:8, 0:HALF], ACT.Ln, bias=C["eps"][:, 0:1]).then_inc(s.ln, 1)
            act.wait_ge(s.ln, 1)
            act.activation(rstd[:, :], rstd[:, :], ACT.Exp, scale=-0.5).then_inc(s.rstd, 1)
            for c in range(2):
                act.wait_ge(s.normed, c + 1)
                act.activation(acc[:, c, :], acc[:, c, :], ACT.Silu, bias=cols[:, c, 33:34], scale=cols[:, c, 32:33]).then_inc(s.swish, 1)

        @block.sync
        def _(sp):
            sp.wait_ge(s.copied, 5)
            sp.dma_start(layer(io.prompt_conv, l)[0], nat[0:CW - 1, 0, :]).then_inc(s.stored, 16)
            sp.dma_start(layer(io.prompt_pool, l)[0], nat[0:PBUF, 1, :]).then_inc(s.stored, 16)
            for h in range(2):
                sp.dma_start(layer(io.sample_conv, l)[4 * h:4 * h + 4].rearrange("b w c -> (b w) c"), nat[:, 2 + h, :]).then_inc(s.stored, 16)
            sp.dma_start(layer(io.sample_pool, l).rearrange("b w c -> (b w) c"), nat[:, 4, :]).then_inc(s.stored, 16)
            sp.wait_ge(s.stored, 80)


def compression_weights(S, l, ctx):
    nc, io, sb, psum, C = S.nc, S.io, S.sb, S.psum, S.C
    S.W1 = sb("W1", [P, 2, 32, P], ctx=ctx)
    S.W2 = sb("W2", [P, 2, P], ctx=ctx)
    S.pe_h = sb("pe_h", [P, 2], ctx=ctx)
    S.kv_s = sb("kv_s", [NS, 6 * P], ctx=ctx)
    pe_n = sb("pe_n", [64, 2, HD], ctx=ctx)
    pe_t = sb("pe_t", [P, 64], ctx=ctx)
    with stage(nc, "cw", "misc", "zero", "first", "second", "pe", "turned", "copied", "product", "out") as (block, s):
        @block.vector
        def _(dve):
            dve.memset(S.W2[:, :, :], 0.0).then_inc(s.zero, 1)
            dve.memset(S.W1[:, 1, :, :], 0.0).then_inc(s.zero, 1)
            dve.wait_ge(s.turned, 1)
            dve.tensor_copy(pe_t[:, :], psum[:, 0, 0:64]).then_inc(s.copied, 1)
            dve.wait_ge(s.product, 1)
            dve.tensor_copy(S.pe_h[:, :], psum[:, 1, 0:2]).then_inc(s.out, 1)

        @block.gpsimd
        def _(pool):
            pool.memset(S.W1[:, 0, :, :], 0.0).then_inc(s.zero, 1)
            pool.memset(S.misc_n[:, QT, :], 0.0).then_inc(s.misc, 1)

        @block.sync
        def _(sp):
            for i in range(2):
                sp.dma_start(pe_n[:, i, :], layer(io.cmp_pe, l).rearrange("c s d -> (c s) d")).then_inc(s.pe, 16)
            sp.wait_ge(s.zero, 3)
            for c in range(2):
                for k in range(KVH):
                    r = slice(64 * k, 64 * k + 64)
                    sp.dma_start(S.W2[r, c, r], layer(io.cmp_w2, l)[c]).then_inc(s.second, 16)
                    sp.dma_start(S.W1[r, c, :, r], layer(io.cmp_w1, l)[c].rearrange("(s d) e -> d s e", d=HD)).then_inc(s.first, 16)
            sp.wait_ge(s.second, 64)

        @block.tensor
        def _(pe):
            pe.wait_ge(s.pe, 32)
            pe.transpose(psum[:, 0, 0:64], pe_n[:, :, :].rearrange("p a b -> p (a b)"), C["ident"][0:64, 0:64]).then_inc(s.turned, 1)
            pe.wait_ge(s.copied, 1)
            pe.wait_ge(s.first, 64)
            for c in range(2):
                for j in range(32):
                    last = pe.matmul(psum[:, 1, c:c + 1], S.W1[:, c, j, :], pe_t[:, 32 * c + j:32 * c + j + 1],
                                     start=(j == 0), stop=(j == 31))
            last.then_inc(s.product, 1)


def prompt_attention(S, l, ctx):
    nc, io, sb, psum, C = S.nc, S.io, S.sb, S.psum, S.C
    H = lambda t: S.HT[:, t - 6, :]
    kvn = sb("kvn", [P, QT, 6 * P], ctx=ctx)
    strip = sb("strip", [P, HEADS, STRIP], ctx=ctx)
    hc = sb("hc", [P, 2, 31], ctx=ctx)
    kc = sb("kc", [P, 31], ctx=ctx)
    vc = sb("vc", [31, P], ctx=ctx)
    with stage(nc, "nat", "turned", "copied_act", "copied_dve", "gates", "stored", "strip", "summed", "swish", "second", "kept") as (block, s):
        @block.tensor
        def _(pe):
            for q in range(QT + 1):
                n = P if q < QT else NS
                a = 2 * (q % 2)
                if q >= 2:
                    pe.wait_ge(s.copied_act, q - 1)
                    pe.wait_ge(s.copied_dve, q - 1)
                for c in range(6):
                    pe.transpose(psum[0:n, a + c // 4, (c % 4) * P:(c % 4) * P + P], H(T_KV + c)[:, q * P:q * P + n], C["ident"])
                pe.transpose(psum[0:n, a + 1, 2 * P:2 * P + M_W], H(T_MISC)[0:M_W, q * P:q * P + n],
                             C["ident"][0:M_W, 0:M_W]).then_inc(s.turned, 1)
            for c in range(2):
                tok = H(T_KV + c)[:, 0:SEQ].rearrange("p (n s) -> p s n", s=16)
                for j in range(32):
                    last = pe.matmul(psum[:, 4 + c, 0:31], S.W1[:, c, j, :], tok[:, j % 16, j // 16:j // 16 + 31],
                                     start=(j == 0), stop=(j == 31))
                last.then_inc(s.summed, 1)
            pe.wait_ge(s.swish, 2)
            pe.matmul(psum[:, 6, 0:31], S.W2[:, 0, :], hc[:, 0, :], start=True, stop=True).then_inc(s.second, 1)
            pe.matmul(psum[0:31, 7, 0:P], hc[:, 1, :], S.W2[:, 1, :], start=True, stop=True).then_inc(s.second, 1)

        @block.scalar
        def _(act):
            for q in range(QT + 1):
                n = P if q < QT else NS
                dst = kvn[:, q, 0:512] if q < QT else S.kv_s[:, 0:512]
                act.wait_ge(s.turned, q + 1)
                act.copy(dst, psum[0:n, 2 * (q % 2), :]).then_inc(s.copied_act, 1)
            for c in range(2):
                act.wait_ge(s.summed, c + 1)
                act.activation(hc[:, c, :], psum[:, 4 + c, 0:31], ACT.Silu, bias=S.pe_h[:, c:c + 1]).then_inc(s.swish, 1)
            act.wait_ge(s.copied_dve, QT + 1)
            act.activation(S.gates[:, 0:QT, :], S.misc_n[:, 0:QT, M_GATE:M_GATE + 12], ACT.Sigmoid).then_inc(s.gates, 1)
            act.activation(S.gates[0:NS, QT, :], S.misc_n[0:NS, QT, M_GATE:M_GATE + 12], ACT.Sigmoid).then_inc(s.gates, 1)

        @block.vector
        def _(dve):
            for q in range(QT + 1):
                n = P if q < QT else NS
                dst = kvn[:, q, 512:768] if q < QT else S.kv_s[:, 512:768]
                dve.wait_ge(s.turned, q + 1)
                dve.tensor_copy(dst, psum[0:n, 2 * (q % 2) + 1, 0:256])
                dve.tensor_copy(S.misc_n[0:n, q, :], psum[0:n, 2 * (q % 2) + 1, 256:256 + M_W]).then_inc(s.copied_dve, 1)
            dve.wait_ge(s.second, 2)
            dve.tensor_copy(kc[:, :], psum[:, 6, 0:31]).then_inc(s.kept, 1)
            dve.tensor_copy(vc[:, :], psum[0:31, 7, 0:P]).then_inc(s.kept, 1)

        @block.sync
        def _(sp):
            src = bass.AP(io.line_dram.tensor, 127, [[LINE - 1, P], [P * LINE, HEADS], [1, STRIP]])
            sp.dma_start(strip[:, :, :], src).then_inc(s.strip, 16)
            sp.wait_ge(s.copied_act, QT + 1)
            sp.wait_ge(s.copied_dve, QT + 1)
            sp.dma_start(layer(io.prompt_nsa, l).rearrange("g t c k d -> t g (c k d)"), kvn[:, :, 0:512]).then_inc(s.stored, 16)
            sp.dma_start(layer(io.prompt_win, l).rearrange("a (q p) c k d -> p (a q) (c k d)", p=P), kvn[:, :, 512:768]).then_inc(s.stored, 16)
            sp.dma_start(layer(io.sample_nsa, l).rearrange("b t c k d -> (b t) (c k d)"), S.kv_s[:, 0:512]).then_inc(s.stored, 16)
            for b in range(NB):
                sp.dma_start(layer(io.sample_win, l)[b, 512 - NT:].rearrange("t c k d -> t (c k d)"),
                             S.kv_s[b * NT:b * NT + NT, 512:768]).then_inc(s.stored, 16)
            sp.wait_ge(s.strip, 16)
            sp.wait_ge(s.stored, 16 * (3 + NB))

    units = [(i, h, br) for i in range(QT) for h in range(HEADS) for br in range(3)]
    N = len(units)
    sc = sb("sc", [P, 3, 512], ctx=ctx)
    pt = sb("pt", [P, 3, 512], ctx=ctx)
    nmax = sb("nmax", [P, N], ctx=ctx)
    esum = sb("esum", [P, N], ctx=ctx)
    coef = sb("coef", [P, N], ctx=ctx)
    o = sb("o", [P, QT, 256], ctx=ctx)
    names = ("scored", "added", "step", "maxed", "exped", "turned", "pt_copied", "pv", "summed", "coef", "o_turned", "o_copied")
    with stage(nc, "att", *names) as (block, s):
        def width(n):
            i, h, br = units[n]
            return 31 if br == 0 else P * (i + 1)

        @block.tensor
        def _(pe):
            def scores(n):
                i, h, br = units[n]
                r = slice(64 * (h // GRP), 64 * (h // GRP) + 64)
                keys = kc[r, :] if br == 0 else H(T_KV + 2 * br)[r, 0:P * (i + 1)]
                if n >= 2:
                    pe.wait_ge(s.added, n - 1)
                pe.matmul(psum[:, n % 2, 0:width(n)], H(T_Q + h % GRP)[r, i * P:i * P + P], keys,
                          start=True, stop=True).then_inc(s.scored, 1)

            def turn(n):
                pe.wait_ge(s.exped, n + 1)
                if n >= 2:
                    pe.wait_ge(s.pt_copied, n - 1)
                w = width(n)
                for j in range(0, w, P):
                    m = min(P, w - j)
                    last = pe.transpose(psum[0:m, 2 + n % 2, j:j + P], sc[:, n % 3, j:j + m], C["ident"])
                last.then_inc(s.turned, 1)

            def values(n):
                i, h, br = units[n]
                k = 64 * (h // GRP)
                pe.wait_ge(s.pt_copied, n + 1)
                if n >= 2:
                    pe.wait_ge(s.summed, n - 1)
                if br == 0:
                    last = pe.matmul(psum[:, 4 + n % 2, 0:HD], pt[0:31, n % 3, 0:P], vc[:, k:k + HD], start=True, stop=True)
                else:
                    for j in range(i + 1):
                        c = (2 * br + 1) * P + k
                        last = pe.matmul(psum[:, 4 + n % 2, 0:HD], pt[:, n % 3, j * P:j * P + P], kvn[:, j, c:c + HD],
                                         start=(j == 0), stop=(j == i))
                last.then_inc(s.pv, 1)

            for n in range(N + 2):
                if n < N:
                    scores(n)
                if 1 <= n <= N:
                    turn(n - 1)
                if n >= 2:
                    values(n - 2)
            pe.wait_ge(s.summed, N)
            for i in range(QT):
                for c in range(2):
                    last = pe.transpose(psum[:, 6 + c, i * P:i * P + P], o[:, i, c * P:c * P + P], C["ident"])
            last.then_inc(s.o_turned, 1)

        @block.scalar
        def _(act):
            for n in range(N + 1):
                if n < N:
                    act.wait_ge(s.maxed, n + 1)
                    x = sc[:, n % 3, 0:width(n)]
                    act.activation(x, x, ACT.Exp, bias=nmax[:, n:n + 1], accum_out=esum[:, n:n + 1]).then_inc(s.exped, 1)
                if n >= 1:
                    m = n - 1
                    act.wait_ge(s.turned, m + 1)
                    if m >= 3:
                        act.wait_ge(s.pv, m - 2)
                    w = 31 if width(m) == 31 else P
                    x = slice(0, P if w == 31 else width(m))
                    act.copy(pt[0:w, m % 3, x], psum[0:w, 2 + m % 2, x]).then_inc(s.pt_copied, 1)
            act.wait_ge(s.o_turned, 1)
            for c in range(2):
                act.copy(S.yT[:, 4 + c, 0:SEQ], psum[:, 6 + c, :]).then_inc(s.o_copied, 1)

        @block.vector
        def _(dve):
            step = Serial(dve, s.step)
            for n in range(N + 2):
                if n < N:
                    i, h, br = units[n]
                    w = width(n)
                    x0 = 415 - P * i if br == 0 else 384 - P * i
                    bias = strip[:, h, x0:x0 + 481:16] if br == 0 else strip[:, h, x0:512]
                    x = sc[:, n % 3, 0:w]
                    dve.wait_ge(s.scored, n + 1)
                    if n >= 3:
                        dve.wait_ge(s.turned, n - 2)
                    step(dve.tensor_tensor(x, psum[:, n % 2, 0:w], bias, ALU.add), s.added)
                    step(dve.tensor_reduce(nmax[:, n:n + 1], x, AX.X, ALU.max, negate=True))
                    dve.tensor_scalar(nmax[:, n:n + 1], nmax[:, n:n + 1], -0.01 * NEG, None, ALU.min).then_inc(s.maxed, 1)
                if 1 <= n <= N:
                    m = n - 1
                    c = coef[:, m:m + 1]
                    dve.wait_ge(s.exped, m + 1)
                    step(dve.tensor_scalar(c, esum[:, m:m + 1], 1e-30, None, ALU.max))
                    step(dve.reciprocal(c, c))
                    i, h, br = units[m]
                    step(dve.tensor_tensor(c, c, S.gates[:, i, 4 * br + h:4 * br + h + 1], ALU.mult))
                if n >= 2:
                    m = n - 2
                    i, h, br = units[m]
                    out, src = o[:, i, h * HD:h * HD + HD], psum[:, 4 + m % 2, 0:HD]
                    dve.wait_ge(s.pv, m + 1)
                    if br == 0:
                        dve.tensor_scalar(out, src, coef[:, m:m + 1], None, ALU.mult).then_inc(s.summed, 1)
                    else:
                        dve.wait_ge(s.summed, m)
                        dve.scalar_tensor_tensor(out, src, coef[:, m:m + 1], out, ALU.mult, ALU.add).then_inc(s.summed, 1)


def sample_scores(S, l, ctx):
    nc, io, sb, psum, C = S.nc, S.io, S.sb, S.psum, S.C
    H = lambda t: S.HT[:, t - 6, :]
    S.q_rows = sb("q_rows", [P, P], ctx=ctx)
    S.st_sel = sb("st_sel", [P, NPG, P], ctx=ctx)
    S.st_cmp = sb("st_cmp", [P, 2, P], ctx=ctx)
    S.st_win = sb("st_win", [P, 4, P], ctx=ctx)
    S.vc = sb("vc_s", [P, 2, NB, P], ctx=ctx)
    with stage(nc, "q", "zero", "placed") as (block, s):
        @block.vector
        def _(dve):
            dve.memset(S.q_rows[:, :], 0.0).then_inc(s.zero, 1)
            dve.wait_ge(s.zero, 1)
            rows = S.q_rows[:, :].rearrange("p (b k g t) -> p b k g t", b=NB, k=KVH, g=GRP)
            for k in range(KVH):
                r = slice(64 * k, 64 * k + 64)
                for g in range(GRP):
                    dve.tensor_copy(rows[r, :, k, g, :], H(T_Q + g)[r, SEQ:].rearrange("p (b t) -> p b t", b=NB)).then_inc(s.placed, 1)

    with ExitStack() as c:
        slots, gp = 3, 4
        NG = NPG // gp
        cache = sb("cache", [P, slots, gp, 3 * P], ctx=c)
        chunks = sb("chunks", [P, 2, 16, NCH], ctx=c)
        kt = sb("kt", [P, 2, gp * P], ctx=c)
        hid = sb("hid", [P, 2, NCB], ctx=c)
        kc = sb("kc_s", [P, NCB], ctx=c)
        wk = sb("wk", [P, 4, P], ctx=c)
        wkt = kt[:, 0, :]
        names = ("turned", "k_copied", "v_copied", "sel_act", "sel_dve", "scored", "sc_copied", "summed", "swish", "second",
                 "kc_copied", "vc_copied", "cmp_scored", "cmp_copied", "w_turned", "w_copied", "w_scored", "w_sc_copied", "w_loaded",
                 "loaded0", "loaded1", "loaded2")
        with nc.Fori(0, NB) as b:
            with stage(nc, "scores", *names) as (block, s):
                loaded = [s.loaded0, s.loaded1, s.loaded2]
                cols = ds(b * 16, 16)

                @block.sync
                def _(sp):
                    for g in range(NG):
                        if g >= slots:
                            sp.wait_ge(s.turned, g - slots + 1)
                        for j in range(gp):
                            page = sp.value_load(S.pages[0:1, ds(b * NPG + (g * gp + j), 1)], min_val=0, max_val=io.n_pool - 1)
                            src = layer(io.cache_nsa_kv, l)[ds(page, 1)].rearrange("a t c k d -> (a t) (c k d)")
                            sp.dma_start(cache[:, g % slots, j, :], src[:, 0:3 * P]).then_inc(loaded[g % slots], 16)
                        if g == 0:
                            src = layer(io.cache_win_kv, l)[ds(b, 1)].rearrange("a (j p) c k d -> p (a j) c (k d)", p=P)
                            sp.dma_start(wk[:, :, :], src[:, :, 0, :]).then_inc(s.w_loaded, 16)

                @block.tensor
                def _(pe):
                    def turn(g):
                        pe.wait_ge(loaded[g % slots], 16 * gp * (g // slots + 1))
                        if g >= 2:
                            pe.wait_ge(s.k_copied, g - 1)
                            pe.wait_ge(s.v_copied, g - 1)
                            pe.wait_ge(s.sel_dve if g % 2 else s.sel_act, g // 2)
                        for c in (2, 0, 1):
                            for j in range(gp):
                                last = pe.transpose(psum[:, 3 * (g % 2) + c, j * P:j * P + P],
                                                    cache[:, g % slots, j, c * P:c * P + P], C["ident"])
                        last.then_inc(s.turned, 1)

                    def score(g):
                        pe.wait_ge(s.sel_dve if g % 2 else s.sel_act, g // 2 + 1)
                        for j in range(gp):
                            t = g * gp + j
                            last = pe.matmul(psum[:, 6, t * 16:t * 16 + 16], kt[:, g % 2, j * P:j * P + P], S.q_rows[:, cols],
                                             start=True, stop=True)
                        last.then_inc(s.scored, 1)

                    for g in range(NG + 1):
                        if g < NG:
                            turn(g)
                        if g >= 1:
                            score(g - 1)
                    pe.wait_ge(s.k_copied, NG)
                    pe.wait_ge(s.v_copied, NG)
                    for c in range(2):
                        for j in range(32):
                            last = pe.matmul(psum[:, 7 - 2 * c, 0:NCB], S.W1[:, c, j, :],
                                             chunks[:, c, j % 16, j // 16:j // 16 + NCB], start=(j == 0), stop=(j == 31))
                        last.then_inc(s.summed, 1)
                    pe.wait_ge(s.w_loaded, 16)
                    for j in range(4):
                        last = pe.transpose(psum[:, 3, j * P:j * P + P], wk[:, j, :], C["ident"])
                    last.then_inc(s.w_turned, 1)
                    pe.wait_ge(s.w_copied, 1)
                    for j in range(4):
                        last = pe.matmul(psum[:, 4, j * 16:j * 16 + 16], wkt[:, j * P:j * P + P], S.q_rows[:, cols], start=True, stop=True)
                    last.then_inc(s.w_scored, 1)
                    pe.wait_ge(s.swish, 2)
                    pe.matmul(psum[:, 0, 0:NCB], S.W2[:, 0, :], hid[:, 0, :], start=True, stop=True).then_inc(s.second, 1)
                    for j in range(2):
                        m = P - j
                        pe.matmul(psum[0:m, 1, j * P:j * P + P], hid[:, 1, j * P:j * P + m], S.W2[:, 1, :], start=True, stop=True).then_inc(s.second, 1)
                    pe.wait_ge(s.kc_copied, 1)
                    for j in range(2):
                        m = P - j
                        pe.matmul(psum[0:m, 2, j * 16:j * 16 + 16], kc[:, j * P:j * P + m], S.q_rows[:, cols],
                                  start=True, stop=True).then_inc(s.cmp_scored, 1)

                def by_position(bank):
                    return bank.rearrange("p (n s) -> p n s", s=16)

                def chunk_cols(c, g):
                    return chunks[:, c, :, g * 32:g * 32 + 32].rearrange("p s n -> p n s")

                @block.scalar
                def _(act):
                    for g in range(NG):
                        act.wait_ge(s.turned, g + 1)
                        if g % 2 == 0:
                            if g >= 2:
                                act.wait_ge(s.scored, g - 1)
                            act.copy(kt[:, 0, :], psum[:, 2, :]).then_inc(s.sel_act, 1)
                        act.copy(chunk_cols(0, g), by_position(psum[:, 3 * (g % 2), :])).then_inc(s.k_copied, 1)
                    for c in range(2):
                        act.wait_ge(s.summed, c + 1)
                        act.activation(hid[:, c, :], psum[:, 7 - 2 * c, 0:NCB], ACT.Silu, bias=S.pe_h[:, c:c + 1]).then_inc(s.swish, 1)
                    act.wait_ge(s.second, 3)
                    for j in range(2):
                        m = P - j
                        act.copy(S.vc[0:m, j, ds(b, 1), :].rearrange("p a n -> p (a n)"), psum[0:m, 1, j * P:j * P + P]).then_inc(s.vc_copied, 1)

                @block.vector
                def _(dve):
                    for g in range(NG):
                        dve.wait_ge(s.turned, g + 1)
                        if g % 2 == 1:
                            if g >= 2:
                                dve.wait_ge(s.scored, g - 1)
                            dve.tensor_copy(kt[:, 1, :], psum[:, 5, :]).then_inc(s.sel_dve, 1)
                        dve.tensor_copy(chunk_cols(1, g), by_position(psum[:, 3 * (g % 2) + 1, :])).then_inc(s.v_copied, 1)
                    dve.wait_ge(s.scored, NG)
                    dve.tensor_copy(S.st_sel[:, :, cols], psum[:, 6, :].rearrange("p (t r) -> p t r", r=16)).then_inc(s.sc_copied, 1)
                    dve.wait_ge(s.w_turned, 1)
                    dve.tensor_copy(wkt, psum[:, 3, :]).then_inc(s.w_copied, 1)
                    dve.wait_ge(s.w_scored, 1)
                    dve.tensor_copy(S.st_win[:, :, cols], psum[:, 4, 0:64].rearrange("p (t r) -> p t r", r=16)).then_inc(s.w_sc_copied, 1)
                    dve.wait_ge(s.second, 3)
                    dve.tensor_copy(kc[:, :], psum[:, 0, 0:NCB]).then_inc(s.kc_copied, 1)
                    dve.wait_ge(s.cmp_scored, 2)
                    for j in range(2):
                        m = P - j
                        dve.tensor_copy(S.st_cmp[0:m, j, cols], psum[0:m, 2, j * 16:j * 16 + 16]).then_inc(s.cmp_copied, 1)


def sample_attention(S, l, ctx):
    nc, io, sb, psum, C = S.nc, S.io, S.sb, S.psum, S.C
    H = lambda t: S.HT[:, t - 6, :]
    NSC = PAST + NS
    near, new, cmp_bias, far = S.sbias[:, 0:128], S.sbias[:, 128:160], S.sbias[:, 160:160 + NCB], S.sbias[:, 415:416]
    by_head = sb("by_head", [P, 3, HEADS], ctx=ctx)
    gate = sb("gate", [P, 3], ctx=ctx)
    stat = sb("stat", [P, 3, 3], ctx=ctx)
    pc = sb("pc", [P, 264], ctx=ctx)
    imp = sb("imp", [P, 2, NBLK + 1], ctx=ctx)
    score = sb("score", [P, 3, NBLK + 1], ctx=ctx)
    top = sb("top", [P, 2, 8], ctx=ctx)
    block_bias = sb("block_bias", [P, NBLK + 1], ctx=ctx)
    diag = sb("diag", [P, 3, P], ctx=ctx)
    pt_cmp = sb("pt_cmp", [P, 2, P], ctx=ctx)
    pt_new = sb("pt_new", [NS, 2, P], ctx=ctx)
    p_sel = sb("p_sel", [P, NSC], ctx=ctx)
    p_win = sb("p_win", [P, 512 + NS], ctx=ctx)
    pt_sel, pt_win = S.st_sel, S.st_win

    with stage(nc, "top", "g_prod", "g_step", "st_turned", "step", "zero", "added", "maxed", "exped", "pc", "imp", "imp2",
               "bb", "diag", "c_turned", "pt_copied") as (block, s):
        @block.tensor
        def _(pe):
            pe.matmul(psum[:, 0, 0:12], C["s_row"], S.gates[0:NS, QT, :], start=True, stop=True).then_inc(s.g_prod, 1)
            for j in range(2):
                m = P - j
                pe.transpose(psum[:, 1, j * P:j * P + m], S.st_cmp[0:m, j, :], C["ident"][0:m, 0:m]).then_inc(s.st_turned, 1)
            pe.wait_ge(s.imp, 1)
            pe.matmul(psum[:, 2, 0:NBLK + 1], C["pair"], imp[:, 1, :], start=True, stop=True).then_inc(s.imp2, 1)
            pe.wait_ge(s.diag, 1)
            for j in range(2):
                m = P - j
                pe.matmul(psum[0:m, 3, j * P:j * P + P], pc[:, 4 + j * P:4 + j * P + m], diag[:, 0, :], start=True, stop=True).then_inc(s.c_turned, 1)

        @block.scalar
        def _(act):
            act.wait_ge(s.maxed, 1)
            act.activation(pc[:, 4:4 + NCB], pc[:, 4:4 + NCB], ACT.Exp, bias=stat[:, 0, 0:1], accum_out=stat[:, 0, 1:2]).then_inc(s.exped, 1)
            act.wait_ge(s.c_turned, 2)
            for j in range(2):
                m = P - j
                act.copy(pt_cmp[0:m, j, :], psum[0:m, 3, j * P:j * P + P]).then_inc(s.pt_copied, 1)

        @block.vector
        def _(dve):
            step = Serial(dve, s.step)
            dve.memset(pc[:, :], 0.0).then_inc(s.zero, 1)
            dve.wait_ge(s.g_prod, 1)
            heads = bass.AP(C["row_head"].tensor, C["row_head"].offset, [list(C["row_head"].ap[0]), [0, 3], [1, HEADS]])
            step(dve.tensor_tensor(by_head[:, :, :], psum[:, 0, 0:12].rearrange("p (c h) -> p c h", c=3), heads, ALU.mult))
            dve.tensor_reduce(gate[:, :], by_head[:, :, :], AX.X, ALU.add).then_inc(s.g_step, 1)
            dve.wait_ge(s.st_turned, 2)
            dve.wait_ge(s.zero, 1)
            step(dve.tensor_tensor(pc[:, 4:4 + NCB], psum[:, 1, 0:NCB], cmp_bias, ALU.add), s.added)
            dve.tensor_reduce(stat[:, 0, 0:1], pc[:, 4:4 + NCB], AX.X, ALU.max, negate=True).then_inc(s.maxed, 1)
            dve.wait_ge(s.exped, 1)
            step(dve.reciprocal(stat[:, 0, 2:3], stat[:, 0, 1:2]))
            step(dve.tensor_scalar(pc[:, 4:4 + NCB], pc[:, 4:4 + NCB], stat[:, 0, 2:3], None, ALU.mult), s.pc)
            dve.wait_ge(s.g_step, 1)
            dve.tensor_scalar(diag[:, 0, :], C["ident"], gate[:, 0:1], None, ALU.mult).then_inc(s.diag, 1)
            step(dve.tensor_reduce(imp[:, 0, :], pc[:, 4:264].rearrange("p (j n) -> p j n", n=4), AX.X, ALU.add))
            dve.tensor_tensor(imp[:, 1, :], imp[:, 0, :], pc[:, 3:3 + 4 * NBLK + 1:4], ALU.add).then_inc(s.imp, 1)
            dve.wait_ge(s.imp2, 1)
            step(dve.tensor_tensor(score[:, 0, :], psum[:, 2, 0:NBLK + 1], C["force"], ALU.add))
            for r in range(2):
                step(dve.max(top[:, r, :], score[:, r, :]))
                step(dve.match_replace(score[:, r + 1, :], top[:, r, :], score[:, r, :], NEG))
            step(dve.tensor_scalar(block_bias[:, :], score[:, 2, :], 0.1 * NEG, NEG, ALU.is_gt, ALU.mult))
            dve.tensor_scalar(block_bias[:, :], block_bias[:, :], far, None, ALU.add).then_inc(s.bb, 1)

    NQ = NPG // 4
    with stage(nc, "soft", "turned", "added", "new_scored", "new_added", "w_step", "maxed", "exped", "step", "diag", "pt_turned",
               "pt_copied") as (block, s):
        @block.tensor
        def _(pe):
            for q in range(NQ + 1):
                if q >= 4:
                    pe.wait_ge(s.added, q - 3)
                src = S.st_sel if q < NQ else S.st_win
                for j in range(4):
                    last = pe.transpose(psum[:, q % 4, j * P:j * P + P], src[:, (4 * q + j) if q < NQ else j, :], C["ident"])
                last.then_inc(s.turned, 1)
            pe.matmul(psum[:, 4, 0:NS], S.q_rows[:, :], H(T_KV + 2)[:, SEQ:], start=True, stop=True).then_inc(s.new_scored, 1)
            pe.matmul(psum[:, 5, 0:NS], S.q_rows[:, :], H(T_KV + 4)[:, SEQ:], start=True, stop=True).then_inc(s.new_scored, 1)
            pe.wait_ge(s.added, NQ + 1)
            for q in range(NQ + 2):
                if q >= 4:
                    pe.wait_ge(s.pt_copied, q - 3)
                br = 1 if q == NQ else 0
                pe.wait_ge(s.diag, 2 if q >= NQ else 1)
                if q <= NQ:
                    for j in range(4):
                        x = p_sel[:, (4 * q + j) * P:(4 * q + j + 1) * P] if q < NQ else p_win[:, j * P:j * P + P]
                        last = pe.matmul(psum[:, q % 4, j * P:j * P + P], x, diag[:, 1 + br, :], start=True, stop=True)
                else:
                    pe.matmul(psum[0:NS, q % 4, 0:P], p_sel[:, PAST:], diag[:, 1, :], start=True, stop=True)
                    last = pe.matmul(psum[0:NS, q % 4, P:2 * P], p_win[:, 512:], diag[:, 2, :], start=True, stop=True)
                last.then_inc(s.pt_turned, 1)

        @block.vector
        def _(dve):
            step = Serial(dve, s.step)
            for q in range(NQ):
                dve.wait_ge(s.turned, q + 1)
                dve.tensor_tensor(p_sel[:, 512 * q:512 * q + 512].rearrange("p (j n) -> p j n", n=64),
                                  psum[:, q % 4, :].rearrange("p (j n) -> p j n", n=64), bc(block_bias[:, 8 * q:8 * q + 8], 64),
                                  ALU.add).then_inc(s.added, 1)
            dve.wait_ge(s.turned, NQ + 1)
            dve.tensor_scalar(p_win[:, 0:512], psum[:, NQ % 4, :], far, None, ALU.add).then_inc(s.added, 1)
            dve.wait_ge(s.new_scored, 2)
            dve.tensor_tensor(p_sel[:, PAST:], psum[:, 4, 0:NS], new, ALU.add).then_inc(s.new_added, 1)
            dve.tensor_tensor(p_win[:, 512:], psum[:, 5, 0:NS], new, ALU.add).then_inc(s.new_added, 1)
            dve.wait_ge(s.added, NQ + 1)
            dve.tensor_tensor(p_sel[:, PAST - P:PAST], p_sel[:, PAST - P:PAST], near, ALU.add).then_inc(s.new_added, 1)
            dve.tensor_tensor(p_win[:, 384:512], p_win[:, 384:512], near, ALU.add).then_inc(s.new_added, 1)
            dve.tensor_tensor(p_win[:, 0:NT], p_win[:, 0:NT], C["win_old"], ALU.add).then_inc(s.new_added, 1)
            dve.wait_ge(s.new_added, 5)
            dve.tensor_reduce(stat[:, 1, 0:1], p_sel[:, :], AX.X, ALU.max, negate=True).then_inc(s.maxed, 1)
            dve.tensor_reduce(stat[:, 2, 0:1], p_win[:, :], AX.X, ALU.max, negate=True).then_inc(s.maxed, 1)
            for br in (1, 2):
                dve.wait_ge(s.exped, br)
                step(dve.reciprocal(stat[:, br, 2:3], stat[:, br, 1:2]))
                step(dve.tensor_tensor(stat[:, br, 2:3], stat[:, br, 2:3], gate[:, br:br + 1], ALU.mult))
                dve.tensor_scalar(diag[:, br, :], C["ident"], stat[:, br, 2:3], None, ALU.mult).then_inc(s.diag, 1)
            for q in range(1, NQ + 2, 2):
                dve.wait_ge(s.pt_turned, q + 1)
                dst = pt_sel[:, 4 * q:4 * q + 4, :] if q < NQ else pt_new[:, :, :]
                src = psum[:, q % 4, :] if q < NQ else psum[0:NS, q % 4, 0:2 * P]
                dve.wait_ge(s.pt_copied, q)
                dve.tensor_copy(dst, src.rearrange("p (t n) -> p t n", n=P)).then_inc(s.pt_copied, 1)

        @block.scalar
        def _(act):
            act.wait_ge(s.maxed, 1)
            act.activation(p_sel[:, :], p_sel[:, :], ACT.Exp, bias=stat[:, 1, 0:1], accum_out=stat[:, 1, 1:2]).then_inc(s.exped, 1)
            act.wait_ge(s.maxed, 2)
            act.activation(p_win[:, :], p_win[:, :], ACT.Exp, bias=stat[:, 2, 0:1], accum_out=stat[:, 2, 1:2]).then_inc(s.exped, 1)
            for q in range(0, NQ + 1, 2):
                act.wait_ge(s.pt_turned, q + 1)
                if q:
                    act.wait_ge(s.pt_copied, q)
                dst = pt_sel[:, 4 * q:4 * q + 4, :] if q < NQ else pt_win[:, :, :]
                act.copy(dst, psum[:, q % 4, :].rearrange("p (t n) -> p t n", n=P)).then_inc(s.pt_copied, 1)

    vsel = sb("vsel", [P, NPG, P], ctx=ctx)
    vwin = sb("vwin", [P, 4, P], ctx=ctx)
    vcmp = sb("vcmp", [P, 2, P], ctx=ctx)
    out = sb("out_s", [P, P], ctx=ctx)
    with nc.Fori(0, NB) as b:
        with stage(nc, "pv", "loaded0", "loaded1", "loaded2", "loaded3", "w_loaded", "moved", "product", "copied") as (block, s):
            loaded = [s.loaded0, s.loaded1, s.loaded2, s.loaded3]
            cols = ds(b * 16, 16)

            @block.sync
            def _(sp):
                for g in range(4):
                    for j in range(8):
                        t = 8 * g + j
                        page = sp.value_load(S.pages[0:1, ds(b * NPG + t, 1)], min_val=0, max_val=io.n_pool - 1)
                        src = layer(io.cache_nsa_kv, l)[ds(page, 1)].rearrange("a t c k d -> (a t) (c k d)")
                        sp.dma_start(vsel[:, t, :], src[:, 3 * P:4 * P]).then_inc(loaded[g], 16)
                    if g == 0:
                        src = layer(io.cache_win_kv, l)[ds(b, 1)].rearrange("a (j p) c k d -> p (a j) c (k d)", p=P)
                        sp.dma_start(vwin[:, :, :], src[:, :, 1, :]).then_inc(s.w_loaded, 16)

            @block.scalar
            def _(act):
                for j in range(2):
                    m = P - j
                    act.copy(vcmp[0:m, j, :], S.vc[0:m, j, ds(b, 1), :].rearrange("p a n -> p (a n)")).then_inc(s.moved, 1)
                act.wait_ge(s.product, 1)
                act.copy(out[:, cols], psum[:, 0, 0:16]).then_inc(s.copied, 1)

            @block.tensor
            def _(pe):
                o = psum[:, 0, 0:16]
                pe.matmul(o, S.kv_s[:, 3 * P:4 * P], pt_new[:, 0, cols], start=True, stop=False)
                pe.matmul(o, S.kv_s[:, 5 * P:6 * P], pt_new[:, 1, cols], start=False, stop=False)
                pe.wait_ge(s.moved, 2)
                for j in range(2):
                    m = P - j
                    pe.matmul(o, vcmp[0:m, j, :], pt_cmp[0:m, j, cols], start=False, stop=False)
                for g in range(4):
                    pe.wait_ge(loaded[g], 128)
                    for t in range(8 * g, 8 * g + 8):
                        pe.matmul(o, vsel[:, t, :], pt_sel[:, t, cols], start=False, stop=False)
                pe.wait_ge(s.w_loaded, 16)
                for j in range(4):
                    last = pe.matmul(o, vwin[:, j, :], pt_win[:, j, cols], start=False, stop=(j == 3))
                last.then_inc(s.product, 1)

    with stage(nc, "place", "placed") as (block, s):
        @block.vector
        def _(dve):
            rows = out[:, :].rearrange("p (b k g t) -> p b k g t", b=NB, k=KVH, g=GRP)
            for k in range(KVH):
                for g in range(GRP):
                    dve.tensor_copy(S.yT[64 * g:64 * g + 64, 4 + k, SEQ:].rearrange("p (b t) -> p b t", b=NB),
                                    rows[64 * k:64 * k + 64, :, k, g, :]).then_inc(s.placed, 1)


def gated_delta(S, l, ctx):
    nc, io, sb, psum, C = S.nc, S.io, S.sb, S.psum, S.C
    H = lambda t: S.HT[:, t - 6, :]
    ident = C["ident"]
    NQ = QT + 1
    rows = [P] * QT + [NS]
    upto = [C["upto"]] * QT + [C["s_upto"]]
    total = [C["ones"]] * QT + [C["s_ones"]]
    after = [C["after"]] * QT + [C["s_after"]]
    a_b = sb("a_log_b", [P, HEADS], ctx=ctx)
    dt_b = sb("dt_bias_b", [P, HEADS], ctx=ctx)
    taps = sb("gtaps", [P, 6, 5], ctx=ctx)
    nat = sb("gnat", [P, NQ, 768], ctx=ctx)
    g = sb("g", [P, NQ, HEADS], ctx=ctx)
    beta = sb("beta", [P, NQ, HEADS], ctx=ctx)
    with ExitStack() as c:
        cv = sb("cv", [P, 6, TOK], ctx=c)
        grow = sb("grow", [5, 768], ctx=c)
        gst = sb("gst", [24, 768], ctx=c)
        us = sb("gus", [P, 6, NB, GC - 1 + NT], ctx=c)
        pack = sb("gpack", [P, 6, 24], ctx=c)
        stp = sb("stp", [GC - 1, 768], ctx=c)
        sts = sb("sts", [24, 768], ctx=c)
        sq = sb("gsq", [P, NQ, 512], ctx=c)
        rn = sb("rn", [P, NQ, 8], ctx=c)
        sp_ = sb("softplus", [P, 3, NQ, HEADS], ctx=c)
        names = ("loaded", "packed", "turned", "copied", "stored", "taps", "conv", "swish", "n_turned", "n_act", "n_dve", "squared",
                 "rsum", "rn", "a_sum", "act_step", "soft", "beta", "step", "normed")
        with stage(nc, "gconv", *names) as (block, s):
            @block.sync
            def _(sp):
                sp.dma_start(grow[0:4, :], layer(io.gdn_conv_w, l)).then_inc(s.loaded, 16)
                for i in range(2):
                    sp.dma_start(grow[4:5, 64 * i:64 * i + 64], io.gdn_norm_g[ds(l, 1)]).then_inc(s.loaded, 16)
                sp.dma_start(gst[:, :], layer(io.state_gdn_conv, l).rearrange("b w c -> (b w) c")).then_inc(s.loaded, 16)
                for dst, src in ((a_b, io.gdn_a_log), (dt_b, io.gdn_dt_bias)):
                    row = src[ds(l, 1)]
                    sp.dma_start(dst[:, :], bass.AP(row.tensor, row.offset, [[0, P], [1, HEADS]])).then_inc(s.loaded, 16)
                sp.wait_ge(s.copied, 6)
                sp.dma_start(layer(io.prompt_gconv, l)[0], stp[:, :]).then_inc(s.stored, 16)
                sp.dma_start(layer(io.sample_gconv, l).rearrange("b w c -> (b w) c"), sts[:, :]).then_inc(s.stored, 16)
                sp.wait_ge(s.stored, 32)

            @block.gpsimd
            def _(pool):
                for j in range(6):
                    x = H(T_GDN + j)[:, SEQ:].rearrange("p (b t) -> p b t", b=NB)
                    pool.tensor_copy(us[:, j, :, GC - 1:], x).then_inc(s.packed, 1)
                    pool.tensor_copy(pack[:, j, :].rearrange("p (b t) -> p b t", b=NB), x[:, :, 1:]).then_inc(s.packed, 1)

            @block.tensor
            def _(pe):
                pe.wait_ge(s.loaded, 96)
                pe.wait_ge(s.packed, 12)
                for j in range(6):
                    f = slice(j * P, j * P + P)
                    n = 5 if j == 0 else 4
                    pe.transpose(psum[:, 0, 8 * j:8 * j + n], grow[0:n, f], ident[0:n, 0:n])
                    pe.transpose(psum[:, 1, 24 * j:24 * j + 24], gst[:, f], ident[0:24, 0:24])
                    at = slice(P * (j % 4), P * (j % 4) + P)
                    pe.transpose(psum[0:GC - 1, 2 + j // 4, at], H(T_GDN + j)[:, SEQ - GC + 1:SEQ], ident)
                    last = pe.transpose(psum[0:24, 4 + j // 4, at], pack[:, j, :], ident)
                last.then_inc(s.turned, 1)
                pe.wait_ge(s.swish, 6)
                for q in range(NQ):
                    n, a = rows[q], 2 * (q % 2)
                    if q >= 2:
                        pe.wait_ge(s.n_act, q - 1)
                        pe.wait_ge(s.n_dve, q - 1)
                    for j in range(6):
                        last = pe.transpose(psum[0:n, a + j // 4, (j % 4) * P:(j % 4) * P + P], cv[:, j, q * P:q * P + n], ident)
                    last.then_inc(s.n_turned, 1)

            @block.scalar
            def _(act):
                act.wait_ge(s.turned, 1)
                tap = psum[:, 0, 0:48].rearrange("p (j n) -> p j n", n=8)
                act.copy(taps[:, 0, :], tap[:, 0, 0:5]).then_inc(s.copied, 1)
                act.copy(taps[:, 1:6, 0:4], tap[:, 1:6, 0:4]).then_inc(s.copied, 1)
                act.copy(stp[:, 0:512], psum[0:GC - 1, 2, :])
                act.copy(stp[:, 512:768], psum[0:GC - 1, 3, 0:256]).then_inc(s.copied, 1)
                act.copy(sts[:, 0:512], psum[0:24, 4, :])
                act.copy(sts[:, 512:768], psum[0:24, 5, 0:256]).then_inc(s.copied, 1)
                for j in range(2):
                    act.copy(us[:, 3 * j:3 * j + 3, :, 0:GC - 1],
                             psum[:, 1, 72 * j:72 * j + 72].rearrange("p (j b w) -> p j b w", j=3, b=NB)).then_inc(s.copied, 1)
                step = Serial(act, s.act_step)
                act.wait_ge(s.a_sum, 1)
                step(act.activation(sp_[:, 1, :, :], sp_[:, 0, :, :], ACT.Abs))
                step(act.activation(sp_[:, 1, :, :], sp_[:, 1, :, :], ACT.Exp, scale=-1.0))
                step(act.activation(a_b[:, :], a_b[:, :], ACT.Exp))
                act.activation(sp_[:, 1, :, :], sp_[:, 1, :, :], ACT.Ln, bias=C["ones"][:, 0:1]).then_inc(s.soft, 1)
                for j in range(6):
                    act.wait_ge(s.conv, j + 1)
                    act.activation(cv[:, j, :], cv[:, j, :], ACT.Silu).then_inc(s.swish, 1)
                act.activation(beta[:, :, :], S.misc_n[:, :, M_B:M_B + 4], ACT.Sigmoid).then_inc(s.beta, 1)
                for j in range(2):
                    act.activation(H(T_Z + j), H(T_Z + j), ACT.Silu).then_inc(s.beta, 1)
                for q in range(NQ):
                    n = rows[q]
                    act.wait_ge(s.n_turned, q + 1)
                    act.copy(nat[0:n, q, 0:512], psum[0:n, 2 * (q % 2), :]).then_inc(s.n_act, 1)
                    act.wait_ge(s.n_act, q + 1)
                    act.activation(sq[0:n, q, :], nat[0:n, q, 0:512], ACT.Square).then_inc(s.squared, 1)
                act.wait_ge(s.rsum, 2)
                step(act.activation(rn[:, :, :], rn[:, :, :], ACT.Ln, bias=C["eps"][:, 1:2]))
                act.activation(rn[:, :, :], rn[:, :, :], ACT.Exp, scale=-0.5).then_inc(s.rn, 1)

            @block.vector
            def _(dve):
                step = Serial(dve, s.step)
                dve.wait_ge(s.loaded, 96)
                dve.tensor_tensor(sp_[:, 0, :, :], S.misc_n[:, :, M_A:M_A + 4], bc_mid(dt_b[:, :], NQ), ALU.add).then_inc(s.a_sum, 1)
                dve.wait_ge(s.copied, 6)
                for j in range(6):
                    x, out = H(T_GDN + j), cv[:, j, :]
                    step(dve.tensor_scalar(out[:, 0:SEQ], x[:, 0:SEQ], taps[:, j, 3:4], None, ALU.mult))
                    outs = out[:, SEQ:].rearrange("p (b t) -> p b t", b=NB)
                    step(dve.tensor_scalar(outs, us[:, j, :, 3:3 + NT], taps[:, j, 3:4], None, ALU.mult))
                    for w in (2, 1, 0):
                        d = 3 - w
                        dve.scalar_tensor_tensor(out[:, d:SEQ], x[:, 0:SEQ - d], taps[:, j, w:w + 1], out[:, d:SEQ], ALU.mult, ALU.add).then_inc(s.taps, 1)
                        dve.scalar_tensor_tensor(outs, us[:, j, :, w:w + NT], taps[:, j, w:w + 1], outs, ALU.mult, ALU.add).then_inc(s.taps, 1)
                        dve.wait_ge(s.taps, 6 * j + 2 * d)
                    dve.engine_nop().then_inc(s.conv, 1)
                dve.wait_ge(s.soft, 1)
                step(dve.tensor_scalar(sp_[:, 0, :, :], sp_[:, 0, :, :], 0.0, None, ALU.max))
                step(dve.tensor_tensor(sp_[:, 0, :, :], sp_[:, 0, :, :], sp_[:, 1, :, :], ALU.add))
                step(dve.tensor_tensor(sp_[:, 0, :, :], sp_[:, 0, :, :], bc_mid(a_b[:, :], NQ), ALU.mult))
                step(dve.tensor_scalar(g[:, :, :], sp_[:, 0, :, :], -1.0, None, ALU.mult))
                dve.memset(rn[:, QT, :], 1.0).then_inc(s.rsum, 1)
                for q in range(NQ):
                    n = rows[q]
                    dve.wait_ge(s.n_turned, q + 1)
                    dve.tensor_copy(nat[0:n, q, 512:768], psum[0:n, 2 * (q % 2) + 1, 0:256]).then_inc(s.n_dve, 1)
                for q in range(NQ):
                    n = rows[q]
                    dve.wait_ge(s.squared, q + 1)
                    dve.wait_ge(s.rsum, 1)
                    last = dve.tensor_reduce(rn[0:n, q, :], sq[0:n, q, :].rearrange("p (j n) -> p j n", n=HD), AX.X, ALU.add)
                last.then_inc(s.rsum, 1)
                dve.wait_ge(s.rn, 1)
                step(dve.tensor_scalar(rn[:, :, 0:4], rn[:, :, 0:4], HD ** -0.5, None, ALU.mult))
                for q in range(NQ):
                    n = rows[q]
                    x = nat[0:n, q, 0:512].rearrange("p (j n) -> p j n", n=HD)
                    dve.tensor_tensor(x, x, bc(rn[0:n, q, :], HD), ALU.mult).then_inc(s.normed, 1)

    DTs = lambda t, q: t[0:rows[q], q, :, 0:rows[q]]
    lt = sb("lt", [P, NQ, HEADS, P], ctx=ctx)
    qk = sb("qk", [P, NQ, HEADS, P], ctx=ctx)
    inv_t = sb("inv_t", [P, NQ, HEADS, P], ctx=ctx)
    inv = sb("inv", [P, NQ, HEADS, P], ctx=ctx)
    uw = sb("uw", [P, NQ, HEADS, P], ctx=ctx)
    kl = sb("kl", [P, NQ, HEADS, HD], ctx=ctx)
    qs = sb("qs", [HD, NQ, HEADS, P], ctx=ctx)
    glast = sb("glast", [HD, HEADS, QT + NB], ctx=ctx)
    with ExitStack() as c:
        gb = sb("gb", [P, HEADS, P], ctx=c)
        egb = sb("egb", [HD, HEADS, P], ctx=c)
        dec = sb("dec", [P, HEADS, P], ctx=c)
        kT = sb("kT", [HD, HEADS, P], ctx=c)
        kbT = sb("kbT", [HD, HEADS, P], ctx=c)
        qT = sb("qT", [HD, HEADS, P], ctx=c)
        kb = sb("kb", [P, HEADS, HD], ctx=c)
        gc = sb("gc", [P, NQ, 5, HEADS], ctx=c)
        names = ("gb", "cum", "cumb", "gcum", "rest", "neg", "exp", "egb", "dec0", "dec", "dstep", "kb", "nats", "turned", "t_copied",
                 "qt", "qs", "products", "lt", "qk")
        with stage(nc, "gmat", *names) as (block, s):
            @block.tensor
            def _(pe):
                for q in range(NQ):
                    n = rows[q]
                    pe.wait_ge(s.gb, q + 1)
                    if q:
                        pe.wait_ge(s.gcum, q)
                        pe.wait_ge(s.dec0, q)
                        pe.wait_ge(s.egb, q)
                    pe.matmul(psum[0:n, 0, 0:4], upto[q], g[0:n, q, :], start=True, stop=True)
                    pe.matmul(psum[0:n, 0, 4:8], total[q], g[0:n, q, :], start=True, stop=True).then_inc(s.cum, 1)
                    for h in range(HEADS):
                        last = pe.matmul(psum[:, 1, h * P:h * P + n], gb[0:n, h, :], upto[q], start=True, stop=True)
                    last.then_inc(s.cumb, 1)
                    pe.wait_ge(s.kb, q + 1)
                    if q:
                        pe.wait_ge(s.t_copied, 3 * q)
                        pe.wait_ge(s.qs, q)
                    for i, src in enumerate((lambda h: nat[0:n, q, 256 + h * HD:320 + h * HD], lambda h: kb[0:n, h, :],
                                             lambda h: nat[0:n, q, h * HD:h * HD + HD])):
                        for h in range(HEADS):
                            last = pe.transpose(psum[0:HD, 2 + i, h * P:h * P + n], src(h), ident[0:n, 0:n])
                        last.then_inc(s.turned, 1)
                    pe.wait_ge(s.t_copied, 3 * q + 3)
                    if q:
                        pe.wait_ge(s.qk, q)
                    for h in range(HEADS):
                        pe.matmul(psum[0:n, 5, h * P:h * P + n], kT[:, h, 0:n], kbT[:, h, 0:n], start=True, stop=True)
                        last = pe.matmul(psum[0:n, 6, h * P:h * P + n], kT[:, h, 0:n], qT[:, h, 0:n], start=True, stop=True)
                    last.then_inc(s.products, 1)

            def heads(bank, n, m):
                return psum[0:n, bank, :].rearrange("p (h m) -> p h m", h=HEADS)[:, :, 0:m]

            @block.scalar
            def _(act):
                for q in range(NQ):
                    n = rows[q]
                    act.wait_ge(s.rest, q + 1)
                    act.activation(gc[0:n, q, 3:5, :], gc[0:n, q, 3:5, :], ACT.Exp).then_inc(s.exp, 1)
                    act.wait_ge(s.dec0, q + 1)
                    if q:
                        act.wait_ge(s.qs, q)
                    act.activation(egb[:, :, 0:n], heads(1, HD, n), ACT.Exp).then_inc(s.egb, 1)
                    for h in range(HEADS):
                        last = act.activation(dec[0:n, h, 0:n], dec[0:n, h, 0:n], ACT.Exp, bias=gc[0:n, q, 2, h:h + 1])
                    last.then_inc(s.dec, 1)
                    for i, dst in enumerate((kT, kbT, qT)):
                        act.wait_ge(s.turned, 3 * q + i + 1)
                        if q and i == 0:
                            act.wait_ge(s.products, q)
                        act.copy(dst[:, :, 0:n], heads(2 + i, HD, n)).then_inc(s.t_copied, 1)

            @block.vector
            def _(dve):
                for q in range(NQ):
                    n = rows[q]
                    k = nat[0:n, q, 256:512].rearrange("p (h d) -> p h d", h=HEADS)
                    v = nat[0:n, q, 512:768].rearrange("p (h d) -> p h d", h=HEADS)
                    if q:
                        dve.wait_ge(s.cumb, q)
                    dve.tensor_copy(gb[0:n, :, :], bc(g[0:n, q, :], P)).then_inc(s.gb, 1)
                    if q:
                        dve.wait_ge(s.turned, 3 * q)
                        dve.wait_ge(s.nats, 3 * q)
                    dve.tensor_tensor(kb[0:n, :, :], k, bc(beta[0:n, q, :], HD), ALU.mult).then_inc(s.kb, 1)
                    dve.tensor_tensor(uw[0:n, q, :, 0:HD], v, bc(beta[0:n, q, :], HD), ALU.mult).then_inc(s.nats, 1)
                    dve.wait_ge(s.cum, q + 1)
                    dve.tensor_copy(gc[0:n, q, 0:2, :], psum[0:n, 0, 0:8].rearrange("p (c h) -> p c h", c=2)).then_inc(s.gcum, 1)
                    dve.wait_ge(s.gcum, q + 1)
                    dve.tensor_copy(gc[0:n, q, 3, :], gc[0:n, q, 0, :])
                    dve.tensor_scalar(gc[0:n, q, 2, :], gc[0:n, q, 0, :], -1.0, None, ALU.mult)
                    dve.tensor_tensor(gc[0:n, q, 4, :], gc[0:n, q, 1, :], gc[0:n, q, 0, :], ALU.subtract).then_inc(s.rest, 1)
                    dve.wait_ge(s.cumb, q + 1)
                    if q:
                        dve.wait_ge(s.qk, q)
                    dve.tensor_tensor(dec[0:n, :, 0:n], heads(1, n, n), bc_mid(after[q], HEADS), ALU.add).then_inc(s.dec0, 1)
                    dve.wait_ge(s.exp, q + 1)
                    dve.wait_ge(s.kb, q + 1)
                    dve.tensor_tensor(uw[0:n, q, :, HD:], kb[0:n, :, :], bc(gc[0:n, q, 3, :], HD), ALU.mult).then_inc(s.nats, 1)
                    dve.tensor_tensor(kl[0:n, q, :, :], k, bc(gc[0:n, q, 4, :], HD), ALU.mult).then_inc(s.nats, 1)
                    dve.wait_ge(s.egb, q + 1)
                    if q < QT:
                        dve.tensor_copy(glast[:, :, q], egb[:, :, P - 1])
                    else:
                        dve.tensor_copy(glast[:, :, QT:], egb[:, :, NT - 1:NS:NT])
                    dve.wait_ge(s.t_copied, 3 * q + 3)
                    dve.tensor_tensor(qs[:, q, :, 0:n], qT[:, :, 0:n], egb[:, :, 0:n], ALU.mult).then_inc(s.qs, 1)
                    dve.wait_ge(s.products, q + 1)
                    dve.wait_ge(s.dec, q + 1)
                    dve.tensor_tensor(DTs(lt, q), heads(5, n, n), dec[0:n, :, 0:n], ALU.mult).then_inc(s.lt, 1)
                    dve.tensor_tensor(DTs(qk, q), heads(6, n, n), dec[0:n, :, 0:n], ALU.mult).then_inc(s.qk, 1)

    with ExitStack() as c:
        lm = sb("lm", [P, 2, HEADS, P], ctx=c)
        y = sb("y", [P, 2, HEADS, P], ctx=c)
        units = [(v, q) for v in range(1, 7) for q in range(NQ) if q < QT or v < 2]
        N = len(units)
        at = {u: n for n, u in enumerate(units)}
        with stage(nc, "ginv", "first", "first_t", "turned", "t_copied", "lm", "y", "y_copied", "delta", "updated", "step") as (block, s):
            def bank(b, q):
                return psum[0:rows[q], b, :].rearrange("p (h m) -> p h m", h=HEADS)[:, :, 0:rows[q]]

            @block.tensor
            def _(pe):
                for q in range(NQ):
                    n = rows[q]
                    pe.wait_ge(s.first_t, q + 1)
                    if q >= 2:
                        pe.wait_ge(s.t_copied, q - 1)
                    for h in range(HEADS):
                        last = pe.transpose(psum[0:n, 6 + q % 2, h * P:h * P + n], inv_t[0:n, q, h, 0:n], ident[0:n, 0:n])
                    last.then_inc(s.turned, 1)

                def lower(m):
                    v, q = units[m]
                    n = rows[q]
                    pe.wait_ge(s.lm, m + 1)
                    if v == 1:
                        pe.wait_ge(s.t_copied, q + 1)
                    else:
                        pe.wait_ge(s.updated, at[(v - 1, q)] + 1)
                    if m >= 2:
                        pe.wait_ge(s.y_copied, m - 1)
                    for h in range(HEADS):
                        last = pe.matmul(psum[0:n, m % 2, h * P:h * P + n], lm[0:n, m % 2, h, 0:n], inv[0:n, q, h, 0:n], start=True, stop=True)
                    last.then_inc(s.y, 1)

                def delta(m):
                    v, q = units[m]
                    n = rows[q]
                    pe.wait_ge(s.y_copied, m + 1)
                    if m >= 2:
                        pe.wait_ge(s.updated, m - 1)
                    for h in range(HEADS):
                        pe.matmul(psum[0:n, 2 + m % 2, h * P:h * P + n], inv_t[0:n, q, h, 0:n], y[0:n, m % 2, h, 0:n], start=True, stop=True)
                        last = pe.matmul(psum[0:n, 4 + m % 2, h * P:h * P + n], y[0:n, m % 2, h, 0:n], inv_t[0:n, q, h, 0:n], start=True, stop=True)
                    last.then_inc(s.delta, 1)

                for m in range(N + 1):
                    if m < N:
                        lower(m)
                    if m:
                        delta(m - 1)

            @block.gpsimd
            def _(pool):
                for m, (v, q) in enumerate(units):
                    n = rows[q]
                    if m >= 2:
                        pool.wait_ge(s.y, m - 1)
                    pool.tensor_tensor(lm[0:n, m % 2, :, 0:n], DTs(lt, q), bc_mid(C[f"level{v}"][0:n, 0:n], HEADS), ALU.mult).then_inc(s.lm, 1)

            @block.scalar
            def _(act):
                for q in range(NQ):
                    act.wait_ge(s.turned, q + 1)
                    act.copy(DTs(inv, q), bank(6 + q % 2, q)).then_inc(s.t_copied, 1)
                for m, (v, q) in enumerate(units):
                    n = rows[q]
                    act.wait_ge(s.y, m + 1)
                    if m >= 2:
                        act.wait_ge(s.delta, m - 1)
                    act.copy(y[0:n, m % 2, :, 0:n], bank(m % 2, q)).then_inc(s.y_copied, 1)

            @block.vector
            def _(dve):
                for q in range(NQ):
                    n = rows[q]
                    dve.tensor_tensor(DTs(inv_t, q), DTs(lt, q), bc_mid(C["level0"][0:n, 0:n], HEADS), ALU.mult).then_inc(s.first, 1)
                    dve.wait_ge(s.first, q + 1)
                    dve.tensor_tensor(DTs(inv_t, q), bc_mid(ident[0:n, 0:n], HEADS), DTs(inv_t, q), ALU.subtract).then_inc(s.first_t, 1)
                for m, (v, q) in enumerate(units):
                    dve.wait_ge(s.delta, m + 1)
                    dve.tensor_tensor(DTs(inv, q), DTs(inv, q), bank(2 + m % 2, q), ALU.subtract)
                    dve.tensor_tensor(DTs(inv_t, q), DTs(inv_t, q), bank(4 + m % 2, q), ALU.subtract).then_inc(s.updated, 1)

    wT = sb("wT", [HD, NQ, HEADS, P], ctx=ctx)
    state = sb("state", [HD, HEADS, HD], ctx=ctx)
    fade = sb("fade", [HD, HEADS, HD], ctx=ctx)
    vnew = sb("vnew", [P, HEADS, HD], ctx=ctx)
    st_s = sb("st_s", [HD, HEADS, NB, HD], ctx=ctx)
    fade_s = sb("fade_s", [HD, NB, HD], ctx=ctx)
    own = sb("own", [NS, NB, HD], ctx=ctx)
    ws = sb("ws", [NS, 2, HEADS, HD], ctx=ctx)
    vb = sb("vb", [NS, HEADS, NB, HD], ctx=ctx)
    rr = sb("rr", [P, NQ, HEADS], ctx=ctx)
    o = lambda q: nat[0:rows[q], q, 0:256].rearrange("p (h d) -> p h d", h=HEADS)
    uv = lambda q: nat[0:rows[q], q, 256:512].rearrange("p (h d) -> p h d", h=HEADS)
    with stage(nc, "guv", "loaded", "uv", "uv_copied", "wt_copied") as (block, s):
        @block.sync
        def _(sp):
            for h in range(HEADS):
                sp.dma_start(st_s[:, h, :, :], layer(io.state_gdn, l)[:, h].rearrange("b k v -> k b v")).then_inc(s.loaded, 16)
            sp.wait_ge(s.loaded, 64)

        @block.tensor
        def _(pe):
            for q in range(NQ):
                n = rows[q]
                if q >= 2:
                    pe.wait_ge(s.uv_copied, q - 1)
                    pe.wait_ge(s.wt_copied, q - 1)
                for h in range(HEADS):
                    pe.matmul(psum[0:n, 2 * (q % 2), h * HD:h * HD + HD], inv_t[0:n, q, h, 0:n], uw[0:n, q, h, 0:HD], start=True, stop=True)
                    last = pe.matmul(psum[0:HD, 2 * (q % 2) + 1, h * P:h * P + n], uw[0:n, q, h, HD:], inv_t[0:n, q, h, 0:n], start=True, stop=True)
                last.then_inc(s.uv, 1)

        @block.vector
        def _(dve):
            for q in range(NQ):
                dve.wait_ge(s.uv, q + 1)
                dve.tensor_copy(uv(q), psum[0:rows[q], 2 * (q % 2), 0:256].rearrange("p (h d) -> p h d", h=HEADS)).then_inc(s.uv_copied, 1)

        @block.scalar
        def _(act):
            for q in range(NQ):
                act.wait_ge(s.uv, q + 1)
                src = psum[0:HD, 2 * (q % 2) + 1, :].rearrange("p (h m) -> p h m", h=HEADS)[:, :, 0:rows[q]]
                act.copy(wT[:, q, :, 0:rows[q]], src).then_inc(s.wt_copied, 1)

    names = ("ws", "vnew", "out", "o_copied", "kv", "fade", "state", "s_w", "s_own", "s_ws", "s_vnew", "s_vb", "s_fade", "s_out",
             "s_kv", "s_state", "s_o", "o_done", "stored", "squared", "rsum", "astep", "rr", "normed", "turned", "yt", "zero", "ystep")
    with stage(nc, "gscan", *names) as (block, s):
        def squares(q):
            return uw[0:rows[q], q, 0:2, :].rearrange("p a b -> p (a b)")

        bank4 = lambda b, n: psum[0:n, b, 0:256].rearrange("p (h d) -> p h d", h=HEADS)

        @block.tensor
        def _(pe):
            for q in range(QT):
                pe.wait_ge(s.zero if q == 0 else s.state, max(q, 1))
                if q:
                    pe.wait_ge(s.o_copied, q)
                for h in range(HEADS):
                    last = pe.matmul(psum[:, 0, h * HD:h * HD + HD], wT[:, q, h, :], state[:, h, :], start=True, stop=True)
                last.then_inc(s.ws, 1)
                pe.wait_ge(s.vnew, q + 1)
                for h in range(HEADS):
                    last = pe.matmul(psum[0:HD, 2, h * HD:h * HD + HD], kl[:, q, h, :], vnew[:, h, :], start=True, stop=True)
                last.then_inc(s.kv, 1)
                for h in range(HEADS):
                    out = psum[:, 1, h * HD:h * HD + HD]
                    pe.matmul(out, qs[:, q, h, :], state[:, h, :], start=True, stop=False)
                    last = pe.matmul(out, qk[:, q, h, :], vnew[:, h, :], start=False, stop=True)
                last.then_inc(s.out, 1)
            for i, left in enumerate((wT, qs)):
                for h in range(HEADS):
                    n = 4 * i + h
                    if n >= 2:
                        pe.wait_ge(s.s_own, n - 1)
                    pe.matmul(psum[0:NS, 3 + n % 2, :], left[:, QT, h, 0:NS], st_s[:, h, :, :].rearrange("p b v -> p (b v)"),
                              start=True, stop=True).then_inc(s.s_w, 1)
            pe.wait_ge(s.s_vnew, 1)
            for h in range(HEADS):
                last = pe.matmul(psum[0:NS, 5, h * HD:h * HD + HD], qk[0:NS, QT, h, 0:NS], vnew[0:NS, h, :], start=True, stop=True)
            last.then_inc(s.s_out, 1)
            for h in range(HEADS):
                pe.wait_ge(s.s_vb, h + 1)
                if h >= 2:
                    pe.wait_ge(s.s_state, h - 1)
                pe.matmul(psum[0:HD, 6 + h % 2, :], kl[0:NS, QT, h, :], vb[:, h, :, :].rearrange("p b v -> p (b v)"),
                          start=True, stop=True).then_inc(s.s_kv, 1)
            pe.wait_ge(s.normed, NQ)
            pe.wait_ge(s.o_copied, QT)
            for q in range(NQ):
                n = rows[q]
                for c in range(2):
                    bankc = (0 if q < QT else 2) + c
                    last = pe.transpose(psum[:, bankc, (q % 4) * P:(q % 4) * P + n], nat[0:n, q, c * P:c * P + P], ident[0:n, 0:n])
            last.then_inc(s.turned, 1)

        @block.gpsimd
        def _(pool):
            pool.memset(state[:, :, :], 0.0).then_inc(s.zero, 1)

        @block.scalar
        def _(act):
            for q in range(QT):
                act.wait_ge(s.out, q + 1)
                act.copy(o(q), bank4(1, P)).then_inc(s.o_copied, 1)
            act.wait_ge(s.o_copied, QT)
            for q in range(QT):
                act.activation(squares(q), nat[:, q, 0:256], ACT.Square).then_inc(s.squared, 1)
            act.wait_ge(s.s_o, 1)
            act.activation(squares(QT), nat[0:NS, QT, 0:256], ACT.Square).then_inc(s.squared, 1)
            act.wait_ge(s.rsum, 2)
            act.activation(rr[:, :, :], rr[:, :, :], ACT.Ln, bias=C["eps"][:, 0:1], scale=1 / HD).then_inc(s.astep, 1)
            act.wait_ge(s.astep, 1)
            act.activation(rr[:, :, :], rr[:, :, :], ACT.Exp, scale=-0.5).then_inc(s.rr, 1)

        @block.vector
        def _(dve):
            for q in range(QT):
                dve.wait_ge(s.ws, q + 1)
                dve.tensor_tensor(vnew[:, :, :], uv(q), bank4(0, P), ALU.subtract).then_inc(s.vnew, 1)
                dve.wait_ge(s.zero if q == 0 else s.state, max(q, 1))
                dve.tensor_tensor(fade[:, :, :], state[:, :, :], bc(glast[:, :, q], HD), ALU.mult).then_inc(s.fade, 1)
                dve.wait_ge(s.fade, q + 1)
                dve.wait_ge(s.out, q + 1)
                dve.tensor_tensor(state[:, :, :], fade[:, :, :], bank4(2, HD), ALU.add).then_inc(s.state, 1)
            for i in range(2):
                for h in range(HEADS):
                    n = 4 * i + h
                    dve.wait_ge(s.s_w, n + 1)
                    if n:
                        dve.wait_ge(s.s_ws, n)
                    dve.tensor_tensor(own[:, :, :], psum[0:NS, 3 + n % 2, :].rearrange("p (b v) -> p b v", b=NB), bc(C["s_batch"], HD),
                                      ALU.mult).then_inc(s.s_own, 1)
                    dve.wait_ge(s.s_own, n + 1)
                    dve.tensor_reduce(ws[:, i, h, :], own[:, :, :].rearrange("p b v -> p v b"), AX.X, ALU.add).then_inc(s.s_ws, 1)
                if i == 0:
                    dve.wait_ge(s.s_ws, 4)
                    dve.tensor_tensor(vnew[0:NS, :, :], uv(QT), ws[:, 0, :, :], ALU.subtract).then_inc(s.s_vnew, 1)
            dve.wait_ge(s.s_vnew, 1)
            for h in range(HEADS):
                v = vnew[0:NS, h, :].unsqueeze(1).broadcast_to([NS, NB, HD])
                dve.tensor_tensor(vb[:, h, :, :], v, bc(C["s_batch"], HD), ALU.mult).then_inc(s.s_vb, 1)
            dve.wait_ge(s.s_out, 1)
            dve.wait_ge(s.s_ws, 8)
            dve.tensor_tensor(o(QT), bank4(5, NS), ws[:, 1, :, :], ALU.add).then_inc(s.s_o, 1)
            for h in range(HEADS):
                if h:
                    dve.wait_ge(s.s_state, h)
                dve.wait_ge(s.s_w, 8)
                dve.tensor_tensor(fade_s[:, :, :], st_s[:, h, :, :], bc(glast[:, h, QT:], HD), ALU.mult).then_inc(s.s_fade, 1)
                dve.wait_ge(s.s_fade, h + 1)
                dve.wait_ge(s.s_kv, h + 1)
                dve.tensor_tensor(st_s[:, h, :, :], fade_s[:, :, :], psum[0:HD, 6 + h % 2, :].rearrange("p (b v) -> p b v", b=NB),
                                  ALU.add).then_inc(s.s_state, 1)
            dve.memset(rr[:, QT, :], 1.0).then_inc(s.rsum, 1)
            dve.wait_ge(s.rsum, 1)
            for q in range(NQ):
                dve.wait_ge(s.squared, q + 1)
                last = dve.tensor_reduce(rr[0:rows[q], q, :], squares(q).rearrange("p (h d) -> p h d", h=HEADS), AX.X, ALU.add)
            last.then_inc(s.rsum, 1)
            dve.wait_ge(s.rr, 1)
            for q in range(NQ):
                dve.tensor_tensor(o(q), o(q), bc(rr[0:rows[q], q, :], HD), ALU.mult).then_inc(s.normed, 1)
            dve.wait_ge(s.turned, 1)
            for c in range(2):
                for b, t in ((c, slice(0, SEQ)), (2 + c, slice(SEQ, TOK))):
                    n = t.stop - t.start
                    dve.scalar_tensor_tensor(S.yT[:, 6 + c, t], psum[:, b, 0:n], taps[:, 0, 4:5], H(T_Z + c)[:, t],
                                             ALU.mult, ALU.mult).then_inc(s.yt, 1)

        @block.sync
        def _(sp):
            sp.wait_ge(s.state, QT)
            sp.dma_start(layer(io.prompt_gdn, l)[0].rearrange("h k v -> k h v"), state[:, :, :]).then_inc(s.stored, 16)
            sp.wait_ge(s.s_state, HEADS)
            for h in range(HEADS):
                sp.dma_start(layer(io.sample_gdn, l)[:, h].rearrange("b k v -> k b v"), st_s[:, h, :, :]).then_inc(s.stored, 16)
            sp.wait_ge(s.stored, 80)


def layer_norm(S, l, ctx, gain, bias, name):
    nc, sb, psum, C, xT = S.nc, S.sb, S.psum, S.C, S.xT
    row = sb(name + "_row", [2, D], ctx=ctx)
    col = sb(name + "_col", [P, KT, 2], ctx=ctx)
    sq = sb(name + "_sq", [P, KT, TOK], ctx=ctx)
    rstd = sb(name + "_rstd", [P, TOK], ctx=ctx)
    with stage(nc, "ln", "loaded", "turned", "copied", "mean", "centred", "squared", "var", "ln", "rstd", "normed", "done") as (block, s):
        @block.sync
        def _(sp):
            sp.dma_start(row[0:1, :], gain[ds(l, 1)]).then_inc(s.loaded, 16)
            sp.dma_start(row[1:2, :], bias[ds(l, 1)]).then_inc(s.loaded, 16)

        @block.tensor
        def _(pe):
            for h in range(2):
                for k in range(KT):
                    last = pe.matmul(psum[:, h, 0:HALF], C["mean_d"], xT[:, k, h * HALF:(h + 1) * HALF], start=(k == 0), stop=(k == KT - 1))
            last.then_inc(s.mean, 1)
            pe.wait_ge(s.loaded, 32)
            for k in range(KT):
                last = pe.transpose(psum[:, 4, 2 * k:2 * k + 2], row[:, k * P:k * P + P], C["ident"][0:2, 0:2])
            last.then_inc(s.turned, 1)
            for k in range(KT):
                pe.wait_ge(s.squared, k + 1)
                for h in range(2):
                    last = pe.matmul(psum[:, 2 + h, 0:HALF], C["mean_d"], sq[:, k, h * HALF:(h + 1) * HALF], start=(k == 0), stop=(k == KT - 1))
            last.then_inc(s.var, 1)

        @block.vector
        def _(dve):
            dve.wait_ge(s.mean, 1)
            for k in range(KT):
                dve.tensor_tensor(halves(xT[:, k, :]), halves(xT[:, k, :]), psum[:, 0:2, 0:HALF], ALU.subtract).then_inc(s.centred, 1)
            dve.wait_ge(s.centred, KT)
            dve.wait_ge(s.rstd, 1)
            for k in range(KT):
                dve.tensor_tensor(xT[:, k, :], xT[:, k, :], rstd[:, :], ALU.mult).then_inc(s.normed, 1)

        @block.scalar
        def _(act):
            for k in range(KT):
                act.wait_ge(s.centred, k + 1)
                act.activation(sq[:, k, :], xT[:, k, :], ACT.Square).then_inc(s.squared, 1)
            act.wait_ge(s.turned, 1)
            act.copy(col[:, :, :], psum[:, 4, 0:2 * KT].rearrange("p (k n) -> p k n", n=2)).then_inc(s.copied, 1)
            act.wait_ge(s.var, 1)
            act.activation(halves(rstd[:, :]), psum[:, 2:4, 0:HALF], ACT.Ln, bias=C["eps"][:, 0:1]).then_inc(s.ln, 1)
            act.wait_ge(s.ln, 1)
            act.activation(rstd[:, :], rstd[:, :], ACT.Exp, scale=-0.5).then_inc(s.rstd, 1)
            act.wait_ge(s.copied, 1)
            for k in range(KT):
                act.wait_ge(s.normed, k + 1)
                act.activation(xT[:, k, :], xT[:, k, :], ACT.Identity, bias=col[:, k, 1:2], scale=col[:, k, 0:1]).then_inc(s.done, 1)


def add_residual(S):
    def evac(dve, t, src, s):
        return dve.scalar_tensor_tensor(halves(S.xT[:, t, :]), halves(S.xT[:, t, :]), ALPHA, src, ALU.mult, ALU.add)
    return evac


def project_out(S, l, ctx):
    ring = S.sb("wo_ring", [P, 3, KT, 256], ctx=ctx)
    w_out = layer(S.io.w_out, l).rearrange("(k p) n -> p k n", p=P)

    def load(sp, g, slot, sem):
        sp.dma_start(ring[:, slot, :, :], w_out[:, :, g * 256:g * 256 + 256]).then_inc(sem, 16)

    dense(S, "out", (3, 2, load, lambda g: 1), KT, lambda k: S.yT[:, k, :],
          lambda t, k: ring[:, (t // 2) % 3, k, (t % 2) * P:(t % 2) * P + P], KT, None, add_residual(S))
    layer_norm(S, l, ctx, S.io.ln1_g, S.io.ln1_b, "ln1")


def feed_forward(S, l, ctx):
    sb, io, xT = S.sb, S.io, S.xT
    FT = DFF // P
    w_up = layer(io.w_up, l).rearrange("(k p) n -> p k n", p=P)
    w_down = layer(io.w_down, l).rearrange("(k p) n -> p k n", p=P)
    with ExitStack() as c:
        f = sb("ff", [P, FT, TOK], ctx=c)
        with ExitStack() as c2:
            ring = sb("up_ring", [P, 3, KT, 256], ctx=c2)
            pos = sb("pos", [P, TOK], ctx=c2)

            def load_up(sp, g, slot, sem):
                sp.dma_start(ring[:, slot, :, :], w_up[:, :, g * 256:g * 256 + 256]).then_inc(sem, 16)

            def squared_dve(dve, t, src, s):
                dve.tensor_scalar(halves(f[:, t, :]), src, 0.0, None, ALU.max).then_inc(s.rect_dve, 1)
                dve.wait_ge(s.rect_dve, t // 2 + 1)
                return dve.tensor_tensor(f[:, t, :], f[:, t, :], f[:, t, :], ALU.mult)

            def squared_act(act, t, src, s):
                if t > 1:
                    act.wait_ge(s.taken_act, t // 2)
                act.activation(halves(pos[:, :]), src, ACT.Relu).then_inc(s.rect_act, 1)
                act.wait_ge(s.rect_act, t // 2 + 1)
                return act.activation(f[:, t, :], pos[:, :], ACT.Square)

            dense(S, "up", (3, 2, load_up, lambda g: 1), KT, lambda k: xT[:, k, :],
                  lambda t, k: ring[:, (t // 2) % 3, k, (t % 2) * P:(t % 2) * P + P], FT, squared_act, squared_dve)
        down = sb("down_ring", [P, 3, FT, P], ctx=c)

        def load_down(sp, g, slot, sem):
            sp.dma_start(down[:, slot, :, :], w_down[:, :, g * P:g * P + P]).then_inc(sem, 16)

        dense(S, "down", (3, 1, load_down, lambda g: 1), FT, lambda k: f[:, k, :],
              lambda t, k: down[:, t % 3, k, :], KT, None, add_residual(S))
    layer_norm(S, l, ctx, io.ln2_g, io.ln2_b, "ln2")


def store_outputs(S):
    nc, io = S.nc, S.io
    with ExitStack() as c:
        y = S.sb("y_out", [P, QT + 1, D], ctx=c)
        with stage(nc, "y", "turned", "copied", "stored") as (block, s):
            @block.tensor
            def _(pe):
                for q in range(QT + 1):
                    n = P if q < QT else NS
                    if q >= 4:
                        pe.wait_ge(s.copied, q - 3)
                    for k in range(KT):
                        last = pe.transpose(S.psum[0:n, 2 * (q % 4) + k // 4, (k % 4) * P:(k % 4) * P + P],
                                            S.xT[:, k, q * P:q * P + n], S.C["ident"])
                    last.then_inc(s.turned, 1)

            @block.vector
            def _(dve):
                for q in range(QT + 1):
                    n = P if q < QT else NS
                    dve.wait_ge(s.turned, q + 1)
                    dve.tensor_copy(y[0:n, q, :].rearrange("p (b n) -> p b n", b=2),
                                    S.psum[0:n, 2 * (q % 4):2 * (q % 4) + 2, :]).then_inc(s.copied, 1)

            @block.sync
            def _(sp):
                for q in range(QT + 1):
                    sp.wait_ge(s.copied, q + 1)
                    dst = io.y_prompt[0, q * P:q * P + P, :] if q < QT else io.y_sample.rearrange("b t n -> (b t) n")
                    sp.dma_start(dst, y[0:P if q < QT else NS, q, :]).then_inc(s.stored, 16)
                sp.wait_ge(s.stored, 16 * (QT + 1))


OUTS = [("y_prompt", (1, SEQ, D)), ("y_sample", (NB, NT, D)),
        ("prompt_nsa", (DEPTH, SEQ // PAGE, PAGE, 4, KVH, HD)), ("prompt_win", (DEPTH, 1, SEQ, 2, KVH, HD)),
        ("prompt_conv", (DEPTH, 1, CW - 1, 256)), ("prompt_pool", (DEPTH, 1, PBUF, 256)),
        ("prompt_gconv", (DEPTH, 1, GC - 1, 768)), ("prompt_gdn", (DEPTH, 1, HEADS, HD, HD)),
        ("sample_nsa", (DEPTH, NB, NT, 4, KVH, HD)), ("sample_win", (DEPTH, NB, 512, 2, KVH, HD)),
        ("sample_conv", (DEPTH, NB, CW - 1, 256)), ("sample_pool", (DEPTH, NB, PBUF, 256)),
        ("sample_gconv", (DEPTH, NB, GC - 1, 768)), ("sample_gdn", (DEPTH, NB, HEADS, HD, HD))]


def kernel(**inputs):
    import concourse.bacc as bacc
    from concourse.bass_utils import run_bass_kernel_spmd

    nc = bacc.Bacc("TRN2", target_bir_lowering=False, num_devices=1)
    arrays, args = {}, {}
    io = Named(args)
    args["n_pool"] = inputs["cache_nsa_kv"].shape[1]
    table, where = pack_tables()
    for name, a in list(inputs.items()) + [("cst", table)]:
        a = np.ascontiguousarray(a)
        arrays[f"in_{name}"] = a
        args[name] = nc.dram_tensor(f"in_{name}", a.shape, mybir.dt.from_np(a.dtype), kind="ExternalInput").ap()
    for name, shape in OUTS:
        args[name] = nc.dram_tensor(f"out_{name}", shape, F32, kind="ExternalOutput").ap()
    args["line_dram"] = nc.dram_tensor("line_dram", (HEADS, P, LINE), F32, kind="Internal").ap()
    build(nc, io, where)
    r = run_bass_kernel_spmd(nc, [arrays], core_ids=[0])
    return tuple(r.results[0][f"out_{name}"] for name, _ in OUTS)
```

```python
from contextlib import ExitStack, contextmanager

import numpy as np

import concourse.bass as bass
from concourse import mybir

F32 = mybir.dt.float32
I32 = mybir.dt.int32
ALU = mybir.AluOpType
ACT = mybir.ActivationFunctionType
AX = mybir.AxisListType
ds = bass.ds

P = 128
DEPTH, D, SEQ, NB, NT = 2, 1024, 512, 8, 4
PAST, PAGE = 4096, 128
NS = NB * NT
TOK = SEQ + NS
HALF = TOK // 2
KT = D // P
QT = SEQ // P
HD, HEADS, KVH, GRP = 64, 4, 2, 2
DFF = 4 * D
CW, PBUF, GC = 31, 15, 4
IN_W = 2836
NCH = PAST // 16
NCB = NCH - 1
NPG = PAST // PAGE
NBLK = PAST // 64
ALPHA = (2 * DEPTH) ** 0.25
NEG = -1e30
STRIP = 896
LINE = 1024
T_CONV, T_GLU, T_POOL, T_Q, T_KV, T_GDN, T_Z, T_MISC = 0, 2, 4, 6, 8, 14, 20, 22
N_IN = 23
M_GATE, M_A, M_B, M_W = 0, 32, 64, 96


def bucket(d):
    d = np.maximum(np.asarray(d), 0)
    log = np.log(np.maximum(d, 1).astype(np.float32) / np.float32(16)) / np.float32(np.log(128 / 16))
    large = np.minimum(16 + (log * np.float32(16)).astype(np.int32), 31)
    return np.where(d < 16, d, large)


def one_hot(d, base=None):
    d = np.asarray(d)
    e = np.zeros((33, d.size), np.float32)
    for j, x in enumerate(d.ravel()):
        if x < 0:
            e[32, j] = 1
        else:
            e[int(bucket(x)), j] += 1
            if base is not None:
                e[base, j] -= 1
    return e


def constant_tables():
    i = np.arange(P)
    s = np.arange(NS)
    row = np.arange(P)
    rb, rh, rt = row // 16, row // 4 % 4, row % 4
    t = {}
    t["ident"] = np.eye(P)
    t["mean_d"] = np.full((P, P), 1 / D)
    t["mean_c"] = np.full((P, P), 1 / 256)
    t["ones"] = np.ones((P, P))
    t["upto"] = i[:, None] <= i[None, :]
    t["after"] = np.where(i[None, :] >= i[:, None], 0, NEG)
    for l in range(7):
        w = 2 << l
        same = i[:, None] // w == i[None, :] // w
        t[f"level{l}"] = same & (i[:, None] % w < w // 2) & (i[None, :] % w >= w // 2)
    sb = s // NT
    same = sb[:, None] == sb[None, :]
    t["s_ones"] = same
    t["s_upto"] = same & (s[:, None] <= s[None, :])
    t["s_after"] = np.where(same & (s[None, :] >= s[:, None]), 0, NEG)
    t["s_batch"] = sb[:, None] == np.arange(NB)[None, :]
    t["s_row"] = (sb[:, None] == rb[None, :]) & (s[:, None] % NT == rt[None, :])
    inv = np.zeros((P, 2, 16))
    wcol = np.zeros((P, 2))
    for c in range(2):
        for q in range(2):
            w = (2, 4, 8, 16)[2 * c + q]
            inv[64 * q:64 * q + 64, c] = 1 / np.minimum(np.arange(16) + 1, w)
            wcol[64 * q:64 * q + 64, c] = 1 / w
    t["pool_first"] = inv.reshape(P, 32)
    t["pool_inv"] = wcol
    t["eps"] = np.tile(np.array([1e-5, 1e-6]), (P, 1))
    t["line"] = one_hot(511 - np.arange(LINE))
    e = np.zeros((33, NT, 416), np.float32)
    for q in range(NT):
        e[:, q, 0:128] = one_hot(128 + q - np.arange(128), 31)
        e[:, q, 128:160] = one_hot(q - np.arange(NS) % NT)
        e[:, q, 160:415] = one_hot(PAST + q - 16 * np.arange(NCB) - 31)
        e[31, q, 415] = 1
    t["s_line"] = e.reshape(33, -1)
    t["other_b"] = np.where(rb[:, None] == sb[None, :], 0, NEG)
    t["win_old"] = np.where(np.arange(NT)[None, :] > rt[:, None], 0, NEG)
    t["pair"] = (rb[:, None] == rb[None, :]) & (rt[:, None] == rt[None, :]) & (rh[:, None] // 2 == rh[None, :] // 2)
    t["row_head"] = rh[:, None] == np.arange(HEADS)[None, :]
    force = np.zeros(NBLK + 1)
    force[[0, NBLK - 1, NBLK]] = 1e4
    t["force"] = np.tile(force, (P, 1))
    return {k: np.asarray(v, np.float32) for k, v in t.items()}


def pack_tables():
    t = constant_tables()
    for k in ("line", "s_line"):
        t[k] = t.pop(k)
    where, n = {}, 0
    for k, v in t.items():
        where[k] = (n, v.shape[0], v.shape[1])
        n += v.shape[1]
    out = np.zeros((P, n), np.float32)
    for k, v in t.items():
        out[:v.shape[0], where[k][0]:where[k][0] + v.shape[1]] = v
    return out, where


class Named:

    def __init__(self, table):
        self.table = table

    def __getattr__(self, name):
        return self.table[name]


POOL = []


@contextmanager
def stage(nc, label, *names):
    while len(POOL) < len(names):
        POOL.append(nc.alloc_semaphore(f"stage_sem{len(POOL)}"))
    used = POOL[:len(names)]
    nums = [x.num for x in used]
    assert nums == list(range(nums[0], nums[0] + len(nums)))
    with nc.Block() as block:
        yield block, Named(dict(zip(names, used)))
    nc.all_engine_barrier(sems_to_clear=range(nums[0], nums[-1] + 1))


class Serial:

    def __init__(self, eng, own):
        self.eng, self.own, self.count = eng, own, {}

    def __call__(self, ins, signal=None):
        sem = self.own if signal is None else signal
        self.count[sem.num] = self.count.get(sem.num, 0) + 1
        ins.then_inc(sem, 1)
        self.eng.wait_ge(sem, self.count[sem.num])


def bc(ap, n):
    ap = ap.unsqueeze(len(ap.shape))
    return ap.broadcast_to(list(ap.shape[:-1]) + [n])


def bc_mid(ap, n):
    ap = ap.unsqueeze(1)
    return ap.broadcast_to([ap.shape[0], n] + list(ap.shape[2:]))


def halves(ap):
    return ap.rearrange("p (h n) -> p h n", h=2)


def build(nc, io, where):
    POOL.clear()
    with ExitStack() as top:
        def sb(name, shape, dt=F32, ctx=top):
            return ctx.enter_context(nc.sbuf_tensor(name, shape, dt))

        S = Named(dict(nc=nc, io=io, where=where, sb=sb))
        S.xT = sb("xT", [P, KT, TOK])
        S.yT = sb("yT", [P, KT, TOK])
        S.cst = sb("cst", [P, where["line"][0]])
        S.C = {k: S.cst[0:r, o:o + n] for k, (o, r, n) in where.items() if k not in ("line", "s_line")}
        S.sbias = sb("sbias", [P, 416])
        S.pages = sb("pages", [1, NB * NPG], I32)
        S.psum = top.enter_context(nc.psum_tensor("psum", [P, 8, 512], F32))
        load_inputs(S)
        with ExitStack() as c:
            bias_tables(S, c)
        with nc.Fori(0, DEPTH) as l:
            with ExitStack() as mix:
                S.HT = sb("HT", [P, N_IN - 6, TOK], ctx=mix)
                S.misc_n = sb("misc_n", [P, QT + 1, M_W], ctx=mix)
                S.gates = sb("gates", [P, QT + 1, 12], ctx=mix)
                with ExitStack() as c:
                    S.HC = sb("HC", [P, 6, TOK], ctx=c)
                    project_in(S, l, c)
                    conv_and_pool(S, l, c)
                with ExitStack() as att:
                    compression_weights(S, l, att)
                    with ExitStack() as c:
                        prompt_attention(S, l, c)
                    with ExitStack() as c:
                        sample_scores(S, l, c)
                        sample_attention(S, l, c)
                with ExitStack() as c:
                    gated_delta(S, l, c)
            with ExitStack() as c:
                project_out(S, l, c)
            with ExitStack() as c:
                feed_forward(S, l, c)
        store_outputs(S)


def load_inputs(S):
    nc, io = S.nc, S.io
    with ExitStack() as c:
        xn = S.sb("xn", [P, QT + 1, D], ctx=c)
        with stage(nc, "in", "loaded", "turned", "copied") as (block, s):
            @block.sync
            def _(sp):
                sp.dma_start(S.cst[:, :], io.cst[:, 0:S.where["line"][0]]).then_inc(s.loaded, 16)
                sp.dma_start(S.pages[:, :], io.page_table.rearrange("(a b) j -> a (b j)", a=1)).then_inc(s.loaded, 16)
                sp.dma_start(xn[:, 0:QT, :], io.x_prompt.rearrange("a (q p) n -> p (a q) n", p=P)).then_inc(s.loaded, 16)
                sp.dma_start(xn[0:NS, QT, :], io.x_sample.rearrange("b t n -> (b t) n")).then_inc(s.loaded, 16)

            @block.tensor
            def _(pe):
                pe.wait_ge(s.loaded, 64)
                for q in range(QT + 1):
                    n = P if q < QT else NS
                    if q >= 2:
                        pe.wait_ge(s.copied, q - 1)
                    for k in range(KT):
                        last = pe.transpose(S.psum[:, 2 * (q % 2) + k // 4, (k % 4) * P:(k % 4) * P + n],
                                            xn[0:n, q, k * P:(k + 1) * P], S.C["ident"][0:n, 0:n])
                    last.then_inc(s.turned, 1)

            @block.vector
            def _(dve):
                for q in range(QT + 1):
                    n = P if q < QT else NS
                    dve.wait_ge(s.turned, q + 1)
                    src = S.psum[:, 2 * (q % 2):2 * (q % 2) + 2, :].rearrange("p b (k n) -> p (b k) n", n=P)
                    dve.tensor_copy(S.xT[:, :, q * P:q * P + n], src[:, :, 0:n]).then_inc(s.copied, 1)


def bias_tables(S, ctx):
    nc, io, sb = S.nc, S.io, S.sb
    line = sb("line", [33, LINE], ctx=ctx)
    sline = sb("sline", [33, NT, 416], ctx=ctx)
    rel = sb("rel", [33, HEADS], ctx=ctx)
    relp = sb("relp", [33, HEADS, P], ctx=ctx)
    rels = sb("rels", [33, NT, P], ctx=ctx)
    rows = sb("rows", [P, HEADS, LINE], ctx=ctx)
    w = S.where
    with stage(nc, "bias", "loaded", "mask", "spread", "product", "copied", "stored") as (block, s):
        @block.sync
        def _(sp):
            sp.dma_start(line[:, :], io.cst[0:33, w["line"][0]:w["line"][0] + LINE]).then_inc(s.loaded, 16)
            sp.dma_start(sline[:, :, :], io.cst[0:33, w["s_line"][0]:w["s_line"][0] + NT * 416]
                         .rearrange("p (t n) -> p t n", t=NT)).then_inc(s.loaded, 16)
            sp.dma_start(rel[0:32, :], io.rel_bias).then_inc(s.loaded, 16)
            sp.wait_ge(s.copied, 2 * HEADS)
            sp.dma_start(io.line_dram.rearrange("h p n -> p h n"), rows[:, :, :]).then_inc(s.stored, 16)
            sp.wait_ge(s.stored, 16)

        @block.vector
        def _(dve):
            step = Serial(dve, s.spread)
            dve.memset(rel[32:33, :], NEG).then_inc(s.mask, 1)
            step(dve.memset(rels[:, :, :], 0.0))
            dve.wait_ge(s.mask, 1)
            dve.wait_ge(s.loaded, 48)
            step(dve.tensor_copy(relp[:, :, :], bc(rel[:, :], P)))
            for t in range(NT):
                dst = rels[:, t, :].rearrange("k (b h q) -> k b h q", b=NB, h=HEADS)[:, :, :, t]
                step(dve.tensor_copy(dst, bc_mid(rel[:, :], NB)))
            for h in range(HEADS):
                for j in range(2):
                    n = 2 * h + j
                    dve.wait_ge(s.product, n + 1)
                    dve.tensor_copy(rows[:, h, j * 512:(j + 1) * 512], S.psum[:, n % 4, :]).then_inc(s.copied, 1)
            dve.wait_ge(s.product, 2 * HEADS + 1)
            dve.tensor_copy(S.sbias[:, :], S.psum[:, 4, 0:416]).then_inc(s.copied, 1)
            dve.wait_ge(s.copied, 2 * HEADS + 1)
            dve.tensor_tensor(S.sbias[:, 128:160], S.sbias[:, 128:160], S.C["other_b"], ALU.add).then_inc(s.copied, 1)

        @block.tensor
        def _(pe):
            pe.wait_ge(s.spread, 2 + NT)
            for h in range(HEADS):
                for j in range(2):
                    n = 2 * h + j
                    if n >= 4:
                        pe.wait_ge(s.copied, n - 3)
                    pe.matmul(S.psum[:, n % 4, :], relp[:, h, :], line[:, j * 512:(j + 1) * 512],
                              start=True, stop=True).then_inc(s.product, 1)
            for t in range(NT):
                last = pe.matmul(S.psum[:, 4, 0:416], rels[:, t, :], sline[:, t, :], start=(t == 0), stop=(t == NT - 1))
            last.then_inc(s.product, 1)


def dense(S, label, weights, kt, moving, lhsT, n_tiles, evac_act, evac_dve, beside=None):
    nc, psum = S.nc, S.psum
    slots, per, load, n_dmas = weights
    n_groups = -(-n_tiles // per)
    names = [f"loaded{i}" for i in range(slots)]
    with stage(nc, label, "product", "taken_dve", "taken_act", "rect_dve", "rect_act", "beside", *names) as (block, s):
        loaded = [s.table[n] for n in names]

        @block.sync
        def _(sp):
            for g in range(n_groups):
                if g >= slots:
                    sp.wait_ge(s.product, per * (g - slots + 1))
                load(sp, g, g % slots, loaded[g % slots])

        @block.tensor
        def _(pe):
            arrived = [0] * slots
            for t in range(n_tiles):
                g = t // per
                if t % per == 0:
                    arrived[g % slots] += 16 * n_dmas(g)
                    pe.wait_ge(loaded[g % slots], arrived[g % slots])
                if t >= 4:
                    if evac_act is None:
                        pe.wait_ge(s.taken_dve, t - 3)
                    else:
                        pe.wait_ge(s.taken_act if t % 2 else s.taken_dve, (t - 4) // 2 + 1)
                for k in range(kt):
                    w = lhsT(t, k)
                    for h in range(2):
                        last = pe.matmul(psum[0:w.shape[1], 2 * (t % 4) + h, 0:HALF], w,
                                         moving(k)[:, h * HALF:(h + 1) * HALF], start=(k == 0), stop=(k == kt - 1))
                last.then_inc(s.product, 1)

        def tile_of(t):
            return psum[:, 2 * (t % 4):2 * (t % 4) + 2, 0:HALF]

        @block.vector
        def _(dve):
            for t in range(0, n_tiles, 1 if evac_act is None else 2):
                dve.wait_ge(s.product, t + 1)
                evac_dve(dve, t, tile_of(t), s).then_inc(s.taken_dve, 1)

        @block.scalar
        def _(act):
            n_beside = beside(act, s.beside) if beside else 0
            for t in range(1, n_tiles, 2) if evac_act else ():
                act.wait_ge(s.product, t + 1)
                evac_act(act, t, tile_of(t), s).then_inc(s.taken_act, 1)
            if n_beside:
                act.wait_ge(s.beside, 16 * n_beside)


def layer(ap, l):
    dims = " ".join(f"d{i}" for i in range(len(ap.shape) - 2))
    return ap[ds(l, 1)].rearrange(f"a b {dims} -> (a b) {dims}")


def project_in(S, l, ctx):
    nc, io, sb = S.nc, S.io, S.sb
    ring = sb("w_ring", [P, 3, KT, 256], ctx=ctx)
    misc = sb("w_misc", [P, KT, M_W], ctx=ctx)
    w_in = layer(io.w_in, l).rearrange("(k p) n -> p k n", p=P)
    start = [0, 256, 512, 768, 1024, 1280, 1536, 1804, 2060, 2316, 2572]

    with stage(nc, "misc", "zero", "loaded") as (block, s):
        @block.gpsimd
        def _(pool):
            pool.memset(misc[:, :, :], 0.0).then_inc(s.zero, 1)

        @block.scalar
        def _(act):
            act.wait_ge(s.zero, 1)
            act.dma_start(misc[:, :, M_GATE:M_GATE + 12], w_in[:, :, 1792:1804]).then_inc(s.loaded, 16)
            act.dma_start(misc[:, :, M_A:M_A + 4], w_in[:, :, 2828:2832]).then_inc(s.loaded, 16)
            act.dma_start(misc[:, :, M_B:M_B + 4], w_in[:, :, 2832:2836]).then_inc(s.loaded, 16)
            act.wait_ge(s.loaded, 48)

    def load(sp, g, slot, sem):
        if g == 3:
            for grp in range(GRP):
                for kh in range(KVH):
                    c = 768 + (kh * GRP + grp) * HD
                    sp.dma_start(ring[:, slot, :, (grp * KVH + kh) * HD:(grp * KVH + kh + 1) * HD],
                                 w_in[:, :, c:c + HD]).then_inc(sem, 16)
        elif g < 11:
            sp.dma_start(ring[:, slot, :, :], w_in[:, :, start[g]:start[g] + 256]).then_inc(sem, 16)

    def lhsT(t, k):
        if t == T_MISC:
            return misc[:, k, :]
        return ring[:, (t // 2) % 3, k, (t % 2) * P:(t % 2) * P + P]

    def dest(t):
        return S.HC[:, t, :] if t < 6 else S.HT[:, t - 6, :]

    def evac_act(act, t, src, s):
        if t == T_Q + 1:
            return act.mul(halves(dest(t)), src, HD ** -0.5)
        return act.copy(halves(dest(t)), src)

    def evac_dve(dve, t, src, s):
        if t == T_Q:
            return dve.tensor_scalar(halves(dest(t)), src, HD ** -0.5, None, ALU.mult)
        if t == T_MISC:
            return dve.tensor_copy(halves(dest(t)[0:M_W]), src[0:M_W])
        return dve.tensor_copy(halves(dest(t)), src)

    def keep_window(act, sem):
        for b in range(NB):
            act.dma_start(layer(io.sample_win, l)[b, 0:512 - NT].rearrange("w c k d -> w (c k d)"),
                          layer(io.cache_win_kv, l)[b, NT:].rearrange("w c k d -> w (c k d)")).then_inc(sem, 16)
        return NB

    dense(S, "proj", (3, 2, load, lambda g: 4 if g == 3 else (0 if g == 11 else 1)), KT, lambda k: S.xT[:, k, :],
          lhsT, N_IN, evac_act, evac_dve, beside=keep_window)


def page_numbers(S, engine, b, first, n):
    where = S.pages[0:1, ds(b * NPG + first, n)]
    _, values = S.nc.values_load_multi_w_load_instructions(where, engines=[engine], min_val=0, max_val=S.io.n_pool - 1,
                                                           skip_runtime_bounds_check_because="each DMA checks its own bounds")
    return values


def conv_and_pool(S, l, ctx):
    nc, io, sb, psum, C, HC = S.nc, S.io, S.sb, S.psum, S.C, S.HC
    vrow = sb("vrow", [35, 256], ctx=ctx)
    cols = sb("cols", [P, 2, 35], ctx=ctx)
    conv_st = sb("conv_st", [120, 2, 256], ctx=ctx)
    pool_st = sb("pool_st", [120, 256], ctx=ctx)
    u = sb("u", [P, 2, CW - 1 + SEQ], ctx=ctx)
    us = sb("us", [P, 2, NB, CW - 1 + NT], ctx=ctx)
    v = sb("v", [P, 2, PBUF + SEQ], ctx=ctx)
    vs = sb("vs", [P, 2, NB, PBUF + NT], ctx=ctx)
    poolw = sb("poolw", [P, 2, P], ctx=ctx)
    pw = sb("pw", [P, 2, 256], ctx=ctx)
    with stage(nc, "glu", "loaded", "linear", "zero", "turned", "sigmoid", "placed", "copied", "moved") as (block, s):
        @block.sync
        def _(sp):
            sp.dma_start(vrow[0:CW, :], layer(io.conv_dw, l)).then_inc(s.loaded, 16)
            for i, a in enumerate((io.conv_dw_b, io.conv_ln_g, io.conv_ln_b, io.pool_scale)):
                sp.dma_start(vrow[CW + i:CW + i + 1, :], a[ds(l, 1)]).then_inc(s.loaded, 16)
            sp.dma_start(conv_st[:, :, :], layer(io.state_conv, l).rearrange("(h b) w c -> (b w) h c", h=2)).then_inc(s.loaded, 16)
            sp.dma_start(pool_st[:, :], layer(io.state_pool, l).rearrange("b w c -> (b w) c")).then_inc(s.loaded, 16)
            sp.dma_start(pw[:, :, :], layer(io.conv_pw, l).rearrange("(k p) n -> p k n", p=P)).then_inc(s.loaded, 16)
            sp.wait_ge(s.zero, 3)
            for g in range(4):
                r = 64 * (g % 2)
                sp.dma_start(poolw[r:r + 64, g // 2, r:r + 64], layer(io.pool_w, l)[g]).then_inc(s.linear, 16)
            sp.wait_ge(s.linear, 16 * 4)

        @block.gpsimd
        def _(pool):
            pool.memset(u[:, :, 0:CW - 1], 0.0).then_inc(s.zero, 1)
            pool.memset(v[:, :, 0:PBUF], 0.0).then_inc(s.zero, 1)
            pool.memset(poolw[:, :, :], 0.0).then_inc(s.zero, 1)
            pool.tensor_copy(v[:, :, PBUF:], HC[:, 4:6, 0:SEQ]).then_inc(s.moved, 1)
            for c in range(2):
                pool.tensor_copy(vs[:, c, :, PBUF:], HC[:, 4 + c, SEQ:].rearrange("p (b t) -> p b t", b=NB)).then_inc(s.moved, 1)

        @block.tensor
        def _(pe):
            pe.wait_ge(s.loaded, 16 * 8)
            for c in range(2):
                f = slice(c * P, c * P + P)
                pe.transpose(psum[:, c, 0:35], vrow[:, f], C["ident"][0:35, 0:35]).then_inc(s.turned, 1)
                pe.transpose(psum[:, 2 + c, 0:120], pool_st[:, f], C["ident"][0:120, 0:120]).then_inc(s.turned, 1)
                for h in range(2):
                    pe.transpose(psum[:, 4 + 2 * c + h, 0:120], conv_st[:, h, f], C["ident"][0:120, 0:120]).then_inc(s.turned, 1)

        @block.scalar
        def _(act):
            act.activation(HC[:, 2:4, :], HC[:, 2:4, :], ACT.Sigmoid).then_inc(s.sigmoid, 1)
            for c in range(2):
                act.wait_ge(s.turned, 4 * c + 4)
                act.copy(cols[:, c, :], psum[:, c, 0:35]).then_inc(s.copied, 1)
                act.copy(vs[:, c, :, 0:PBUF], psum[:, 2 + c, 0:120].rearrange("p (b w) -> p b w", b=NB)).then_inc(s.copied, 1)
                for h in range(2):
                    act.copy(us[:, c, 4 * h:4 * h + 4, 0:CW - 1],
                             psum[:, 4 + 2 * c + h, 0:120].rearrange("p (b w) -> p b w", b=4)).then_inc(s.copied, 1)

        @block.vector
        def _(dve):
            dve.wait_ge(s.sigmoid, 1)
            dve.tensor_tensor(u[:, :, CW - 1:], HC[:, 0:2, 0:SEQ], HC[:, 2:4, 0:SEQ], ALU.mult).then_inc(s.placed, 1)
            for c in range(2):
                dve.tensor_tensor(us[:, c, :, CW - 1:], HC[:, c, SEQ:].rearrange("p (b t) -> p b t", b=NB),
                                  HC[:, 2 + c, SEQ:].rearrange("p (b t) -> p b t", b=NB), ALU.mult).then_inc(s.placed, 1)

    pack = sb("pack", [P, 2, 3 * 120], ctx=ctx)
    nat = sb("nat", [120, 5, 256], ctx=ctx)
    acc = sb("acc", [P, 2, TOK], ctx=ctx)
    sq = sb("sq", [P, 2, TOK], ctx=ctx)
    rstd = sb("rstd", [P, TOK], ctx=ctx)
    sums = [sb(f"sum{w}", [P, 2, PBUF + SEQ], ctx=ctx) for w in (2, 4, 8, 16)]
    sums_s = [sb(f"sums{w}", [P, 2, NB, PBUF + NT], ctx=ctx) for w in (2, 4, 8, 16)]
    pd = sb("pd", [P, 2, TOK], ctx=ctx)
    names = ("packed", "turned", "copied", "stored", "taps", "conv", "mean", "centred", "squared", "var", "ln", "rstd",
             "normed", "swish", "pooled", "psteps", "linear", "scaled", "pointwise", "out", "dsteps")
    with stage(nc, "conv", *names) as (block, s):
        @block.gpsimd
        def _(pool):
            for c in range(2):
                for h in range(2):
                    pool.tensor_copy(pack[:, c, h * 120:h * 120 + 120].rearrange("p (b w) -> p b w", b=4),
                                     us[:, c, 4 * h:4 * h + 4, NT:]).then_inc(s.packed, 1)
                pool.tensor_copy(pack[:, c, 240:360].rearrange("p (b w) -> p b w", b=NB), vs[:, c, :, NT:]).then_inc(s.packed, 1)
            step = Serial(pool, s.psteps)
            a, b = v, vs
            for i, w in enumerate((2, 4, 8, 16)):
                h = w // 2
                step(pool.tensor_tensor(sums[i][:, :, w - 1:], a[:, :, w - 1:], a[:, :, w - 1 - h:PBUF + SEQ - h], ALU.add))
                for c in range(2):
                    step(pool.tensor_tensor(sums_s[i][:, c, :, w - 1:], b[:, c, :, w - 1:], b[:, c, :, w - 1 - h:PBUF + NT - h], ALU.add))
                a, b = sums[i], sums_s[i]
            for i in range(4):
                c, r = i // 2, slice(64 * (i % 2), 64 * (i % 2) + 64)
                inv = C["pool_inv"][r, c:c + 1]
                pool.tensor_scalar(pd[r, c, 16:SEQ], sums[i][r, c, PBUF + 16:], inv, None, ALU.mult)
                pool.tensor_tensor(pd[r, c, 0:16], sums[i][r, c, PBUF:PBUF + 16], C["pool_first"][r, 16 * c:16 * c + 16], ALU.mult)
                step(pool.tensor_scalar(pd[r, c, SEQ:].rearrange("p (b t) -> p b t", b=NB), sums_s[i][r, c, :, PBUF:], inv, None, ALU.mult))
            pool.tensor_tensor(pd[:, :, :], pd[:, :, :], HC[:, 4:6, :], ALU.subtract).then_inc(s.pooled, 1)

        @block.vector
        def _(dve):
            def tap(n, w, c, out, src):
                if n >= 4:
                    dve.wait_ge(s.taps, n - 3)
                if w == 0:
                    dve.tensor_scalar(out, src, cols[:, c, 0:1], cols[:, c, 31:32], ALU.mult, ALU.add).then_inc(s.taps, 1)
                else:
                    dve.scalar_tensor_tensor(out, src, cols[:, c, w:w + 1], out, ALU.mult, ALU.add).then_inc(s.taps, 1)

            for w in range(CW):
                for c in range(2):
                    tap(4 * w + 2 * c, w, c, acc[:, c, 0:SEQ], u[:, c, w:w + SEQ])
                    tap(4 * w + 2 * c + 1, w, c, acc[:, c, SEQ:].rearrange("p (b t) -> p b t", b=NB), us[:, c, :, w:w + NT])
            dve.wait_ge(s.mean, 1)
            for c in range(2):
                dve.tensor_tensor(halves(acc[:, c, :]), halves(acc[:, c, :]), psum[:, 6:8, 0:HALF], ALU.subtract).then_inc(s.centred, 1)
            dve.wait_ge(s.rstd, 1)
            for c in range(2):
                dve.wait_ge(s.centred, 2)
                dve.tensor_tensor(acc[:, c, :], acc[:, c, :], rstd[:, :], ALU.mult).then_inc(s.normed, 1)
            for c in range(2):
                dve.wait_ge(s.pointwise, c + 1)
                dve.tensor_copy(halves(S.yT[:, c, :]), psum[:, 2 * c:2 * c + 2, 0:HALF]).then_inc(s.out, 1)

        @block.tensor
        def _(pe):
            pe.wait_ge(s.packed, 6)
            for c in range(2):
                srcs = (u[:, c, SEQ:], v[:, c, SEQ:], pack[:, c, 0:120], pack[:, c, 120:240], pack[:, c, 240:360])
                for j, src in enumerate(srcs):
                    pe.transpose(psum[0:src.shape[1], j, c * P:c * P + P], src, C["ident"]).then_inc(s.turned, 1)
            pe.wait_ge(s.taps, 4 * CW)
            for h in range(2):
                for c in range(2):
                    last = pe.matmul(psum[:, 6 + h, 0:HALF], C["mean_c"], acc[:, c, h * HALF:(h + 1) * HALF], start=(c == 0), stop=(c == 1))
            last.then_inc(s.mean, 1)
            pe.wait_ge(s.pooled, 1)
            pe.wait_ge(s.copied, 5)
            for c in range(2):
                for h in range(2):
                    last = pe.matmul(psum[:, 2 * c + h, 0:HALF], poolw[:, c, :], pd[:, c, h * HALF:(h + 1) * HALF], start=True, stop=True)
                last.then_inc(s.linear, 1)
            pe.wait_ge(s.squared, 1)
            for h in range(2):
                for c in range(2):
                    last = pe.matmul(psum[:, 6 + h, 0:HALF], C["mean_c"], sq[:, c, h * HALF:(h + 1) * HALF], start=(c == 0), stop=(c == 1))
            last.then_inc(s.var, 1)
            pe.wait_ge(s.swish, 2)
            pe.wait_ge(s.scaled, 2)
            for c in range(2):
                for k in range(2):
                    for h in range(2):
                        last = pe.matmul(psum[:, 2 * c + h, 0:HALF], pw[:, k, c * P:c * P + P], acc[:, k, h * HALF:(h + 1) * HALF],
                                         start=(k == 0), stop=(k == 1))
                last.then_inc(s.pointwise, 1)

        @block.scalar
        def _(act):
            act.wait_ge(s.turned, 10)
            for j, n in enumerate((CW - 1, PBUF, 120, 120, 120)):
                act.copy(nat[0:n, j, :], psum[0:n, j, 0:256]).then_inc(s.copied, 1)
            for c in range(2):
                act.wait_ge(s.linear, c + 1)
                act.mul(halves(S.yT[:, 2 + c, :]), psum[:, 2 * c:2 * c + 2, 0:HALF], cols[:, c, 34:35]).then_inc(s.scaled, 1)
            act.wait_ge(s.centred, 2)
            act.activation(sq[:, :, :], acc[:, :, :], ACT.Square).then_inc(s.squared, 1)
            act.wait_ge(s.var, 1)
            act.activation(halves(rstd[:, :]), psum[:, 6:8, 0:HALF], ACT.Ln, bias=C["eps"][:, 0:1]).then_inc(s.ln, 1)
            act.wait_ge(s.ln, 1)
            act.activation(rstd[:, :], rstd[:, :], ACT.Exp, scale=-0.5).then_inc(s.rstd, 1)
            for c in range(2):
                act.wait_ge(s.normed, c + 1)
                act.activation(acc[:, c, :], acc[:, c, :], ACT.Silu, bias=cols[:, c, 33:34], scale=cols[:, c, 32:33]).then_inc(s.swish, 1)

        @block.sync
        def _(sp):
            sp.wait_ge(s.copied, 5)
            sp.dma_start(layer(io.prompt_conv, l)[0], nat[0:CW - 1, 0, :]).then_inc(s.stored, 16)
            sp.dma_start(layer(io.prompt_pool, l)[0], nat[0:PBUF, 1, :]).then_inc(s.stored, 16)
            for h in range(2):
                sp.dma_start(layer(io.sample_conv, l)[4 * h:4 * h + 4].rearrange("b w c -> (b w) c"), nat[:, 2 + h, :]).then_inc(s.stored, 16)
            sp.dma_start(layer(io.sample_pool, l).rearrange("b w c -> (b w) c"), nat[:, 4, :]).then_inc(s.stored, 16)
            sp.wait_ge(s.stored, 80)


def compression_weights(S, l, ctx):
    nc, io, sb, psum, C = S.nc, S.io, S.sb, S.psum, S.C
    S.W1 = sb("W1", [P, 2, 8, P], ctx=ctx)
    S.W2 = sb("W2", [P, 2, P], ctx=ctx)
    S.pe_h = sb("pe_h", [P, 2], ctx=ctx)
    S.kv_s = sb("kv_s", [NS, 6 * P], ctx=ctx)
    pe_n = sb("pe_n", [32, P], ctx=ctx)
    pe_t = sb("pe_t", [P, 2, 2, 8], ctx=ctx)
    pe_b = sb("pe_b", [HD, 2], ctx=ctx)
    with stage(nc, "cw", "misc", "zero", "first", "second", "pe", "turned", "copied", "product", "half", "out") as (block, s):
        @block.vector
        def _(dve):
            dve.wait_ge(s.turned, 1)
            dve.tensor_copy(pe_t[:, :, :, :].rearrange("p c h j -> p (c h j)"), psum[:, 0, 0:32]).then_inc(s.copied, 1)
            dve.wait_ge(s.product, 1)
            sums = psum[:, 1, 0:4].rearrange("p (c h) -> p c h", c=2)
            dve.tensor_copy(pe_b[:, :], sums[HD:P, :, 1]).then_inc(s.half, 1)
            dve.wait_ge(s.half, 1)
            for k in range(KVH):
                dve.tensor_tensor(S.pe_h[HD * k:HD * k + HD, :], sums[0:HD, :, 0], pe_b[:, :], ALU.add).then_inc(s.out, 1)

        @block.gpsimd
        def _(pool):
            pool.memset(S.W2[:, :, :], 0.0).then_inc(s.zero, 1)
            pool.memset(S.misc_n[:, QT, :], 0.0).then_inc(s.misc, 1)

        @block.sync
        def _(sp):
            sp.dma_start(pe_n[:, :], layer(io.cmp_pe, l).rearrange("c (h j t) d -> (c h j) (t d)", h=2, j=8)).then_inc(s.pe, 16)
            for c in range(2):
                for h in range(2):
                    src = layer(io.cmp_w1, l)[c, 1024 * h:1024 * h + 1024].rearrange("(j q) e -> q j e", q=P)
                    sp.dma_start(S.W1[:, c, :, HD * h:HD * h + HD], src).then_inc(s.first, 16)
            sp.wait_ge(s.zero, 1)
            for c in range(2):
                for k in range(KVH):
                    r = slice(64 * k, 64 * k + 64)
                    sp.dma_start(S.W2[r, c, r], layer(io.cmp_w2, l)[c]).then_inc(s.second, 16)
            sp.wait_ge(s.second, 64)

        @block.tensor
        def _(pe):
            pe.wait_ge(s.pe, 16)
            pe.transpose(psum[:, 0, 0:32], pe_n[:, :], C["ident"][0:32, 0:32]).then_inc(s.turned, 1)
            pe.wait_ge(s.copied, 1)
            pe.wait_ge(s.first, 64)
            for c in range(2):
                for j in range(8):
                    last = pe.matmul(psum[:, 1, 2 * c:2 * c + 2], S.W1[:, c, j, :], pe_t[:, c, :, j],
                                     start=(j == 0), stop=(j == 7))
            last.then_inc(s.product, 1)


def prompt_attention(S, l, ctx):
    nc, io, sb, psum, C = S.nc, S.io, S.sb, S.psum, S.C
    H = lambda t: S.HT[:, t - 6, :]
    kvn = sb("kvn", [P, QT, 6 * P], ctx=ctx)
    strip = sb("strip", [P, HEADS, STRIP], ctx=ctx)
    tok = sb("tok", [P, 2, KVH, SEQ // 2], ctx=ctx)
    hb = sb("hb_p", [HD, 2, KVH, 31], ctx=ctx)
    hc = sb("hc", [P, 2, 31], ctx=ctx)
    kc = sb("kc", [P, 31], ctx=ctx)
    vc = sb("vc", [31, P], ctx=ctx)
    with stage(nc, "nat", "turned", "copied_act", "copied_dve", "gates", "stored", "strip", "paired", "summed",
               "half", "added", "swish", "second", "kept") as (block, s):
        def by_head(ap):
            return ap.rearrange("p (k n) -> p k n", k=KVH)

        @block.gpsimd
        def _(pool):
            for c in range(2):
                for k in range(KVH):
                    for i in range(2):
                        pool.tensor_copy(tok[HD * i:HD * i + HD, c, k, :],
                                         H(T_KV + c)[HD * k:HD * k + HD, i:SEQ:2]).then_inc(s.paired, 1)

        @block.tensor
        def _(pe):
            for q in range(QT + 1):
                n = P if q < QT else NS
                a = 2 * (q % 2)
                if q >= 2:
                    pe.wait_ge(s.copied_act, q - 1)
                    pe.wait_ge(s.copied_dve, q - 1)
                for c in range(6):
                    pe.transpose(psum[0:n, a + c // 4, (c % 4) * P:(c % 4) * P + P], H(T_KV + c)[:, q * P:q * P + n], C["ident"])
                pe.transpose(psum[0:n, a + 1, 2 * P:2 * P + M_W], H(T_MISC)[0:M_W, q * P:q * P + n],
                             C["ident"][0:M_W, 0:M_W]).then_inc(s.turned, 1)
            pe.wait_ge(s.paired, 8)
            for c in range(2):
                for k in range(KVH):
                    for j in range(8):
                        last = pe.matmul(psum[:, 4 + c, 32 * k:32 * k + 32], S.W1[:, c, j, :], tok[:, c, k, j::8],
                                         start=(j == 0), stop=(j == 7))
                last.then_inc(s.summed, 1)
            pe.wait_ge(s.swish, 2)
            pe.matmul(psum[:, 6, 0:31], S.W2[:, 0, :], hc[:, 0, :], start=True, stop=True).then_inc(s.second, 1)
            pe.matmul(psum[0:31, 7, 0:P], hc[:, 1, :], S.W2[:, 1, :], start=True, stop=True).then_inc(s.second, 1)

        @block.scalar
        def _(act):
            for q in range(QT + 1):
                n = P if q < QT else NS
                dst = kvn[:, q, 0:512] if q < QT else S.kv_s[:, 0:512]
                act.wait_ge(s.turned, q + 1)
                act.copy(dst, psum[0:n, 2 * (q % 2), :]).then_inc(s.copied_act, 1)
            for c in range(2):
                act.wait_ge(s.summed, c + 1)
                act.copy(hb[:, c, :, :], by_head(psum[HD:P, 4 + c, 0:64])[:, :, 1:32]).then_inc(s.half, 1)
            for c in range(2):
                act.wait_ge(s.added, 2 * c + 2)
                act.activation(hc[:, c, :], hc[:, c, :], ACT.Silu, bias=S.pe_h[:, c:c + 1]).then_inc(s.swish, 1)
            act.wait_ge(s.copied_dve, QT + 1)
            act.activation(S.gates[:, 0:QT, :], S.misc_n[:, 0:QT, M_GATE:M_GATE + 12], ACT.Sigmoid).then_inc(s.gates, 1)
            act.activation(S.gates[0:NS, QT, :], S.misc_n[0:NS, QT, M_GATE:M_GATE + 12], ACT.Sigmoid).then_inc(s.gates, 1)

        @block.vector
        def _(dve):
            for q in range(QT + 1):
                n = P if q < QT else NS
                dst = kvn[:, q, 512:768] if q < QT else S.kv_s[:, 512:768]
                dve.wait_ge(s.turned, q + 1)
                dve.tensor_copy(dst, psum[0:n, 2 * (q % 2) + 1, 0:256])
                dve.tensor_copy(S.misc_n[0:n, q, :], psum[0:n, 2 * (q % 2) + 1, 256:256 + M_W]).then_inc(s.copied_dve, 1)
            for c in range(2):
                dve.wait_ge(s.half, c + 1)
                for k in range(KVH):
                    dve.tensor_tensor(hc[HD * k:HD * k + HD, c, :], by_head(psum[0:HD, 4 + c, 0:64])[:, k, 0:31], hb[:, c, k, :],
                                      ALU.add).then_inc(s.added, 1)
            dve.wait_ge(s.second, 2)
            dve.tensor_copy(kc[:, :], psum[:, 6, 0:31]).then_inc(s.kept, 1)
            dve.tensor_copy(vc[:, :], psum[0:31, 7, 0:P]).then_inc(s.kept, 1)

        @block.sync
        def _(sp):
            src = bass.AP(io.line_dram.tensor, 127, [[LINE - 1, P], [P * LINE, HEADS], [1, STRIP]])
            sp.dma_start(strip[:, :, :], src).then_inc(s.strip, 16)
            sp.wait_ge(s.copied_act, QT + 1)
            sp.wait_ge(s.copied_dve, QT + 1)
            sp.dma_start(layer(io.prompt_nsa, l).rearrange("g t c k d -> t g (c k d)"), kvn[:, :, 0:512]).then_inc(s.stored, 16)
            sp.dma_start(layer(io.prompt_win, l).rearrange("a (q p) c k d -> p (a q) (c k d)", p=P), kvn[:, :, 512:768]).then_inc(s.stored, 16)
            sp.dma_start(layer(io.sample_nsa, l).rearrange("b t c k d -> (b t) (c k d)"), S.kv_s[:, 0:512]).then_inc(s.stored, 16)
            for b in range(NB):
                sp.dma_start(layer(io.sample_win, l)[b, 512 - NT:].rearrange("t c k d -> t (c k d)"),
                             S.kv_s[b * NT:b * NT + NT, 512:768]).then_inc(s.stored, 16)
            sp.wait_ge(s.strip, 16)
            sp.wait_ge(s.stored, 16 * (3 + NB))

    units = [(i, h, br) for i in range(QT) for h in range(HEADS) for br in range(3)]
    N = len(units)
    sc = sb("sc", [P, 3, 512], ctx=ctx)
    pt = sb("pt", [P, 3, 512], ctx=ctx)
    nmax = sb("nmax", [P, N], ctx=ctx)
    esum = sb("esum", [P, N], ctx=ctx)
    coef = sb("coef", [P, N], ctx=ctx)
    o = sb("o", [P, QT, 256], ctx=ctx)
    names = ("scored", "added", "step", "maxed", "exped", "turned", "pt_copied", "pv", "summed", "coef", "o_turned", "o_copied")
    with stage(nc, "att", *names) as (block, s):
        def width(n):
            i, h, br = units[n]
            return 31 if br == 0 else P * (i + 1)

        @block.tensor
        def _(pe):
            def scores(n):
                i, h, br = units[n]
                r = slice(64 * (h // GRP), 64 * (h // GRP) + 64)
                keys = kc[r, :] if br == 0 else H(T_KV + 2 * br)[r, 0:P * (i + 1)]
                if n >= 2:
                    pe.wait_ge(s.added, n - 1)
                pe.matmul(psum[:, n % 2, 0:width(n)], H(T_Q + h % GRP)[r, i * P:i * P + P], keys,
                          start=True, stop=True).then_inc(s.scored, 1)

            def turn(n):
                pe.wait_ge(s.exped, n + 1)
                if n >= 2:
                    pe.wait_ge(s.pt_copied, n - 1)
                w = width(n)
                for j in range(0, w, P):
                    m = min(P, w - j)
                    last = pe.transpose(psum[0:m, 2 + n % 2, j:j + P], sc[:, n % 3, j:j + m], C["ident"])
                last.then_inc(s.turned, 1)

            def values(n):
                i, h, br = units[n]
                k = 64 * (h // GRP)
                pe.wait_ge(s.pt_copied, n + 1)
                if n >= 2:
                    pe.wait_ge(s.summed, n - 1)
                if br == 0:
                    last = pe.matmul(psum[:, 4 + n % 2, 0:HD], pt[0:31, n % 3, 0:P], vc[:, k:k + HD], start=True, stop=True)
                else:
                    for j in range(i + 1):
                        c = (2 * br + 1) * P + k
                        last = pe.matmul(psum[:, 4 + n % 2, 0:HD], pt[:, n % 3, j * P:j * P + P], kvn[:, j, c:c + HD],
                                         start=(j == 0), stop=(j == i))
                last.then_inc(s.pv, 1)

            for n in range(N + 2):
                if n < N:
                    scores(n)
                if 1 <= n <= N:
                    turn(n - 1)
                if n >= 2:
                    values(n - 2)
            pe.wait_ge(s.summed, N)
            for i in range(QT):
                for c in range(2):
                    last = pe.transpose(psum[:, 6 + c, i * P:i * P + P], o[:, i, c * P:c * P + P], C["ident"])
            last.then_inc(s.o_turned, 1)

        @block.scalar
        def _(act):
            for n in range(N + 1):
                if n < N:
                    act.wait_ge(s.maxed, n + 1)
                    x = sc[:, n % 3, 0:width(n)]
                    act.activation(x, x, ACT.Exp, bias=nmax[:, n:n + 1], accum_out=esum[:, n:n + 1]).then_inc(s.exped, 1)
                if n >= 1:
                    m = n - 1
                    act.wait_ge(s.turned, m + 1)
                    if m >= 3:
                        act.wait_ge(s.pv, m - 2)
                    w = 31 if width(m) == 31 else P
                    x = slice(0, P if w == 31 else width(m))
                    act.copy(pt[0:w, m % 3, x], psum[0:w, 2 + m % 2, x]).then_inc(s.pt_copied, 1)
            act.wait_ge(s.o_turned, 1)
            for c in range(2):
                act.copy(S.yT[:, 4 + c, 0:SEQ], psum[:, 6 + c, :]).then_inc(s.o_copied, 1)

        @block.vector
        def _(dve):
            step = Serial(dve, s.step)
            for n in range(N + 2):
                if n < N:
                    i, h, br = units[n]
                    w = width(n)
                    x0 = 415 - P * i if br == 0 else 384 - P * i
                    bias = strip[:, h, x0:x0 + 481:16] if br == 0 else strip[:, h, x0:512]
                    x = sc[:, n % 3, 0:w]
                    dve.wait_ge(s.scored, n + 1)
                    if n >= 3:
                        dve.wait_ge(s.turned, n - 2)
                    step(dve.tensor_tensor(x, psum[:, n % 2, 0:w], bias, ALU.add), s.added)
                    step(dve.tensor_reduce(nmax[:, n:n + 1], x, AX.X, ALU.max, negate=True))
                    dve.tensor_scalar(nmax[:, n:n + 1], nmax[:, n:n + 1], -0.01 * NEG, None, ALU.min).then_inc(s.maxed, 1)
                if 1 <= n <= N:
                    m = n - 1
                    c = coef[:, m:m + 1]
                    dve.wait_ge(s.exped, m + 1)
                    step(dve.tensor_scalar(c, esum[:, m:m + 1], 1e-30, None, ALU.max))
                    step(dve.reciprocal(c, c))
                    i, h, br = units[m]
                    step(dve.tensor_tensor(c, c, S.gates[:, i, 4 * br + h:4 * br + h + 1], ALU.mult))
                if n >= 2:
                    m = n - 2
                    i, h, br = units[m]
                    out, src = o[:, i, h * HD:h * HD + HD], psum[:, 4 + m % 2, 0:HD]
                    dve.wait_ge(s.pv, m + 1)
                    if br == 0:
                        dve.tensor_scalar(out, src, coef[:, m:m + 1], None, ALU.mult).then_inc(s.summed, 1)
                    else:
                        dve.wait_ge(s.summed, m)
                        dve.scalar_tensor_tensor(out, src, coef[:, m:m + 1], out, ALU.mult, ALU.add).then_inc(s.summed, 1)


def sample_scores(S, l, ctx):
    nc, io, sb, psum, C = S.nc, S.io, S.sb, S.psum, S.C
    H = lambda t: S.HT[:, t - 6, :]
    S.q_rows = sb("q_rows", [P, P], ctx=ctx)
    S.st_sel = sb("st_sel", [P, NPG, P], ctx=ctx)
    S.st_cmp = sb("st_cmp", [P, 2, P], ctx=ctx)
    S.st_win = sb("st_win", [P, 4, P], ctx=ctx)
    S.vc = sb("vc_s", [P, 2, NB, P], ctx=ctx)
    with stage(nc, "q", "zero", "placed") as (block, s):
        @block.vector
        def _(dve):
            dve.memset(S.q_rows[:, :], 0.0).then_inc(s.zero, 1)
            dve.wait_ge(s.zero, 1)
            rows = S.q_rows[:, :].rearrange("p (b k g t) -> p b k g t", b=NB, k=KVH, g=GRP)
            for k in range(KVH):
                r = slice(64 * k, 64 * k + 64)
                for g in range(GRP):
                    dve.tensor_copy(rows[r, :, k, g, :], H(T_Q + g)[r, SEQ:].rearrange("p (b t) -> p b t", b=NB)).then_inc(s.placed, 1)

    with ExitStack() as c:
        slots, gp = 4, 4
        NG = NPG // gp
        cache = sb("cache", [P, slots, gp, 3 * P], ctx=c)
        chunks = sb("chunks", [P, 2, KVH, 8, NCH], ctx=c)
        kt = sb("kt", [P, 2, gp * P], ctx=c)
        hb = sb("hb", [HD, 2, KVH, NCB], ctx=c)
        hid = sb("hid", [P, 2, NCB], ctx=c)
        kc = sb("kc_s", [P, NCB], ctx=c)
        wk = sb("wk", [P, 4, P], ctx=c)
        wkt = sb("wkt", [P, 4 * P], ctx=c)
        names = ("turned", "k_copied", "v_copied", "sel_act", "sel_dve", "scored", "sc_copied", "summed", "half", "added", "swish",
                 "second", "kc_copied", "vc_copied", "cmp_scored", "cmp_copied", "w_turned", "w_copied", "w_scored", "w_sc_copied",
                 "w_loaded", "loaded0", "loaded1", "loaded2", "loaded3")
        with stage(nc, "scores", *names) as (block, s):
            loaded = [s.loaded0, s.loaded1, s.loaded2, s.loaded3]
            hidden_bank = (7, 0)

            def cols(b):
                return ds(b * 16, 16)

            def pairs(bank, k, i):
                return psum[HD * k:HD * k + HD, bank, :].rearrange("p (n j i) -> p i j n", j=8, i=2)[:, i]

            def pairs_to(c, k, i, g):
                return chunks[HD * i:HD * i + HD, c, k, :, g * 32:g * 32 + 32]

            @block.sync
            def _(sp):
                def sequence(b, first):
                    for g in range(NG):
                        if not first or g >= slots:
                            sp.wait_ge(s.turned, b * NG + (g - slots + 1))
                        if g % 2 == 0:
                            numbers = page_numbers(S, mybir.EngineType.SP, b, g * gp, 2 * gp)
                        for j in range(gp):
                            page = numbers[(g % 2) * gp + j]
                            src = layer(io.cache_nsa_kv, l)[ds(page, 1)].rearrange("a t c k d -> (a t) (c k d)")
                            sp.dma_start(cache[:, g % slots, j, :], src[:, 0:3 * P]).then_inc(loaded[g % slots], 16)
                        if g == 0:
                            if not first:
                                sp.wait_ge(s.w_turned, b)
                            src = layer(io.cache_win_kv, l)[ds(b, 1)].rearrange("a (j p) c k d -> p (a j) c (k d)", p=P)
                            sp.dma_start(wk[:, :, :], src[:, :, 0, :]).then_inc(s.w_loaded, 16)

                sequence(0, True)
                with sp.Fori(0, NB - 1) as i:
                    sequence(i + 1, False)

            @block.tensor
            def _(pe):
                def turn(b, g, first):
                    pe.wait_ge(loaded[g % slots], b * (16 * gp * NG // slots) + 16 * gp * (g // slots + 1))
                    if not first or g >= 2:
                        pe.wait_ge(s.k_copied, b * NG + (g - 1))
                        pe.wait_ge(s.v_copied, b * NG + (g - 1))
                        pe.wait_ge(s.sel_dve if g % 2 else s.sel_act, b * (NG // 2) + g // 2)
                    if not first and g == 0:
                        pe.wait_ge(s.added, b * 4 - 2)
                    for c in (2, 0, 1):
                        for j in range(gp):
                            last = pe.transpose(psum[:, 3 * (g % 2) + c, j * P:j * P + P],
                                                cache[:, g % slots, j, c * P:c * P + P], C["ident"])
                    last.then_inc(s.turned, 1)

                def score(b, g, first):
                    if not first and g == 0:
                        pe.wait_ge(s.sc_copied, b)
                    pe.wait_ge(s.sel_dve if g % 2 else s.sel_act, b * (NG // 2) + (g // 2 + 1))
                    for j in range(gp):
                        t = g * gp + j
                        last = pe.matmul(psum[:, 6, t * 16:t * 16 + 16], kt[:, g % 2, j * P:j * P + P], S.q_rows[:, cols(b)],
                                         start=True, stop=True)
                    last.then_inc(s.scored, 1)

                def hidden(b):
                    pe.wait_ge(s.k_copied, b * NG + NG)
                    pe.wait_ge(s.v_copied, b * NG + NG)
                    for c in (1, 0):
                        if c == 0:
                            pe.wait_ge(s.w_sc_copied, b + 1)
                        for k in range(KVH):
                            for j in range(8):
                                last = pe.matmul(psum[:, hidden_bank[c], k * NCH:(k + 1) * NCH], S.W1[:, c, j, :],
                                                 chunks[:, c, k, j, :], start=(j == 0), stop=(j == 7))
                        last.then_inc(s.summed, 1)

                def window_turn(b, first):
                    pe.wait_ge(s.w_loaded, b * 16 + 16)
                    if not first:
                        pe.wait_ge(s.cmp_copied, b * 2)
                    for j in range(4):
                        last = pe.transpose(psum[:, 7, j * P:j * P + P], wk[:, j, :], C["ident"])
                    last.then_inc(s.w_turned, 1)

                def window_score(b):
                    pe.wait_ge(s.w_copied, b + 1)
                    for j in range(4):
                        last = pe.matmul(psum[:, 7, j * 16:j * 16 + 16], wkt[:, j * P:j * P + P], S.q_rows[:, cols(b)],
                                         start=True, stop=True)
                    last.then_inc(s.w_scored, 1)

                def second_layer(b):
                    pe.wait_ge(s.swish, b * 2 + 2)
                    pe.matmul(psum[:, 7, 0:NCB], S.W2[:, 0, :], hid[:, 0, :], start=True, stop=True)
                    for j in range(2):
                        m = P - j
                        last = pe.matmul(psum[0:m, 7, (2 + j) * P:(3 + j) * P], hid[:, 1, j * P:j * P + m], S.W2[:, 1, :], start=True, stop=True)
                    last.then_inc(s.second, 1)

                def cmp_score(b):
                    pe.wait_ge(s.kc_copied, b + 1)
                    pe.wait_ge(s.vc_copied, b * 2 + 2)
                    for j in range(2):
                        m = P - j
                        last = pe.matmul(psum[0:m, 7, j * 16:j * 16 + 16], kc[:, j * P:j * P + m], S.q_rows[:, cols(b)],
                                         start=True, stop=True)
                    last.then_inc(s.cmp_scored, 1)

                def sequence(b, before):
                    first = before is None
                    for g in range(NG):
                        turn(b, g, first)
                        if g >= 1:
                            score(b, g - 1, first)
                        if g == 1 and not first:
                            second_layer(before)
                        if g == 2 and not first:
                            cmp_score(before)
                        if g == 3:
                            window_turn(b, first)
                        if g == 4:
                            window_score(b)
                    score(b, NG - 1, first)
                    hidden(b)

                sequence(0, None)
                with pe.Fori(0, NB - 1) as i:
                    sequence(i + 1, i)
                second_layer(NB - 1)
                cmp_score(NB - 1)

            @block.scalar
            def _(act):
                def vc_out(b):
                    act.wait_ge(s.second, b + 1)
                    act.wait_ge(s.kc_copied, b + 1)
                    for j in range(2):
                        m = P - j
                        act.copy(S.vc[0:m, j, ds(b, 1), :].rearrange("p a n -> p (a n)"),
                                 psum[0:m, 7, (2 + j) * P:(3 + j) * P]).then_inc(s.vc_copied, 1)

                def sequence(b, before):
                    first = before is None
                    for g in range(NG):
                        act.wait_ge(s.turned, b * NG + (g + 1))
                        if g % 2 == 0:
                            if not first or g >= 2:
                                act.wait_ge(s.scored, b * NG + (g - 1))
                            act.copy(kt[:, 0, :], psum[:, 2, :]).then_inc(s.sel_act, 1)
                        if not first and g == 0:
                            act.wait_ge(s.summed, b * 2)
                        for k in range(KVH):
                            for i in range(2):
                                last = act.copy(pairs_to(0, k, i, g), pairs(3 * (g % 2), k, i))
                        last.then_inc(s.k_copied, 1)
                        if g == 1 and not first:
                            vc_out(before)
                    for n, c in enumerate((1, 0)):
                        act.wait_ge(s.summed, b * 2 + (n + 1))
                        src = psum[HD:P, hidden_bank[c], :].rearrange("p (k n) -> p k n", k=KVH)[:, :, 1:NCH]
                        act.copy(hb[:, c, :, :], src).then_inc(s.half, 1)
                    for n, c in enumerate((1, 0)):
                        act.wait_ge(s.added, b * 4 + (2 * n + 2))
                        act.activation(hid[:, c, :], hid[:, c, :], ACT.Silu, bias=S.pe_h[:, c:c + 1]).then_inc(s.swish, 1)

                sequence(0, None)
                with act.Fori(0, NB - 1) as i:
                    sequence(i + 1, i)
                vc_out(NB - 1)

            @block.vector
            def _(dve):
                def kc_out(b):
                    dve.wait_ge(s.second, b + 1)
                    dve.tensor_copy(kc[:, :], psum[:, 7, 0:NCB]).then_inc(s.kc_copied, 1)

                def cmp_out(b):
                    dve.wait_ge(s.cmp_scored, b + 1)
                    for j in range(2):
                        m = P - j
                        dve.tensor_copy(S.st_cmp[0:m, j, cols(b)], psum[0:m, 7, j * 16:j * 16 + 16]).then_inc(s.cmp_copied, 1)

                def sequence(b, before):
                    first = before is None
                    for g in range(NG):
                        dve.wait_ge(s.turned, b * NG + (g + 1))
                        if g % 2 == 1:
                            if not first or g >= 2:
                                dve.wait_ge(s.scored, b * NG + (g - 1))
                            dve.tensor_copy(kt[:, 1, :], psum[:, 5, :]).then_inc(s.sel_dve, 1)
                        if not first and g == 0:
                            dve.wait_ge(s.summed, b * 2)
                        for k in range(KVH):
                            for i in range(2):
                                last = dve.tensor_copy(pairs_to(1, k, i, g), pairs(3 * (g % 2) + 1, k, i))
                        last.then_inc(s.v_copied, 1)
                        if g == 1 and not first:
                            kc_out(before)
                        if g == 2 and not first:
                            cmp_out(before)
                        if g == 3:
                            dve.wait_ge(s.w_turned, b + 1)
                            dve.tensor_copy(wkt[:, :], psum[:, 7, :]).then_inc(s.w_copied, 1)
                        if g == 4:
                            dve.wait_ge(s.w_scored, b + 1)
                            dve.tensor_copy(S.st_win[:, :, cols(b)], psum[:, 7, 0:64].rearrange("p (t r) -> p t r", r=16)).then_inc(s.w_sc_copied, 1)
                    dve.wait_ge(s.scored, b * NG + NG)
                    dve.tensor_copy(S.st_sel[:, :, cols(b)], psum[:, 6, :].rearrange("p (t r) -> p t r", r=16)).then_inc(s.sc_copied, 1)
                    for n, c in enumerate((1, 0)):
                        dve.wait_ge(s.half, b * 2 + (n + 1))
                        for k in range(KVH):
                            dve.tensor_tensor(hid[HD * k:HD * k + HD, c, :], psum[0:HD, hidden_bank[c], k * NCH:k * NCH + NCB],
                                              hb[:, c, k, :], ALU.add).then_inc(s.added, 1)

                sequence(0, None)
                with dve.Fori(0, NB - 1) as i:
                    sequence(i + 1, i)
                kc_out(NB - 1)
                cmp_out(NB - 1)


def sample_attention(S, l, ctx):
    nc, io, sb, psum, C = S.nc, S.io, S.sb, S.psum, S.C
    H = lambda t: S.HT[:, t - 6, :]
    NSC = PAST + NS
    near, new, cmp_bias, far = S.sbias[:, 0:128], S.sbias[:, 128:160], S.sbias[:, 160:160 + NCB], S.sbias[:, 415:416]
    by_head = sb("by_head", [P, 3, HEADS], ctx=ctx)
    gate = sb("gate", [P, 3], ctx=ctx)
    stat = sb("stat", [P, 3, 3], ctx=ctx)
    pc = sb("pc", [P, 264], ctx=ctx)
    imp = sb("imp", [P, 2, NBLK + 1], ctx=ctx)
    score = sb("score", [P, 3, NBLK + 1], ctx=ctx)
    top = sb("top", [P, 2, 8], ctx=ctx)
    block_bias = sb("block_bias", [P, NBLK + 1], ctx=ctx)
    diag = sb("diag", [P, 3, P], ctx=ctx)
    pt_cmp = sb("pt_cmp", [P, 2, P], ctx=ctx)
    pt_new = sb("pt_new", [NS, 2, P], ctx=ctx)
    rows_ctx = ExitStack()
    p_sel = sb("p_sel", [P, NSC], ctx=rows_ctx)
    p_win = sb("p_win", [P, 512 + NS], ctx=rows_ctx)
    pt_sel, pt_win = S.st_sel, S.st_win

    with stage(nc, "top", "g_prod", "g_step", "st_turned", "step", "zero", "added", "maxed", "exped", "pc", "imp", "imp2",
               "bb", "diag", "c_turned", "pt_copied") as (block, s):
        @block.tensor
        def _(pe):
            pe.matmul(psum[:, 0, 0:12], C["s_row"], S.gates[0:NS, QT, :], start=True, stop=True).then_inc(s.g_prod, 1)
            for j in range(2):
                m = P - j
                pe.transpose(psum[:, 1, j * P:j * P + m], S.st_cmp[0:m, j, :], C["ident"][0:m, 0:m]).then_inc(s.st_turned, 1)
            pe.wait_ge(s.imp, 1)
            pe.matmul(psum[:, 2, 0:NBLK + 1], C["pair"], imp[:, 1, :], start=True, stop=True).then_inc(s.imp2, 1)
            pe.wait_ge(s.diag, 1)
            for j in range(2):
                m = P - j
                pe.matmul(psum[0:m, 3, j * P:j * P + P], pc[:, 4 + j * P:4 + j * P + m], diag[:, 0, :], start=True, stop=True).then_inc(s.c_turned, 1)

        @block.scalar
        def _(act):
            act.wait_ge(s.maxed, 1)
            act.activation(pc[:, 4:4 + NCB], pc[:, 4:4 + NCB], ACT.Exp, bias=stat[:, 0, 0:1], accum_out=stat[:, 0, 1:2]).then_inc(s.exped, 1)
            act.wait_ge(s.c_turned, 2)
            for j in range(2):
                m = P - j
                act.copy(pt_cmp[0:m, j, :], psum[0:m, 3, j * P:j * P + P]).then_inc(s.pt_copied, 1)

        @block.vector
        def _(dve):
            step = Serial(dve, s.step)
            dve.memset(pc[:, :], 0.0).then_inc(s.zero, 1)
            dve.wait_ge(s.g_prod, 1)
            heads = bass.AP(C["row_head"].tensor, C["row_head"].offset, [list(C["row_head"].ap[0]), [0, 3], [1, HEADS]])
            step(dve.tensor_tensor(by_head[:, :, :], psum[:, 0, 0:12].rearrange("p (c h) -> p c h", c=3), heads, ALU.mult))
            dve.tensor_reduce(gate[:, :], by_head[:, :, :], AX.X, ALU.add).then_inc(s.g_step, 1)
            dve.wait_ge(s.st_turned, 2)
            dve.wait_ge(s.zero, 1)
            step(dve.tensor_tensor(pc[:, 4:4 + NCB], psum[:, 1, 0:NCB], cmp_bias, ALU.add), s.added)
            dve.tensor_reduce(stat[:, 0, 0:1], pc[:, 4:4 + NCB], AX.X, ALU.max, negate=True).then_inc(s.maxed, 1)
            dve.wait_ge(s.exped, 1)
            step(dve.reciprocal(stat[:, 0, 2:3], stat[:, 0, 1:2]))
            step(dve.tensor_scalar(pc[:, 4:4 + NCB], pc[:, 4:4 + NCB], stat[:, 0, 2:3], None, ALU.mult), s.pc)
            dve.wait_ge(s.g_step, 1)
            dve.tensor_scalar(diag[:, 0, :], C["ident"], gate[:, 0:1], None, ALU.mult).then_inc(s.diag, 1)
            step(dve.tensor_reduce(imp[:, 0, :], pc[:, 4:264].rearrange("p (j n) -> p j n", n=4), AX.X, ALU.add))
            dve.tensor_tensor(imp[:, 1, :], imp[:, 0, :], pc[:, 3:3 + 4 * NBLK + 1:4], ALU.add).then_inc(s.imp, 1)
            dve.wait_ge(s.imp2, 1)
            step(dve.tensor_tensor(score[:, 0, :], psum[:, 2, 0:NBLK + 1], C["force"], ALU.add))
            for r in range(2):
                step(dve.max(top[:, r, :], score[:, r, :]))
                step(dve.match_replace(score[:, r + 1, :], top[:, r, :], score[:, r, :], NEG))
            step(dve.tensor_scalar(block_bias[:, :], score[:, 2, :], 0.1 * NEG, NEG, ALU.is_gt, ALU.mult))
            dve.tensor_scalar(block_bias[:, :], block_bias[:, :], far, None, ALU.add).then_inc(s.bb, 1)

    NQ = NPG // 4
    with stage(nc, "soft", "turned", "added", "new_scored", "new_added", "w_step", "maxed", "exped", "step", "diag", "pt_turned",
               "pt_copied") as (block, s):
        @block.tensor
        def _(pe):
            for q in range(NQ + 1):
                if q >= 4:
                    pe.wait_ge(s.added, q - 3)
                src = S.st_sel if q < NQ else S.st_win
                for j in range(4):
                    last = pe.transpose(psum[:, q % 4, j * P:j * P + P], src[:, (4 * q + j) if q < NQ else j, :], C["ident"])
                last.then_inc(s.turned, 1)
            pe.matmul(psum[:, 4, 0:NS], S.q_rows[:, :], H(T_KV + 2)[:, SEQ:], start=True, stop=True).then_inc(s.new_scored, 1)
            pe.matmul(psum[:, 5, 0:NS], S.q_rows[:, :], H(T_KV + 4)[:, SEQ:], start=True, stop=True).then_inc(s.new_scored, 1)
            pe.wait_ge(s.added, NQ + 1)
            for q in range(NQ + 2):
                if q >= 4:
                    pe.wait_ge(s.pt_copied, q - 3)
                br = 1 if q == NQ else 0
                pe.wait_ge(s.diag, 2 if q >= NQ else 1)
                if q <= NQ:
                    for j in range(4):
                        x = p_sel[:, (4 * q + j) * P:(4 * q + j + 1) * P] if q < NQ else p_win[:, j * P:j * P + P]
                        last = pe.matmul(psum[:, q % 4, j * P:j * P + P], x, diag[:, 1 + br, :], start=True, stop=True)
                else:
                    pe.matmul(psum[0:NS, q % 4, 0:P], p_sel[:, PAST:], diag[:, 1, :], start=True, stop=True)
                    last = pe.matmul(psum[0:NS, q % 4, P:2 * P], p_win[:, 512:], diag[:, 2, :], start=True, stop=True)
                last.then_inc(s.pt_turned, 1)

        @block.vector
        def _(dve):
            step = Serial(dve, s.step)
            for q in range(NQ):
                dve.wait_ge(s.turned, q + 1)
                dve.tensor_tensor(p_sel[:, 512 * q:512 * q + 512].rearrange("p (j n) -> p j n", n=64),
                                  psum[:, q % 4, :].rearrange("p (j n) -> p j n", n=64), bc(block_bias[:, 8 * q:8 * q + 8], 64),
                                  ALU.add).then_inc(s.added, 1)
            dve.wait_ge(s.turned, NQ + 1)
            dve.tensor_scalar(p_win[:, 0:512], psum[:, NQ % 4, :], far, None, ALU.add).then_inc(s.added, 1)
            dve.wait_ge(s.new_scored, 2)
            dve.tensor_tensor(p_sel[:, PAST:], psum[:, 4, 0:NS], new, ALU.add).then_inc(s.new_added, 1)
            dve.tensor_tensor(p_win[:, 512:], psum[:, 5, 0:NS], new, ALU.add).then_inc(s.new_added, 1)
            dve.wait_ge(s.added, NQ + 1)
            dve.tensor_tensor(p_sel[:, PAST - P:PAST], p_sel[:, PAST - P:PAST], near, ALU.add).then_inc(s.new_added, 1)
            dve.tensor_tensor(p_win[:, 384:512], p_win[:, 384:512], near, ALU.add).then_inc(s.new_added, 1)
            dve.tensor_tensor(p_win[:, 0:NT], p_win[:, 0:NT], C["win_old"], ALU.add).then_inc(s.new_added, 1)
            dve.wait_ge(s.new_added, 5)
            dve.tensor_reduce(stat[:, 1, 0:1], p_sel[:, :], AX.X, ALU.max, negate=True).then_inc(s.maxed, 1)
            dve.tensor_reduce(stat[:, 2, 0:1], p_win[:, :], AX.X, ALU.max, negate=True).then_inc(s.maxed, 1)
            for br in (1, 2):
                dve.wait_ge(s.exped, br)
                step(dve.reciprocal(stat[:, br, 2:3], stat[:, br, 1:2]))
                step(dve.tensor_tensor(stat[:, br, 2:3], stat[:, br, 2:3], gate[:, br:br + 1], ALU.mult))
                dve.tensor_scalar(diag[:, br, :], C["ident"], stat[:, br, 2:3], None, ALU.mult).then_inc(s.diag, 1)
            for q in range(1, NQ + 2, 2):
                dve.wait_ge(s.pt_turned, q + 1)
                dst = pt_sel[:, 4 * q:4 * q + 4, :] if q < NQ else pt_new[:, :, :]
                src = psum[:, q % 4, :] if q < NQ else psum[0:NS, q % 4, 0:2 * P]
                dve.wait_ge(s.pt_copied, q)
                dve.tensor_copy(dst, src.rearrange("p (t n) -> p t n", n=P)).then_inc(s.pt_copied, 1)

        @block.scalar
        def _(act):
            act.wait_ge(s.maxed, 1)
            act.activation(p_sel[:, :], p_sel[:, :], ACT.Exp, bias=stat[:, 1, 0:1], accum_out=stat[:, 1, 1:2]).then_inc(s.exped, 1)
            act.wait_ge(s.maxed, 2)
            act.activation(p_win[:, :], p_win[:, :], ACT.Exp, bias=stat[:, 2, 0:1], accum_out=stat[:, 2, 1:2]).then_inc(s.exped, 1)
            for q in range(0, NQ + 1, 2):
                act.wait_ge(s.pt_turned, q + 1)
                if q:
                    act.wait_ge(s.pt_copied, q)
                dst = pt_sel[:, 4 * q:4 * q + 4, :] if q < NQ else pt_win[:, :, :]
                act.copy(dst, psum[:, q % 4, :].rearrange("p (t n) -> p t n", n=P)).then_inc(s.pt_copied, 1)

    rows_ctx.close()
    vsel = sb("vsel", [P, 2, NPG, P], ctx=ctx)
    vwin = sb("vwin", [P, 2, 4, P], ctx=ctx)
    vcmp = sb("vcmp", [P, 2, 2, P], ctx=ctx)
    out = sb("out_s", [P, P], ctx=ctx)
    with stage(nc, "pv", "sp_pages0", "sp_pages1", "act_pages0", "act_pages1", "window0", "window1", "moved", "product", "copied") as (block, s):
        sp_pages, act_pages, window = (s.sp_pages0, s.sp_pages1), (s.act_pages0, s.act_pages1), (s.window0, s.window1)
        half = NPG // 2

        def fetch(eng, kind, b, slot, first, loaded):
            for g in range(2):
                numbers = page_numbers(S, kind, b, first + 8 * g, 8)
                for j in range(8):
                    src = layer(io.cache_nsa_kv, l)[ds(numbers[j], 1)].rearrange("a t c k d -> (a t) (c k d)")
                    eng.dma_start(vsel[:, slot, first + 8 * g + j, :], src[:, 3 * P:4 * P]).then_inc(loaded, 16)

        @block.sync
        def _(sp):
            with sp.Fori(0, NB // 2) as i:
                for k in range(2):
                    b = i * 2 + k
                    sp.wait_ge(s.product, b + 1)
                    src = layer(io.cache_win_kv, l)[ds(b, 1)].rearrange("a (j p) c k d -> p (a j) c (k d)", p=P)
                    sp.dma_start(vwin[:, k, :, :], src[:, :, 1, :]).then_inc(window[k], 16)
                    fetch(sp, mybir.EngineType.SP, b, k, 0, sp_pages[k])

        @block.scalar
        def _(act):
            with act.Fori(0, NB // 2) as i:
                for k in range(2):
                    b = i * 2 + k
                    act.wait_ge(s.product, b + 1)
                    fetch(act, mybir.EngineType.Activation, b, k, half, act_pages[k])

        @block.vector
        def _(dve):
            with dve.Fori(0, NB // 2) as i:
                for k in range(2):
                    b = i * 2 + k
                    dve.wait_ge(s.product, b + 1)
                    for j in range(2):
                        m = P - j
                        dve.tensor_copy(vcmp[0:m, k, j, :], S.vc[0:m, j, ds(b, 1), :].rearrange("p a n -> p (a n)")).then_inc(s.moved, 1)
                    if k == 1:
                        for n in range(2):
                            dve.wait_ge(s.product, i * 2 + (n + 3))
                            dve.tensor_copy(out[:, ds((i * 2 + n) * 16, 16)], psum[:, n, 0:16]).then_inc(s.copied, 1)

        @block.tensor
        def _(pe):
            pe.sem_inc(s.product, 2)
            pe.sem_inc(s.copied, 2)
            with pe.Fori(0, NB // 2) as i:
                for k in range(2):
                    b = i * 2 + k
                    cols = ds(b * 16, 16)
                    o = psum[:, k, 0:16]
                    pe.wait_ge(s.copied, b + 1)
                    pe.matmul(o, S.kv_s[:, 3 * P:4 * P], pt_new[:, 0, cols], start=True, stop=False)
                    pe.matmul(o, S.kv_s[:, 5 * P:6 * P], pt_new[:, 1, cols], start=False, stop=False)
                    pe.wait_ge(s.moved, b * 2 + 2)
                    for j in range(2):
                        m = P - j
                        pe.matmul(o, vcmp[0:m, k, j, :], pt_cmp[0:m, j, cols], start=False, stop=False)
                    pe.wait_ge(window[k], i * 16 + 16)
                    for j in range(4):
                        pe.matmul(o, vwin[:, k, j, :], pt_win[:, j, cols], start=False, stop=False)
                    pe.wait_ge(sp_pages[k], i * (16 * half) + 16 * half)
                    pe.wait_ge(act_pages[k], i * (16 * half) + 16 * half)
                    for t in range(NPG):
                        last = pe.matmul(o, vsel[:, k, t, :], pt_sel[:, t, cols], start=False, stop=(t == NPG - 1))
                    last.then_inc(s.product, 1)

    with stage(nc, "place", "placed") as (block, s):
        @block.vector
        def _(dve):
            rows = out[:, :].rearrange("p (b k g t) -> p b k g t", b=NB, k=KVH, g=GRP)
            for k in range(KVH):
                for g in range(GRP):
                    dve.tensor_copy(S.yT[64 * g:64 * g + 64, 4 + k, SEQ:].rearrange("p (b t) -> p b t", b=NB),
                                    rows[64 * k:64 * k + 64, :, k, g, :]).then_inc(s.placed, 1)


def gated_delta(S, l, ctx):
    nc, io, sb, psum, C = S.nc, S.io, S.sb, S.psum, S.C
    H = lambda t: S.HT[:, t - 6, :]
    ident = C["ident"]
    NQ = QT + 1
    rows = [P] * QT + [NS]
    upto = [C["upto"]] * QT + [C["s_upto"]]
    total = [C["ones"]] * QT + [C["s_ones"]]
    after = [C["after"]] * QT + [C["s_after"]]
    a_b = sb("a_log_b", [P, HEADS], ctx=ctx)
    dt_b = sb("dt_bias_b", [P, HEADS], ctx=ctx)
    taps = sb("gtaps", [P, 6, 5], ctx=ctx)
    nat = sb("gnat", [P, NQ, 768], ctx=ctx)
    g = sb("g", [P, NQ, HEADS], ctx=ctx)
    beta = sb("beta", [P, NQ, HEADS], ctx=ctx)
    with ExitStack() as c:
        cv = sb("cv", [P, 6, TOK], ctx=c)
        grow = sb("grow", [5, 768], ctx=c)
        gst = sb("gst", [24, 768], ctx=c)
        us = sb("gus", [P, 6, NB, GC - 1 + NT], ctx=c)
        pack = sb("gpack", [P, 6, 24], ctx=c)
        stp = sb("stp", [GC - 1, 768], ctx=c)
        sts = sb("sts", [24, 768], ctx=c)
        sq = sb("gsq", [P, NQ, 512], ctx=c)
        rn = sb("rn", [P, NQ, 8], ctx=c)
        sp_ = sb("softplus", [P, 3, NQ, HEADS], ctx=c)
        names = ("loaded", "packed", "turned", "copied", "stored", "taps", "conv", "swish", "n_turned", "n_act", "n_dve", "squared",
                 "rsum", "rn", "a_sum", "act_step", "soft", "beta", "step", "normed")
        with stage(nc, "gconv", *names) as (block, s):
            @block.sync
            def _(sp):
                sp.dma_start(grow[0:4, :], layer(io.gdn_conv_w, l)).then_inc(s.loaded, 16)
                for i in range(2):
                    sp.dma_start(grow[4:5, 64 * i:64 * i + 64], io.gdn_norm_g[ds(l, 1)]).then_inc(s.loaded, 16)
                sp.dma_start(gst[:, :], layer(io.state_gdn_conv, l).rearrange("b w c -> (b w) c")).then_inc(s.loaded, 16)
                for dst, src in ((a_b, io.gdn_a_log), (dt_b, io.gdn_dt_bias)):
                    row = src[ds(l, 1)]
                    sp.dma_start(dst[:, :], bass.AP(row.tensor, row.offset, [[0, P], [1, HEADS]])).then_inc(s.loaded, 16)
                sp.wait_ge(s.copied, 6)
                sp.dma_start(layer(io.prompt_gconv, l)[0], stp[:, :]).then_inc(s.stored, 16)
                sp.dma_start(layer(io.sample_gconv, l).rearrange("b w c -> (b w) c"), sts[:, :]).then_inc(s.stored, 16)
                sp.wait_ge(s.stored, 32)

            @block.gpsimd
            def _(pool):
                for j in range(6):
                    x = H(T_GDN + j)[:, SEQ:].rearrange("p (b t) -> p b t", b=NB)
                    pool.tensor_copy(us[:, j, :, GC - 1:], x).then_inc(s.packed, 1)
                    pool.tensor_copy(pack[:, j, :].rearrange("p (b t) -> p b t", b=NB), x[:, :, 1:]).then_inc(s.packed, 1)

            @block.tensor
            def _(pe):
                pe.wait_ge(s.loaded, 96)
                pe.wait_ge(s.packed, 12)
                for j in range(6):
                    f = slice(j * P, j * P + P)
                    n = 5 if j == 0 else 4
                    pe.transpose(psum[:, 0, 8 * j:8 * j + n], grow[0:n, f], ident[0:n, 0:n])
                    pe.transpose(psum[:, 1, 24 * j:24 * j + 24], gst[:, f], ident[0:24, 0:24])
                    at = slice(P * (j % 4), P * (j % 4) + P)
                    pe.transpose(psum[0:GC - 1, 2 + j // 4, at], H(T_GDN + j)[:, SEQ - GC + 1:SEQ], ident)
                    last = pe.transpose(psum[0:24, 4 + j // 4, at], pack[:, j, :], ident)
                last.then_inc(s.turned, 1)
                pe.wait_ge(s.swish, 6)
                for q in range(NQ):
                    n, a = rows[q], 2 * (q % 2)
                    if q >= 2:
                        pe.wait_ge(s.n_act, q - 1)
                        pe.wait_ge(s.n_dve, q - 1)
                    for j in range(6):
                        last = pe.transpose(psum[0:n, a + j // 4, (j % 4) * P:(j % 4) * P + P], cv[:, j, q * P:q * P + n], ident)
                    last.then_inc(s.n_turned, 1)

            @block.scalar
            def _(act):
                act.wait_ge(s.turned, 1)
                tap = psum[:, 0, 0:48].rearrange("p (j n) -> p j n", n=8)
                act.copy(taps[:, 0, :], tap[:, 0, 0:5]).then_inc(s.copied, 1)
                act.copy(taps[:, 1:6, 0:4], tap[:, 1:6, 0:4]).then_inc(s.copied, 1)
                act.copy(stp[:, 0:512], psum[0:GC - 1, 2, :])
                act.copy(stp[:, 512:768], psum[0:GC - 1, 3, 0:256]).then_inc(s.copied, 1)
                act.copy(sts[:, 0:512], psum[0:24, 4, :])
                act.copy(sts[:, 512:768], psum[0:24, 5, 0:256]).then_inc(s.copied, 1)
                for j in range(2):
                    act.copy(us[:, 3 * j:3 * j + 3, :, 0:GC - 1],
                             psum[:, 1, 72 * j:72 * j + 72].rearrange("p (j b w) -> p j b w", j=3, b=NB)).then_inc(s.copied, 1)
                step = Serial(act, s.act_step)
                act.wait_ge(s.a_sum, 1)
                step(act.activation(sp_[:, 1, :, :], sp_[:, 0, :, :], ACT.Abs))
                step(act.activation(sp_[:, 1, :, :], sp_[:, 1, :, :], ACT.Exp, scale=-1.0))
                step(act.activation(a_b[:, :], a_b[:, :], ACT.Exp))
                act.activation(sp_[:, 1, :, :], sp_[:, 1, :, :], ACT.Ln, bias=C["ones"][:, 0:1]).then_inc(s.soft, 1)
                for j in range(6):
                    act.wait_ge(s.conv, j + 1)
                    act.activation(cv[:, j, :], cv[:, j, :], ACT.Silu).then_inc(s.swish, 1)
                act.activation(beta[:, :, :], S.misc_n[:, :, M_B:M_B + 4], ACT.Sigmoid).then_inc(s.beta, 1)
                for j in range(2):
                    act.activation(H(T_Z + j), H(T_Z + j), ACT.Silu).then_inc(s.beta, 1)
                for q in range(NQ):
                    n = rows[q]
                    act.wait_ge(s.n_turned, q + 1)
                    act.copy(nat[0:n, q, 0:512], psum[0:n, 2 * (q % 2), :]).then_inc(s.n_act, 1)
                    act.wait_ge(s.n_act, q + 1)
                    act.activation(sq[0:n, q, :], nat[0:n, q, 0:512], ACT.Square).then_inc(s.squared, 1)
                act.wait_ge(s.rsum, 2)
                step(act.activation(rn[:, :, :], rn[:, :, :], ACT.Ln, bias=C["eps"][:, 1:2]))
                act.activation(rn[:, :, :], rn[:, :, :], ACT.Exp, scale=-0.5).then_inc(s.rn, 1)

            @block.vector
            def _(dve):
                step = Serial(dve, s.step)
                dve.wait_ge(s.loaded, 96)
                dve.tensor_tensor(sp_[:, 0, :, :], S.misc_n[:, :, M_A:M_A + 4], bc_mid(dt_b[:, :], NQ), ALU.add).then_inc(s.a_sum, 1)
                dve.wait_ge(s.copied, 6)
                for j in range(6):
                    x, out = H(T_GDN + j), cv[:, j, :]
                    step(dve.tensor_scalar(out[:, 0:SEQ], x[:, 0:SEQ], taps[:, j, 3:4], None, ALU.mult))
                    outs = out[:, SEQ:].rearrange("p (b t) -> p b t", b=NB)
                    step(dve.tensor_scalar(outs, us[:, j, :, 3:3 + NT], taps[:, j, 3:4], None, ALU.mult))
                    for w in (2, 1, 0):
                        d = 3 - w
                        dve.scalar_tensor_tensor(out[:, d:SEQ], x[:, 0:SEQ - d], taps[:, j, w:w + 1], out[:, d:SEQ], ALU.mult, ALU.add).then_inc(s.taps, 1)
                        dve.scalar_tensor_tensor(outs, us[:, j, :, w:w + NT], taps[:, j, w:w + 1], outs, ALU.mult, ALU.add).then_inc(s.taps, 1)
                        dve.wait_ge(s.taps, 6 * j + 2 * d)
                    dve.engine_nop().then_inc(s.conv, 1)
                dve.wait_ge(s.soft, 1)
                step(dve.tensor_scalar(sp_[:, 0, :, :], sp_[:, 0, :, :], 0.0, None, ALU.max))
                step(dve.tensor_tensor(sp_[:, 0, :, :], sp_[:, 0, :, :], sp_[:, 1, :, :], ALU.add))
                step(dve.tensor_tensor(sp_[:, 0, :, :], sp_[:, 0, :, :], bc_mid(a_b[:, :], NQ), ALU.mult))
                step(dve.tensor_scalar(g[:, :, :], sp_[:, 0, :, :], -1.0, None, ALU.mult))
                dve.memset(rn[:, QT, :], 1.0).then_inc(s.rsum, 1)
                for q in range(NQ):
                    n = rows[q]
                    dve.wait_ge(s.n_turned, q + 1)
                    dve.tensor_copy(nat[0:n, q, 512:768], psum[0:n, 2 * (q % 2) + 1, 0:256]).then_inc(s.n_dve, 1)
                for q in range(NQ):
                    n = rows[q]
                    dve.wait_ge(s.squared, q + 1)
                    dve.wait_ge(s.rsum, 1)
                    last = dve.tensor_reduce(rn[0:n, q, :], sq[0:n, q, :].rearrange("p (j n) -> p j n", n=HD), AX.X, ALU.add)
                last.then_inc(s.rsum, 1)
                dve.wait_ge(s.rn, 1)
                step(dve.tensor_scalar(rn[:, :, 0:4], rn[:, :, 0:4], HD ** -0.5, None, ALU.mult))
                for q in range(NQ):
                    n = rows[q]
                    x = nat[0:n, q, 0:512].rearrange("p (j n) -> p j n", n=HD)
                    dve.tensor_tensor(x, x, bc(rn[0:n, q, :], HD), ALU.mult).then_inc(s.normed, 1)

    DTs = lambda t, q: t[0:rows[q], q, :, 0:rows[q]]
    lt = sb("lt", [P, NQ, HEADS, P], ctx=ctx)
    qk = sb("qk", [P, NQ, HEADS, P], ctx=ctx)
    inv_t = sb("inv_t", [P, NQ, HEADS, P], ctx=ctx)
    inv = sb("inv", [P, NQ, HEADS, P], ctx=ctx)
    uw = sb("uw", [P, NQ, HEADS, P], ctx=ctx)
    kl = sb("kl", [P, NQ, HEADS, HD], ctx=ctx)
    qs = sb("qs", [HD, NQ, HEADS, P], ctx=ctx)
    glast = sb("glast", [HD, HEADS, QT + NB], ctx=ctx)
    with ExitStack() as c:
        gb = sb("gb", [P, HEADS, P], ctx=c)
        egb = sb("egb", [HD, HEADS, P], ctx=c)
        dec = sb("dec", [P, HEADS, P], ctx=c)
        kT = sb("kT", [HD, HEADS, P], ctx=c)
        kbT = sb("kbT", [HD, HEADS, P], ctx=c)
        qT = sb("qT", [HD, HEADS, P], ctx=c)
        kb = sb("kb", [P, HEADS, HD], ctx=c)
        gc = sb("gc", [P, NQ, 5, HEADS], ctx=c)
        names = ("gb", "cum", "cumb", "gcum", "rest", "neg", "exp", "egb", "dec0", "dec", "dstep", "kb", "nats", "turned", "t_copied",
                 "qt", "qs", "products", "lt", "qk")
        with stage(nc, "gmat", *names) as (block, s):
            @block.tensor
            def _(pe):
                for q in range(NQ):
                    n = rows[q]
                    pe.wait_ge(s.gb, q + 1)
                    if q:
                        pe.wait_ge(s.gcum, q)
                        pe.wait_ge(s.dec0, q)
                        pe.wait_ge(s.egb, q)
                    pe.matmul(psum[0:n, 0, 0:4], upto[q], g[0:n, q, :], start=True, stop=True)
                    pe.matmul(psum[0:n, 0, 4:8], total[q], g[0:n, q, :], start=True, stop=True).then_inc(s.cum, 1)
                    for h in range(HEADS):
                        last = pe.matmul(psum[:, 1, h * P:h * P + n], gb[0:n, h, :], upto[q], start=True, stop=True)
                    last.then_inc(s.cumb, 1)
                    pe.wait_ge(s.kb, q + 1)
                    if q:
                        pe.wait_ge(s.t_copied, 3 * q)
                        pe.wait_ge(s.qs, q)
                    for i, src in enumerate((lambda h: nat[0:n, q, 256 + h * HD:320 + h * HD], lambda h: kb[0:n, h, :],
                                             lambda h: nat[0:n, q, h * HD:h * HD + HD])):
                        for h in range(HEADS):
                            last = pe.transpose(psum[0:HD, 2 + i, h * P:h * P + n], src(h), ident[0:n, 0:n])
                        last.then_inc(s.turned, 1)
                    pe.wait_ge(s.t_copied, 3 * q + 3)
                    if q:
                        pe.wait_ge(s.qk, q)
                    for h in range(HEADS):
                        pe.matmul(psum[0:n, 5, h * P:h * P + n], kT[:, h, 0:n], kbT[:, h, 0:n], start=True, stop=True)
                        last = pe.matmul(psum[0:n, 6, h * P:h * P + n], kT[:, h, 0:n], qT[:, h, 0:n], start=True, stop=True)
                    last.then_inc(s.products, 1)

            def heads(bank, n, m):
                return psum[0:n, bank, :].rearrange("p (h m) -> p h m", h=HEADS)[:, :, 0:m]

            @block.scalar
            def _(act):
                for q in range(NQ):
                    n = rows[q]
                    act.wait_ge(s.rest, q + 1)
                    act.activation(gc[0:n, q, 3:5, :], gc[0:n, q, 3:5, :], ACT.Exp).then_inc(s.exp, 1)
                    act.wait_ge(s.dec0, q + 1)
                    if q:
                        act.wait_ge(s.qs, q)
                    act.activation(egb[:, :, 0:n], heads(1, HD, n), ACT.Exp).then_inc(s.egb, 1)
                    for h in range(HEADS):
                        last = act.activation(dec[0:n, h, 0:n], dec[0:n, h, 0:n], ACT.Exp, bias=gc[0:n, q, 2, h:h + 1])
                    last.then_inc(s.dec, 1)
                    for i, dst in enumerate((kT, kbT, qT)):
                        act.wait_ge(s.turned, 3 * q + i + 1)
                        if q and i == 0:
                            act.wait_ge(s.products, q)
                        act.copy(dst[:, :, 0:n], heads(2 + i, HD, n)).then_inc(s.t_copied, 1)

            @block.vector
            def _(dve):
                for q in range(NQ):
                    n = rows[q]
                    k = nat[0:n, q, 256:512].rearrange("p (h d) -> p h d", h=HEADS)
                    v = nat[0:n, q, 512:768].rearrange("p (h d) -> p h d", h=HEADS)
                    if q:
                        dve.wait_ge(s.cumb, q)
                    dve.tensor_copy(gb[0:n, :, :], bc(g[0:n, q, :], P)).then_inc(s.gb, 1)
                    if q:
                        dve.wait_ge(s.turned, 3 * q)
                        dve.wait_ge(s.nats, 3 * q)
                    dve.tensor_tensor(kb[0:n, :, :], k, bc(beta[0:n, q, :], HD), ALU.mult).then_inc(s.kb, 1)
                    dve.tensor_tensor(uw[0:n, q, :, 0:HD], v, bc(beta[0:n, q, :], HD), ALU.mult).then_inc(s.nats, 1)
                    dve.wait_ge(s.cum, q + 1)
                    dve.tensor_copy(gc[0:n, q, 0:2, :], psum[0:n, 0, 0:8].rearrange("p (c h) -> p c h", c=2)).then_inc(s.gcum, 1)
                    dve.wait_ge(s.gcum, q + 1)
                    dve.tensor_copy(gc[0:n, q, 3, :], gc[0:n, q, 0, :])
                    dve.tensor_scalar(gc[0:n, q, 2, :], gc[0:n, q, 0, :], -1.0, None, ALU.mult)
                    dve.tensor_tensor(gc[0:n, q, 4, :], gc[0:n, q, 1, :], gc[0:n, q, 0, :], ALU.subtract).then_inc(s.rest, 1)
                    dve.wait_ge(s.cumb, q + 1)
                    if q:
                        dve.wait_ge(s.qk, q)
                    dve.tensor_tensor(dec[0:n, :, 0:n], heads(1, n, n), bc_mid(after[q], HEADS), ALU.add).then_inc(s.dec0, 1)
                    dve.wait_ge(s.exp, q + 1)
                    dve.wait_ge(s.kb, q + 1)
                    dve.tensor_tensor(uw[0:n, q, :, HD:], kb[0:n, :, :], bc(gc[0:n, q, 3, :], HD), ALU.mult).then_inc(s.nats, 1)
                    dve.tensor_tensor(kl[0:n, q, :, :], k, bc(gc[0:n, q, 4, :], HD), ALU.mult).then_inc(s.nats, 1)
                    dve.wait_ge(s.egb, q + 1)
                    if q < QT:
                        dve.tensor_copy(glast[:, :, q], egb[:, :, P - 1])
                    else:
                        dve.tensor_copy(glast[:, :, QT:], egb[:, :, NT - 1:NS:NT])
                    dve.wait_ge(s.t_copied, 3 * q + 3)
                    dve.tensor_tensor(qs[:, q, :, 0:n], qT[:, :, 0:n], egb[:, :, 0:n], ALU.mult).then_inc(s.qs, 1)
                    dve.wait_ge(s.products, q + 1)
                    dve.wait_ge(s.dec, q + 1)
                    dve.tensor_tensor(DTs(lt, q), heads(5, n, n), dec[0:n, :, 0:n], ALU.mult).then_inc(s.lt, 1)
                    dve.tensor_tensor(DTs(qk, q), heads(6, n, n), dec[0:n, :, 0:n], ALU.mult).then_inc(s.qk, 1)

    with ExitStack() as c:
        lm = sb("lm", [P, 2, HEADS, P], ctx=c)
        y = sb("y", [P, 2, HEADS, P], ctx=c)
        units = [(v, q) for v in range(1, 7) for q in range(NQ) if q < QT or v < 2]
        N = len(units)
        at = {u: n for n, u in enumerate(units)}
        with stage(nc, "ginv", "first", "first_t", "turned", "t_copied", "lm", "y", "y_copied", "delta", "updated", "step") as (block, s):
            def bank(b, q):
                return psum[0:rows[q], b, :].rearrange("p (h m) -> p h m", h=HEADS)[:, :, 0:rows[q]]

            @block.tensor
            def _(pe):
                for q in range(NQ):
                    n = rows[q]
                    pe.wait_ge(s.first_t, q + 1)
                    if q >= 2:
                        pe.wait_ge(s.t_copied, q - 1)
                    for h in range(HEADS):
                        last = pe.transpose(psum[0:n, 6 + q % 2, h * P:h * P + n], inv_t[0:n, q, h, 0:n], ident[0:n, 0:n])
                    last.then_inc(s.turned, 1)

                def lower(m):
                    v, q = units[m]
                    n = rows[q]
                    pe.wait_ge(s.lm, m + 1)
                    if v == 1:
                        pe.wait_ge(s.t_copied, q + 1)
                    else:
                        pe.wait_ge(s.updated, at[(v - 1, q)] + 1)
                    if m >= 2:
                        pe.wait_ge(s.y_copied, m - 1)
                    for h in range(HEADS):
                        last = pe.matmul(psum[0:n, m % 2, h * P:h * P + n], lm[0:n, m % 2, h, 0:n], inv[0:n, q, h, 0:n], start=True, stop=True)
                    last.then_inc(s.y, 1)

                def delta(m):
                    v, q = units[m]
                    n = rows[q]
                    pe.wait_ge(s.y_copied, m + 1)
                    if m >= 2:
                        pe.wait_ge(s.updated, m - 1)
                    for h in range(HEADS):
                        pe.matmul(psum[0:n, 2 + m % 2, h * P:h * P + n], inv_t[0:n, q, h, 0:n], y[0:n, m % 2, h, 0:n], start=True, stop=True)
                        last = pe.matmul(psum[0:n, 4 + m % 2, h * P:h * P + n], y[0:n, m % 2, h, 0:n], inv_t[0:n, q, h, 0:n], start=True, stop=True)
                    last.then_inc(s.delta, 1)

                for m in range(N + 1):
                    if m < N:
                        lower(m)
                    if m:
                        delta(m - 1)

            @block.gpsimd
            def _(pool):
                for m, (v, q) in enumerate(units):
                    n = rows[q]
                    if m >= 2:
                        pool.wait_ge(s.y, m - 1)
                    pool.tensor_tensor(lm[0:n, m % 2, :, 0:n], DTs(lt, q), bc_mid(C[f"level{v}"][0:n, 0:n], HEADS), ALU.mult).then_inc(s.lm, 1)

            @block.scalar
            def _(act):
                for q in range(NQ):
                    act.wait_ge(s.turned, q + 1)
                    act.copy(DTs(inv, q), bank(6 + q % 2, q)).then_inc(s.t_copied, 1)
                for m, (v, q) in enumerate(units):
                    n = rows[q]
                    act.wait_ge(s.y, m + 1)
                    if m >= 2:
                        act.wait_ge(s.delta, m - 1)
                    act.copy(y[0:n, m % 2, :, 0:n], bank(m % 2, q)).then_inc(s.y_copied, 1)

            @block.vector
            def _(dve):
                for q in range(NQ):
                    n = rows[q]
                    dve.tensor_tensor(DTs(inv_t, q), DTs(lt, q), bc_mid(C["level0"][0:n, 0:n], HEADS), ALU.mult).then_inc(s.first, 1)
                    dve.wait_ge(s.first, q + 1)
                    dve.tensor_tensor(DTs(inv_t, q), bc_mid(ident[0:n, 0:n], HEADS), DTs(inv_t, q), ALU.subtract).then_inc(s.first_t, 1)
                for m, (v, q) in enumerate(units):
                    dve.wait_ge(s.delta, m + 1)
                    dve.tensor_tensor(DTs(inv, q), DTs(inv, q), bank(2 + m % 2, q), ALU.subtract)
                    dve.tensor_tensor(DTs(inv_t, q), DTs(inv_t, q), bank(4 + m % 2, q), ALU.subtract).then_inc(s.updated, 1)

    wT = sb("wT", [HD, NQ, HEADS, P], ctx=ctx)
    state = sb("state", [HD, HEADS, HD], ctx=ctx)
    fade = sb("fade", [HD, HEADS, HD], ctx=ctx)
    vnew = sb("vnew", [P, HEADS, HD], ctx=ctx)
    st_s = sb("st_s", [HD, HEADS, NB, HD], ctx=ctx)
    fade_s = sb("fade_s", [HD, NB, HD], ctx=ctx)
    own = sb("own", [NS, NB, HD], ctx=ctx)
    ws = sb("ws", [NS, 2, HEADS, HD], ctx=ctx)
    vb = sb("vb", [NS, HEADS, NB, HD], ctx=ctx)
    rr = sb("rr", [P, NQ, HEADS], ctx=ctx)
    o = lambda q: nat[0:rows[q], q, 0:256].rearrange("p (h d) -> p h d", h=HEADS)
    uv = lambda q: nat[0:rows[q], q, 256:512].rearrange("p (h d) -> p h d", h=HEADS)
    with stage(nc, "guv", "loaded", "uv", "uv_copied", "wt_copied") as (block, s):
        @block.sync
        def _(sp):
            for h in range(HEADS):
                sp.dma_start(st_s[:, h, :, :], layer(io.state_gdn, l)[:, h].rearrange("b k v -> k b v")).then_inc(s.loaded, 16)
            sp.wait_ge(s.loaded, 64)

        @block.tensor
        def _(pe):
            for q in range(NQ):
                n = rows[q]
                if q >= 2:
                    pe.wait_ge(s.uv_copied, q - 1)
                    pe.wait_ge(s.wt_copied, q - 1)
                for h in range(HEADS):
                    pe.matmul(psum[0:n, 2 * (q % 2), h * HD:h * HD + HD], inv_t[0:n, q, h, 0:n], uw[0:n, q, h, 0:HD], start=True, stop=True)
                    last = pe.matmul(psum[0:HD, 2 * (q % 2) + 1, h * P:h * P + n], uw[0:n, q, h, HD:], inv_t[0:n, q, h, 0:n], start=True, stop=True)
                last.then_inc(s.uv, 1)

        @block.vector
        def _(dve):
            for q in range(NQ):
                dve.wait_ge(s.uv, q + 1)
                dve.tensor_copy(uv(q), psum[0:rows[q], 2 * (q % 2), 0:256].rearrange("p (h d) -> p h d", h=HEADS)).then_inc(s.uv_copied, 1)

        @block.scalar
        def _(act):
            for q in range(NQ):
                act.wait_ge(s.uv, q + 1)
                src = psum[0:HD, 2 * (q % 2) + 1, :].rearrange("p (h m) -> p h m", h=HEADS)[:, :, 0:rows[q]]
                act.copy(wT[:, q, :, 0:rows[q]], src).then_inc(s.wt_copied, 1)

    names = ("ws", "vnew", "out", "o_copied", "kv", "fade", "state", "s_w", "s_own", "s_ws", "s_vnew", "s_vb", "s_fade", "s_out",
             "s_kv", "s_state", "s_o", "o_done", "stored", "squared", "rsum", "astep", "rr", "normed", "turned", "yt", "zero", "ystep")
    with stage(nc, "gscan", *names) as (block, s):
        def squares(q):
            return uw[0:rows[q], q, 0:2, :].rearrange("p a b -> p (a b)")

        bank4 = lambda b, n: psum[0:n, b, 0:256].rearrange("p (h d) -> p h d", h=HEADS)

        @block.tensor
        def _(pe):
            for q in range(QT):
                pe.wait_ge(s.zero if q == 0 else s.state, max(q, 1))
                if q:
                    pe.wait_ge(s.o_copied, q)
                for h in range(HEADS):
                    last = pe.matmul(psum[:, 0, h * HD:h * HD + HD], wT[:, q, h, :], state[:, h, :], start=True, stop=True)
                last.then_inc(s.ws, 1)
                pe.wait_ge(s.vnew, q + 1)
                for h in range(HEADS):
                    last = pe.matmul(psum[0:HD, 2, h * HD:h * HD + HD], kl[:, q, h, :], vnew[:, h, :], start=True, stop=True)
                last.then_inc(s.kv, 1)
                for h in range(HEADS):
                    out = psum[:, 1, h * HD:h * HD + HD]
                    pe.matmul(out, qs[:, q, h, :], state[:, h, :], start=True, stop=False)
                    last = pe.matmul(out, qk[:, q, h, :], vnew[:, h, :], start=False, stop=True)
                last.then_inc(s.out, 1)
            for i, left in enumerate((wT, qs)):
                for h in range(HEADS):
                    n = 4 * i + h
                    if n >= 2:
                        pe.wait_ge(s.s_own, n - 1)
                    pe.matmul(psum[0:NS, 3 + n % 2, :], left[:, QT, h, 0:NS], st_s[:, h, :, :].rearrange("p b v -> p (b v)"),
                              start=True, stop=True).then_inc(s.s_w, 1)
            pe.wait_ge(s.s_vnew, 1)
            for h in range(HEADS):
                last = pe.matmul(psum[0:NS, 5, h * HD:h * HD + HD], qk[0:NS, QT, h, 0:NS], vnew[0:NS, h, :], start=True, stop=True)
            last.then_inc(s.s_out, 1)
            for h in range(HEADS):
                pe.wait_ge(s.s_vb, h + 1)
                if h >= 2:
                    pe.wait_ge(s.s_state, h - 1)
                pe.matmul(psum[0:HD, 6 + h % 2, :], kl[0:NS, QT, h, :], vb[:, h, :, :].rearrange("p b v -> p (b v)"),
                          start=True, stop=True).then_inc(s.s_kv, 1)
            pe.wait_ge(s.normed, NQ)
            pe.wait_ge(s.o_copied, QT)
            for q in range(NQ):
                n = rows[q]
                for c in range(2):
                    bankc = (0 if q < QT else 2) + c
                    last = pe.transpose(psum[:, bankc, (q % 4) * P:(q % 4) * P + n], nat[0:n, q, c * P:c * P + P], ident[0:n, 0:n])
            last.then_inc(s.turned, 1)

        @block.gpsimd
        def _(pool):
            pool.memset(state[:, :, :], 0.0).then_inc(s.zero, 1)

        @block.scalar
        def _(act):
            for q in range(QT):
                act.wait_ge(s.out, q + 1)
                act.copy(o(q), bank4(1, P)).then_inc(s.o_copied, 1)
            act.wait_ge(s.o_copied, QT)
            for q in range(QT):
                act.activation(squares(q), nat[:, q, 0:256], ACT.Square).then_inc(s.squared, 1)
            act.wait_ge(s.s_o, 1)
            act.activation(squares(QT), nat[0:NS, QT, 0:256], ACT.Square).then_inc(s.squared, 1)
            act.wait_ge(s.rsum, 2)
            act.activation(rr[:, :, :], rr[:, :, :], ACT.Ln, bias=C["eps"][:, 0:1], scale=1 / HD).then_inc(s.astep, 1)
            act.wait_ge(s.astep, 1)
            act.activation(rr[:, :, :], rr[:, :, :], ACT.Exp, scale=-0.5).then_inc(s.rr, 1)

        @block.vector
        def _(dve):
            for q in range(QT):
                dve.wait_ge(s.ws, q + 1)
                dve.tensor_tensor(vnew[:, :, :], uv(q), bank4(0, P), ALU.subtract).then_inc(s.vnew, 1)
                dve.wait_ge(s.zero if q == 0 else s.state, max(q, 1))
                dve.tensor_tensor(fade[:, :, :], state[:, :, :], bc(glast[:, :, q], HD), ALU.mult).then_inc(s.fade, 1)
                dve.wait_ge(s.fade, q + 1)
                dve.wait_ge(s.out, q + 1)
                dve.tensor_tensor(state[:, :, :], fade[:, :, :], bank4(2, HD), ALU.add).then_inc(s.state, 1)
            for i in range(2):
                for h in range(HEADS):
                    n = 4 * i + h
                    dve.wait_ge(s.s_w, n + 1)
                    if n:
                        dve.wait_ge(s.s_ws, n)
                    dve.tensor_tensor(own[:, :, :], psum[0:NS, 3 + n % 2, :].rearrange("p (b v) -> p b v", b=NB), bc(C["s_batch"], HD),
                                      ALU.mult).then_inc(s.s_own, 1)
                    dve.wait_ge(s.s_own, n + 1)
                    dve.tensor_reduce(ws[:, i, h, :], own[:, :, :].rearrange("p b v -> p v b"), AX.X, ALU.add).then_inc(s.s_ws, 1)
                if i == 0:
                    dve.wait_ge(s.s_ws, 4)
                    dve.tensor_tensor(vnew[0:NS, :, :], uv(QT), ws[:, 0, :, :], ALU.subtract).then_inc(s.s_vnew, 1)
            dve.wait_ge(s.s_vnew, 1)
            for h in range(HEADS):
                v = vnew[0:NS, h, :].unsqueeze(1).broadcast_to([NS, NB, HD])
                dve.tensor_tensor(vb[:, h, :, :], v, bc(C["s_batch"], HD), ALU.mult).then_inc(s.s_vb, 1)
            dve.wait_ge(s.s_out, 1)
            dve.wait_ge(s.s_ws, 8)
            dve.tensor_tensor(o(QT), bank4(5, NS), ws[:, 1, :, :], ALU.add).then_inc(s.s_o, 1)
            for h in range(HEADS):
                if h:
                    dve.wait_ge(s.s_state, h)
                dve.wait_ge(s.s_w, 8)
                dve.tensor_tensor(fade_s[:, :, :], st_s[:, h, :, :], bc(glast[:, h, QT:], HD), ALU.mult).then_inc(s.s_fade, 1)
                dve.wait_ge(s.s_fade, h + 1)
                dve.wait_ge(s.s_kv, h + 1)
                dve.tensor_tensor(st_s[:, h, :, :], fade_s[:, :, :], psum[0:HD, 6 + h % 2, :].rearrange("p (b v) -> p b v", b=NB),
                                  ALU.add).then_inc(s.s_state, 1)
            dve.memset(rr[:, QT, :], 1.0).then_inc(s.rsum, 1)
            dve.wait_ge(s.rsum, 1)
            for q in range(NQ):
                dve.wait_ge(s.squared, q + 1)
                last = dve.tensor_reduce(rr[0:rows[q], q, :], squares(q).rearrange("p (h d) -> p h d", h=HEADS), AX.X, ALU.add)
            last.then_inc(s.rsum, 1)
            dve.wait_ge(s.rr, 1)
            for q in range(NQ):
                dve.tensor_tensor(o(q), o(q), bc(rr[0:rows[q], q, :], HD), ALU.mult).then_inc(s.normed, 1)
            dve.wait_ge(s.turned, 1)
            for c in range(2):
                for b, t in ((c, slice(0, SEQ)), (2 + c, slice(SEQ, TOK))):
                    n = t.stop - t.start
                    dve.scalar_tensor_tensor(S.yT[:, 6 + c, t], psum[:, b, 0:n], taps[:, 0, 4:5], H(T_Z + c)[:, t],
                                             ALU.mult, ALU.mult).then_inc(s.yt, 1)

        @block.sync
        def _(sp):
            sp.wait_ge(s.state, QT)
            sp.dma_start(layer(io.prompt_gdn, l)[0].rearrange("h k v -> k h v"), state[:, :, :]).then_inc(s.stored, 16)
            sp.wait_ge(s.s_state, HEADS)
            for h in range(HEADS):
                sp.dma_start(layer(io.sample_gdn, l)[:, h].rearrange("b k v -> k b v"), st_s[:, h, :, :]).then_inc(s.stored, 16)
            sp.wait_ge(s.stored, 80)


def layer_norm(S, l, ctx, gain, bias, name):
    nc, sb, psum, C, xT = S.nc, S.sb, S.psum, S.C, S.xT
    row = sb(name + "_row", [2, D], ctx=ctx)
    col = sb(name + "_col", [P, KT, 2], ctx=ctx)
    sq = sb(name + "_sq", [P, KT, TOK], ctx=ctx)
    rstd = sb(name + "_rstd", [P, TOK], ctx=ctx)
    with stage(nc, "ln", "loaded", "turned", "copied", "mean", "centred", "squared", "var", "ln", "rstd", "normed", "done") as (block, s):
        @block.sync
        def _(sp):
            sp.dma_start(row[0:1, :], gain[ds(l, 1)]).then_inc(s.loaded, 16)
            sp.dma_start(row[1:2, :], bias[ds(l, 1)]).then_inc(s.loaded, 16)

        @block.tensor
        def _(pe):
            for h in range(2):
                for k in range(KT):
                    last = pe.matmul(psum[:, h, 0:HALF], C["mean_d"], xT[:, k, h * HALF:(h + 1) * HALF], start=(k == 0), stop=(k == KT - 1))
            last.then_inc(s.mean, 1)
            pe.wait_ge(s.loaded, 32)
            for k in range(KT):
                last = pe.transpose(psum[:, 4, 2 * k:2 * k + 2], row[:, k * P:k * P + P], C["ident"][0:2, 0:2])
            last.then_inc(s.turned, 1)
            for k in range(KT):
                pe.wait_ge(s.squared, k + 1)
                for h in range(2):
                    last = pe.matmul(psum[:, 2 + h, 0:HALF], C["mean_d"], sq[:, k, h * HALF:(h + 1) * HALF], start=(k == 0), stop=(k == KT - 1))
            last.then_inc(s.var, 1)

        @block.vector
        def _(dve):
            dve.wait_ge(s.mean, 1)
            for k in range(KT):
                dve.tensor_tensor(halves(xT[:, k, :]), halves(xT[:, k, :]), psum[:, 0:2, 0:HALF], ALU.subtract).then_inc(s.centred, 1)
            dve.wait_ge(s.centred, KT)
            dve.wait_ge(s.rstd, 1)
            for k in range(KT):
                dve.tensor_tensor(xT[:, k, :], xT[:, k, :], rstd[:, :], ALU.mult).then_inc(s.normed, 1)

        @block.scalar
        def _(act):
            for k in range(KT):
                act.wait_ge(s.centred, k + 1)
                act.activation(sq[:, k, :], xT[:, k, :], ACT.Square).then_inc(s.squared, 1)
            act.wait_ge(s.turned, 1)
            act.copy(col[:, :, :], psum[:, 4, 0:2 * KT].rearrange("p (k n) -> p k n", n=2)).then_inc(s.copied, 1)
            act.wait_ge(s.var, 1)
            act.activation(halves(rstd[:, :]), psum[:, 2:4, 0:HALF], ACT.Ln, bias=C["eps"][:, 0:1]).then_inc(s.ln, 1)
            act.wait_ge(s.ln, 1)
            act.activation(rstd[:, :], rstd[:, :], ACT.Exp, scale=-0.5).then_inc(s.rstd, 1)
            act.wait_ge(s.copied, 1)
            for k in range(KT):
                act.wait_ge(s.normed, k + 1)
                act.activation(xT[:, k, :], xT[:, k, :], ACT.Identity, bias=col[:, k, 1:2], scale=col[:, k, 0:1]).then_inc(s.done, 1)


def add_residual(S):
    def evac(dve, t, src, s):
        return dve.scalar_tensor_tensor(halves(S.xT[:, t, :]), halves(S.xT[:, t, :]), ALPHA, src, ALU.mult, ALU.add)
    return evac


def project_out(S, l, ctx):
    ring = S.sb("wo_ring", [P, 3, KT, 256], ctx=ctx)
    w_out = layer(S.io.w_out, l).rearrange("(k p) n -> p k n", p=P)

    def load(sp, g, slot, sem):
        sp.dma_start(ring[:, slot, :, :], w_out[:, :, g * 256:g * 256 + 256]).then_inc(sem, 16)

    dense(S, "out", (3, 2, load, lambda g: 1), KT, lambda k: S.yT[:, k, :],
          lambda t, k: ring[:, (t // 2) % 3, k, (t % 2) * P:(t % 2) * P + P], KT, None, add_residual(S))
    layer_norm(S, l, ctx, S.io.ln1_g, S.io.ln1_b, "ln1")


def feed_forward(S, l, ctx):
    sb, io, xT = S.sb, S.io, S.xT
    FT = DFF // P
    w_up = layer(io.w_up, l).rearrange("(k p) n -> p k n", p=P)
    w_down = layer(io.w_down, l).rearrange("(k p) n -> p k n", p=P)
    with ExitStack() as c:
        f = sb("ff", [P, FT, TOK], ctx=c)
        with ExitStack() as c2:
            ring = sb("up_ring", [P, 3, KT, 256], ctx=c2)
            pos = sb("pos", [P, TOK], ctx=c2)

            def load_up(sp, g, slot, sem):
                sp.dma_start(ring[:, slot, :, :], w_up[:, :, g * 256:g * 256 + 256]).then_inc(sem, 16)

            def squared_dve(dve, t, src, s):
                dve.tensor_scalar(halves(f[:, t, :]), src, 0.0, None, ALU.max).then_inc(s.rect_dve, 1)
                dve.wait_ge(s.rect_dve, t // 2 + 1)
                return dve.tensor_tensor(f[:, t, :], f[:, t, :], f[:, t, :], ALU.mult)

            def squared_act(act, t, src, s):
                if t > 1:
                    act.wait_ge(s.taken_act, t // 2)
                act.activation(halves(pos[:, :]), src, ACT.Relu).then_inc(s.rect_act, 1)
                act.wait_ge(s.rect_act, t // 2 + 1)
                return act.activation(f[:, t, :], pos[:, :], ACT.Square)

            dense(S, "up", (3, 2, load_up, lambda g: 1), KT, lambda k: xT[:, k, :],
                  lambda t, k: ring[:, (t // 2) % 3, k, (t % 2) * P:(t % 2) * P + P], FT, squared_act, squared_dve)
        down = sb("down_ring", [P, 3, FT, P], ctx=c)

        def load_down(sp, g, slot, sem):
            sp.dma_start(down[:, slot, :, :], w_down[:, :, g * P:g * P + P]).then_inc(sem, 16)

        dense(S, "down", (3, 1, load_down, lambda g: 1), FT, lambda k: f[:, k, :],
              lambda t, k: down[:, t % 3, k, :], KT, None, add_residual(S))
    layer_norm(S, l, ctx, io.ln2_g, io.ln2_b, "ln2")


def store_outputs(S):
    nc, io = S.nc, S.io
    with ExitStack() as c:
        y = S.sb("y_out", [P, QT + 1, D], ctx=c)
        with stage(nc, "y", "turned", "copied", "stored") as (block, s):
            @block.tensor
            def _(pe):
                for q in range(QT + 1):
                    n = P if q < QT else NS
                    if q >= 4:
                        pe.wait_ge(s.copied, q - 3)
                    for k in range(KT):
                        last = pe.transpose(S.psum[0:n, 2 * (q % 4) + k // 4, (k % 4) * P:(k % 4) * P + P],
                                            S.xT[:, k, q * P:q * P + n], S.C["ident"])
                    last.then_inc(s.turned, 1)

            @block.vector
            def _(dve):
                for q in range(QT + 1):
                    n = P if q < QT else NS
                    dve.wait_ge(s.turned, q + 1)
                    dve.tensor_copy(y[0:n, q, :].rearrange("p (b n) -> p b n", b=2),
                                    S.psum[0:n, 2 * (q % 4):2 * (q % 4) + 2, :]).then_inc(s.copied, 1)

            @block.sync
            def _(sp):
                for q in range(QT + 1):
                    sp.wait_ge(s.copied, q + 1)
                    dst = io.y_prompt[0, q * P:q * P + P, :] if q < QT else io.y_sample.rearrange("b t n -> (b t) n")
                    sp.dma_start(dst, y[0:P if q < QT else NS, q, :]).then_inc(s.stored, 16)
                sp.wait_ge(s.stored, 16 * (QT + 1))


OUTS = [("y_prompt", (1, SEQ, D)), ("y_sample", (NB, NT, D)),
        ("prompt_nsa", (DEPTH, SEQ // PAGE, PAGE, 4, KVH, HD)), ("prompt_win", (DEPTH, 1, SEQ, 2, KVH, HD)),
        ("prompt_conv", (DEPTH, 1, CW - 1, 256)), ("prompt_pool", (DEPTH, 1, PBUF, 256)),
        ("prompt_gconv", (DEPTH, 1, GC - 1, 768)), ("prompt_gdn", (DEPTH, 1, HEADS, HD, HD)),
        ("sample_nsa", (DEPTH, NB, NT, 4, KVH, HD)), ("sample_win", (DEPTH, NB, 512, 2, KVH, HD)),
        ("sample_conv", (DEPTH, NB, CW - 1, 256)), ("sample_pool", (DEPTH, NB, PBUF, 256)),
        ("sample_gconv", (DEPTH, NB, GC - 1, 768)), ("sample_gdn", (DEPTH, NB, HEADS, HD, HD))]


def kernel(**inputs):
    import concourse.bacc as bacc
    from concourse.bass_utils import run_bass_kernel_spmd

    nc = bacc.Bacc("TRN2", target_bir_lowering=False, num_devices=1)
    arrays, args = {}, {}
    io = Named(args)
    args["n_pool"] = inputs["cache_nsa_kv"].shape[1]
    table, where = pack_tables()
    for name, a in list(inputs.items()) + [("cst", table)]:
        a = np.ascontiguousarray(a)
        arrays[f"in_{name}"] = a
        args[name] = nc.dram_tensor(f"in_{name}", a.shape, mybir.dt.from_np(a.dtype), kind="ExternalInput").ap()
    for name, shape in OUTS:
        args[name] = nc.dram_tensor(f"out_{name}", shape, F32, kind="ExternalOutput").ap()
    args["line_dram"] = nc.dram_tensor("line_dram", (HEADS, P, LINE), F32, kind="Internal").ap()
    build(nc, io, where)
    r = run_bass_kernel_spmd(nc, [arrays], core_ids=[0])
    return tuple(r.results[0][f"out_{name}"] for name, _ in OUTS)
```

```python
from contextlib import ExitStack, contextmanager

import numpy as np

import concourse.bass as bass
from concourse import mybir

F32 = mybir.dt.float32
I32 = mybir.dt.int32
ALU = mybir.AluOpType
ACT = mybir.ActivationFunctionType
AX = mybir.AxisListType
ds = bass.ds

P = 128
DEPTH, D, SEQ, NB, NT = 2, 1024, 512, 8, 4
PAST, PAGE = 4096, 128
NS = NB * NT
TOK = SEQ + NS
HALF = TOK // 2
KT = D // P
QT = SEQ // P
HD, HEADS, KVH, GRP = 64, 4, 2, 2
DFF = 4 * D
CW, PBUF, GC = 31, 15, 4
IN_W = 2836
NCH = PAST // 16
NCB = NCH - 1
NPG = PAST // PAGE
NBLK = PAST // 64
ALPHA = (2 * DEPTH) ** 0.25
NEG = -1e30
STRIP = 896
LINE = 1024
T_CONV, T_GLU, T_POOL, T_Q, T_KV, T_GDN, T_Z, T_MISC = 0, 2, 4, 6, 8, 14, 20, 22
N_IN = 23
M_GATE, M_A, M_B, M_W = 0, 32, 64, 96


def bucket(d):
    d = np.maximum(np.asarray(d), 0)
    log = np.log(np.maximum(d, 1).astype(np.float32) / np.float32(16)) / np.float32(np.log(128 / 16))
    large = np.minimum(16 + (log * np.float32(16)).astype(np.int32), 31)
    return np.where(d < 16, d, large)


def one_hot(d, base=None):
    d = np.asarray(d)
    e = np.zeros((33, d.size), np.float32)
    for j, x in enumerate(d.ravel()):
        if x < 0:
            e[32, j] = 1
        else:
            e[int(bucket(x)), j] += 1
            if base is not None:
                e[base, j] -= 1
    return e


def constant_tables():
    i = np.arange(P)
    s = np.arange(NS)
    row = np.arange(P)
    rb, rh, rt = row // 16, row // 4 % 4, row % 4
    t = {}
    t["ident"] = np.eye(P)
    t["mean_d"] = np.full((P, P), 1 / D)
    t["mean_c"] = np.full((P, P), 1 / 256)
    t["ones"] = np.ones((P, P))
    t["upto"] = i[:, None] <= i[None, :]
    t["after"] = np.where(i[None, :] >= i[:, None], 0, NEG)
    for l in range(7):
        w = 2 << l
        same = i[:, None] // w == i[None, :] // w
        t[f"level{l}"] = same & (i[:, None] % w < w // 2) & (i[None, :] % w >= w // 2)
    sb = s // NT
    same = sb[:, None] == sb[None, :]
    t["s_ones"] = same
    t["s_upto"] = same & (s[:, None] <= s[None, :])
    t["s_after"] = np.where(same & (s[None, :] >= s[:, None]), 0, NEG)
    t["s_batch"] = sb[:, None] == np.arange(NB)[None, :]
    t["s_row"] = (sb[:, None] == rb[None, :]) & (s[:, None] % NT == rt[None, :])
    inv = np.zeros((P, 2, 16))
    wcol = np.zeros((P, 2))
    for c in range(2):
        for q in range(2):
            w = (2, 4, 8, 16)[2 * c + q]
            inv[64 * q:64 * q + 64, c] = 1 / np.minimum(np.arange(16) + 1, w)
            wcol[64 * q:64 * q + 64, c] = 1 / w
    t["pool_first"] = inv.reshape(P, 32)
    t["pool_inv"] = wcol
    t["eps"] = np.tile(np.array([1e-5, 1e-6]), (P, 1))
    t["line"] = one_hot(511 - np.arange(LINE))
    e = np.zeros((33, NT, 416), np.float32)
    for q in range(NT):
        e[:, q, 0:128] = one_hot(128 + q - np.arange(128), 31)
        e[:, q, 128:160] = one_hot(q - np.arange(NS) % NT)
        e[:, q, 160:415] = one_hot(PAST + q - 16 * np.arange(NCB) - 31)
        e[31, q, 415] = 1
    t["s_line"] = e.reshape(33, -1)
    t["other_b"] = np.where(rb[:, None] == sb[None, :], 0, NEG)
    t["win_old"] = np.where(np.arange(NT)[None, :] > rt[:, None], 0, NEG)
    t["pair"] = (rb[:, None] == rb[None, :]) & (rt[:, None] == rt[None, :]) & (rh[:, None] // 2 == rh[None, :] // 2)
    t["row_head"] = rh[:, None] == np.arange(HEADS)[None, :]
    force = np.zeros(NBLK + 1)
    force[[0, NBLK - 1, NBLK]] = 1e4
    t["force"] = np.tile(force, (P, 1))
    return {k: np.asarray(v, np.float32) for k, v in t.items()}


def pack_tables():
    t = constant_tables()
    for k in ("line", "s_line"):
        t[k] = t.pop(k)
    where, n = {}, 0
    for k, v in t.items():
        where[k] = (n, v.shape[0], v.shape[1])
        n += v.shape[1]
    out = np.zeros((P, n), np.float32)
    for k, v in t.items():
        out[:v.shape[0], where[k][0]:where[k][0] + v.shape[1]] = v
    return out, where


class Named:

    def __init__(self, table):
        self.table = table

    def __getattr__(self, name):
        return self.table[name]


POOL = []


@contextmanager
def stage(nc, label, *names):
    while len(POOL) < len(names):
        POOL.append(nc.alloc_semaphore(f"stage_sem{len(POOL)}"))
    used = POOL[:len(names)]
    nums = [x.num for x in used]
    assert nums == list(range(nums[0], nums[0] + len(nums)))
    with nc.Block() as block:
        yield block, Named(dict(zip(names, used)))
    nc.all_engine_barrier(sems_to_clear=range(nums[0], nums[-1] + 1))


class Serial:

    def __init__(self, eng, own):
        self.eng, self.own, self.count = eng, own, {}

    def __call__(self, ins, signal=None):
        sem = self.own if signal is None else signal
        self.count[sem.num] = self.count.get(sem.num, 0) + 1
        ins.then_inc(sem, 1)
        self.eng.wait_ge(sem, self.count[sem.num])


def bc(ap, n):
    ap = ap.unsqueeze(len(ap.shape))
    return ap.broadcast_to(list(ap.shape[:-1]) + [n])


def bc_mid(ap, n):
    ap = ap.unsqueeze(1)
    return ap.broadcast_to([ap.shape[0], n] + list(ap.shape[2:]))


def halves(ap):
    return ap.rearrange("p (h n) -> p h n", h=2)


def build(nc, io, where):
    POOL.clear()
    with ExitStack() as top:
        def sb(name, shape, dt=F32, ctx=top):
            return ctx.enter_context(nc.sbuf_tensor(name, shape, dt))

        S = Named(dict(nc=nc, io=io, where=where, sb=sb))
        S.xT = sb("xT", [P, KT, TOK])
        S.yT = sb("yT", [P, KT, TOK])
        S.cst = sb("cst", [P, where["line"][0]])
        S.C = {k: S.cst[0:r, o:o + n] for k, (o, r, n) in where.items() if k not in ("line", "s_line")}
        S.sbias = sb("sbias", [P, 416])
        S.pages = sb("pages", [1, NB * NPG], I32)
        S.psum = top.enter_context(nc.psum_tensor("psum", [P, 8, 512], F32))
        with ExitStack() as c:
            load_inputs(S, c)
        S.HT = sb("HT", [P, N_IN - 6, TOK])
        S.misc_n = sb("misc_n", [P, QT + 1, M_W])
        S.gates = sb("gates", [P, QT + 1, 12])
        S.gtaps = sb("gtaps", [P, 6, 5])
        S.gtail = sb("gtail", [P, 6, GC - 1 + 24])
        with nc.Fori(0, DEPTH) as l:
            with ExitStack() as cmp:
                compression_buffers(S, cmp)
                with ExitStack() as c:
                    S.HC = sb("HC", [P, 6, TOK], ctx=c)
                    conv_buffers(S, c)
                    with ExitStack() as c2:
                        project_in(S, l, c2)
                    conv_and_pool(S, l, c)
                attention_buffers(S, cmp)
                with ExitStack() as c:
                    natural_keys(S, l, c)
                with ExitStack() as c:
                    sample_scores(S, l, c)
                    sample_softmax(S, l, c)
                attention_outputs(S, l, cmp)
            with ExitStack() as c:
                gated_delta(S, l, c)
            with ExitStack() as c:
                S.up_ring = sb("up_ring", [P, 3, KT, 256], ctx=c)
                S.xsum = sb("xsum", [P, TOK], ctx=c)
                with ExitStack() as c2:
                    project_out(S, l, c2)
                feed_forward(S, l, c)
        store_outputs(S)


def load_inputs(S, ctx):
    nc, io, sb = S.nc, S.io, S.sb
    line = sb("line", [33, LINE], ctx=ctx)
    sline = sb("sline", [33, NT, 416], ctx=ctx)
    rel = sb("rel", [33, HEADS], ctx=ctx)
    relp = sb("relp", [33, HEADS, P], ctx=ctx)
    rels = sb("rels", [33, NT, P], ctx=ctx)
    rows = sb("rows", [P, HEADS, LINE], ctx=ctx)
    w = S.where
    xn = sb("xn", [P, QT + 1, D], ctx=ctx)
    with stage(nc, "in", "cst", "x_loaded", "loaded", "mask", "spread", "product", "copied", "stored", "turned", "x_copied") as (block, s):
        @block.scalar
        def _(act):
            act.dma_start(S.cst[:, :], io.cst[:, 0:S.where["line"][0]]).then_inc(s.cst, 16)
            act.dma_start(S.pages[:, :], io.page_table.rearrange("(a b) j -> a (b j)", a=1)).then_inc(s.cst, 16)
            act.dma_start(xn[:, 0:QT, :], io.x_prompt.rearrange("a (q p) n -> p (a q) n", p=P)).then_inc(s.x_loaded, 16)
            act.dma_start(xn[0:NS, QT, :], io.x_sample.rearrange("b t n -> (b t) n")).then_inc(s.x_loaded, 16)

        @block.sync
        def _(sp):
            sp.dma_start(line[:, :], io.cst[0:33, w["line"][0]:w["line"][0] + LINE]).then_inc(s.loaded, 16)
            sp.dma_start(sline[:, :, :], io.cst[0:33, w["s_line"][0]:w["s_line"][0] + NT * 416]
                         .rearrange("p (t n) -> p t n", t=NT)).then_inc(s.loaded, 16)
            sp.dma_start(rel[0:32, :], io.rel_bias).then_inc(s.loaded, 16)
            sp.wait_ge(s.copied, 2 * HEADS)
            sp.dma_start(io.line_dram.rearrange("h p n -> p h n"), rows[:, :, :]).then_inc(s.stored, 16)
            sp.wait_ge(s.stored, 16)

        @block.vector
        def _(dve):
            step = Serial(dve, s.spread)
            dve.memset(rel[32:33, :], NEG).then_inc(s.mask, 1)
            step(dve.memset(rels[:, :, :], 0.0))
            dve.wait_ge(s.mask, 1)
            dve.wait_ge(s.loaded, 48)
            step(dve.tensor_copy(relp[:, :, :], bc(rel[:, :], P)))
            for t in range(NT):
                dst = rels[:, t, :].rearrange("k (b h q) -> k b h q", b=NB, h=HEADS)[:, :, :, t]
                step(dve.tensor_copy(dst, bc_mid(rel[:, :], NB)))
            for h in range(HEADS):
                for j in range(2):
                    n = 2 * h + j
                    dve.wait_ge(s.product, n + 1)
                    dve.tensor_copy(rows[:, h, j * 512:(j + 1) * 512], S.psum[:, n % 4, :]).then_inc(s.copied, 1)
            dve.wait_ge(s.product, 2 * HEADS + 1)
            dve.tensor_copy(S.sbias[:, :], S.psum[:, 4, 0:416]).then_inc(s.copied, 1)
            dve.wait_ge(s.copied, 2 * HEADS + 1)
            dve.wait_ge(s.cst, 32)
            dve.tensor_tensor(S.sbias[:, 128:160], S.sbias[:, 128:160], S.C["other_b"], ALU.add).then_inc(s.copied, 1)
            for q in range(QT + 1):
                n = P if q < QT else NS
                dve.wait_ge(s.turned, q + 1)
                src = S.psum[:, 2 * (q % 2):2 * (q % 2) + 2, :].rearrange("p b (k n) -> p (b k) n", n=P)
                dve.tensor_copy(S.xT[:, :, q * P:q * P + n], src[:, :, 0:n]).then_inc(s.x_copied, 1)

        @block.tensor
        def _(pe):
            pe.wait_ge(s.spread, 2 + NT)
            for h in range(HEADS):
                for j in range(2):
                    n = 2 * h + j
                    if n >= 4:
                        pe.wait_ge(s.copied, n - 3)
                    pe.matmul(S.psum[:, n % 4, :], relp[:, h, :], line[:, j * 512:(j + 1) * 512],
                              start=True, stop=True).then_inc(s.product, 1)
            for t in range(NT):
                last = pe.matmul(S.psum[:, 4, 0:416], rels[:, t, :], sline[:, t, :], start=(t == 0), stop=(t == NT - 1))
            last.then_inc(s.product, 1)
            pe.wait_ge(s.cst, 32)
            pe.wait_ge(s.x_loaded, 32)
            for q in range(QT + 1):
                n = P if q < QT else NS
                if q < 2:
                    pe.wait_ge(s.copied, 2 * HEADS)
                else:
                    pe.wait_ge(s.x_copied, q - 1)
                for k in range(KT):
                    last = pe.transpose(S.psum[:, 2 * (q % 2) + k // 4, (k % 4) * P:(k % 4) * P + n],
                                        xn[0:n, q, k * P:(k + 1) * P], S.C["ident"][0:n, 0:n])
                last.then_inc(s.turned, 1)


def dense(S, label, weights, kt, moving, lhsT, n_tiles, evac_act, evac_dve, beside=None, on_dve=None, more_names=(), more={}, ready=0):
    nc, psum = S.nc, S.psum
    if on_dve is None:
        on_dve = lambda t: evac_act is None or t % 2 == 0

    def taken_before(t):
        return sum(on_dve(i) == on_dve(t) for i in range(t))

    slots, per, load, n_dmas = weights
    n_groups = -(-n_tiles // per)
    names = [f"loaded{i}" for i in range(slots)]
    with stage(nc, label, "product", "taken_dve", "taken_act", "rect_dve", "rect_act", "beside", *names, *more_names) as (block, s):
        loaded = [s.table[n] for n in names]

        @block.sync
        def _(sp):
            for g in range(ready, n_groups):
                if g >= slots:
                    sp.wait_ge(s.product, per * (g - slots + 1))
                load(sp, g, g % slots, loaded[g % slots])

        @block.tensor
        def _(pe):
            arrived = [0] * slots
            for t in range(n_tiles):
                g = t // per
                if t % per == 0 and g >= ready:
                    arrived[g % slots] += 16 * n_dmas(g)
                    pe.wait_ge(loaded[g % slots], arrived[g % slots])
                if t >= 4:
                    pe.wait_ge(s.taken_dve if on_dve(t - 4) else s.taken_act, taken_before(t - 4) + 1)
                for k in range(kt):
                    w = lhsT(t, k)
                    for h in range(2):
                        last = pe.matmul(psum[0:w.shape[1], 2 * (t % 4) + h, 0:HALF], w,
                                         moving(k)[:, h * HALF:(h + 1) * HALF], start=(k == 0), stop=(k == kt - 1))
                last.then_inc(s.product, 1)

        def tile_of(t):
            return psum[:, 2 * (t % 4):2 * (t % 4) + 2, 0:HALF]

        @block.vector
        def _(dve):
            for t in filter(on_dve, range(n_tiles)):
                dve.wait_ge(s.product, t + 1)
                evac_dve(dve, t, tile_of(t), s).then_inc(s.taken_dve, 1)
            if "vector" in more:
                more["vector"](dve, s)

        @block.scalar
        def _(act):
            n_beside = beside(act, s.beside) if beside else 0
            for t in range(n_tiles):
                if not on_dve(t):
                    act.wait_ge(s.product, t + 1)
                    evac_act(act, t, tile_of(t), s).then_inc(s.taken_act, 1)
                if t in more:
                    more[t](act, s)
            if n_beside:
                act.wait_ge(s.beside, 16 * n_beside)

        if "gpsimd" in more:
            @block.gpsimd
            def _(pool):
                more["gpsimd"](pool, s)


def layer(ap, l):
    dims = " ".join(f"d{i}" for i in range(len(ap.shape) - 2))
    return ap[ds(l, 1)].rearrange(f"a b {dims} -> (a b) {dims}")


def project_in(S, l, ctx):
    nc, io, sb, psum, C = S.nc, S.io, S.sb, S.psum, S.C
    conv_st = sb("conv_st", [120, 2, 256], ctx=ctx)
    pool_st = sb("pool_st", [120, 256], ctx=ctx)
    grow = sb("grow", [5, 768], ctx=ctx)
    gst = sb("gst", [24, 768], ctx=ctx)
    S.gus = sb("gus", [P, 6, NB, GC - 1 + NT], ctx=ctx)
    ring = sb("w_ring", [P, 3, KT, 256], ctx=ctx)
    misc = sb("w_misc", [P, KT, M_W], ctx=ctx)
    w_in = layer(io.w_in, l).rearrange("(k p) n -> p k n", p=P)
    start = [0, 256, 512, 768, 1024, 1280, 1536, 1804, 2060, 2316, 2572]

    def load(sp, g, slot, sem):
        if g == 3:
            for grp in range(GRP):
                for kh in range(KVH):
                    c = 768 + (kh * GRP + grp) * HD
                    sp.dma_start(ring[:, slot, :, (grp * KVH + kh) * HD:(grp * KVH + kh + 1) * HD],
                                 w_in[:, :, c:c + HD]).then_inc(sem, 16)
        elif g < 11:
            sp.dma_start(ring[:, slot, :, :], w_in[:, :, start[g]:start[g] + 256]).then_inc(sem, 16)

    u, us, v, vs = S.u, S.us, S.v, S.vs
    with stage(nc, "prep", "first", "zero", "w_loaded", "loaded", "linear", "turned", "copied") as (block, s):
        @block.gpsimd
        def _(pool):
            pool.memset(misc[:, :, :], 0.0).then_inc(s.zero, 1)
            pool.memset(S.poolw[:, :, :], 0.0).then_inc(s.zero, 1)
            pool.memset(u[:, :, 0:CW - 1], 0.0).then_inc(s.zero, 1)
            pool.memset(v[:, :, 0:PBUF], 0.0).then_inc(s.zero, 1)

        @block.sync
        def _(sp):
            sp.dma_start(S.vrow[0:CW, :], layer(io.conv_dw, l)).then_inc(s.loaded, 16)
            for i, a in enumerate((io.conv_dw_b, io.conv_ln_g, io.conv_ln_b, io.pool_scale)):
                sp.dma_start(S.vrow[CW + i:CW + i + 1, :], a[ds(l, 1)]).then_inc(s.loaded, 16)
            sp.dma_start(conv_st[:, :, :], layer(io.state_conv, l).rearrange("(h b) w c -> (b w) h c", h=2)).then_inc(s.loaded, 16)
            sp.dma_start(pool_st[:, :], layer(io.state_pool, l).rearrange("b w c -> (b w) c")).then_inc(s.loaded, 16)
            sp.dma_start(S.pw[:, :, :], layer(io.conv_pw, l).rearrange("(k p) n -> p k n", p=P)).then_inc(s.loaded, 16)
            sp.dma_start(grow[0:4, :], layer(io.gdn_conv_w, l)).then_inc(s.loaded, 16)
            for i in range(2):
                sp.dma_start(grow[4:5, 64 * i:64 * i + 64], io.gdn_norm_g[ds(l, 1)]).then_inc(s.loaded, 16)
            sp.dma_start(gst[:, :], layer(io.state_gdn_conv, l).rearrange("b w c -> (b w) c")).then_inc(s.loaded, 16)
            load(sp, 0, 0, s.first)
            sp.wait_ge(s.first, 16)

        @block.tensor
        def _(pe):
            pe.wait_ge(s.loaded, 16 * 12)
            for j in range(6):
                f = slice(j * P, j * P + P)
                n = 5 if j == 0 else 4
                pe.transpose(psum[:, 0, P + 8 * j:P + 8 * j + n], grow[0:n, f], C["ident"][0:n, 0:n])
                pe.transpose(psum[:, 2, P + 24 * j:P + 24 * j + 24], gst[:, f], C["ident"][0:24, 0:24])
            for c in range(2):
                f = slice(c * P, c * P + P)
                pe.transpose(psum[:, c, 0:35], S.vrow[:, f], C["ident"][0:35, 0:35]).then_inc(s.turned, 1)
                pe.transpose(psum[:, 2 + c, 0:120], pool_st[:, f], C["ident"][0:120, 0:120]).then_inc(s.turned, 1)
                for h in range(2):
                    pe.transpose(psum[:, 4 + 2 * c + h, 0:120], conv_st[:, h, f], C["ident"][0:120, 0:120]).then_inc(s.turned, 1)

        @block.vector
        def _(dve):
            for c in range(2):
                dve.wait_ge(s.turned, 4 * c + 4)
                dve.tensor_copy(S.cols[:, c, :], psum[:, c, 0:35]).then_inc(s.copied, 1)
                dve.tensor_copy(vs[:, c, :, 0:PBUF], psum[:, 2 + c, 0:120].rearrange("p (b w) -> p b w", b=NB)).then_inc(s.copied, 1)
                for h in range(2):
                    dve.tensor_copy(us[:, c, 4 * h:4 * h + 4, 0:CW - 1],
                                    psum[:, 4 + 2 * c + h, 0:120].rearrange("p (b w) -> p b w", b=4)).then_inc(s.copied, 1)
            tap = psum[:, 0, P:P + 48].rearrange("p (j n) -> p j n", n=8)
            dve.tensor_copy(S.gtaps[:, 0, :], tap[:, 0, 0:5]).then_inc(s.copied, 1)
            dve.tensor_copy(S.gtaps[:, 1:6, 0:4], tap[:, 1:6, 0:4]).then_inc(s.copied, 1)
            for j in range(2):
                dve.tensor_copy(S.gus[:, 3 * j:3 * j + 3, :, 0:GC - 1],
                                psum[:, 2, P + 72 * j:P + 72 * j + 72].rearrange("p (j b w) -> p j b w", j=3, b=NB)).then_inc(s.copied, 1)

        @block.scalar
        def _(act):
            act.wait_ge(s.zero, 2)
            act.dma_start(misc[:, :, M_GATE:M_GATE + 12], w_in[:, :, 1792:1804]).then_inc(s.w_loaded, 16)
            act.dma_start(misc[:, :, M_A:M_A + 4], w_in[:, :, 2828:2832]).then_inc(s.w_loaded, 16)
            act.dma_start(misc[:, :, M_B:M_B + 4], w_in[:, :, 2832:2836]).then_inc(s.w_loaded, 16)
            for g in range(4):
                r = 64 * (g % 2)
                act.dma_start(S.poolw[r:r + 64, g // 2, r:r + 64], layer(io.pool_w, l)[g]).then_inc(s.linear, 16)
            act.wait_ge(s.w_loaded, 48)
            act.wait_ge(s.linear, 64)

    def lhsT(t, k):
        if t == T_MISC:
            return misc[:, k, :]
        return ring[:, (t // 2) % 3, k, (t % 2) * P:(t % 2) * P + P]

    def dest(t):
        return S.HC[:, t, :] if t < 6 else S.HT[:, t - 6, :]

    def on_dve(t):
        return t in (T_CONV, T_GLU, T_POOL)

    def evac_act(act, t, src, s):
        if T_Q <= t < T_KV:
            return act.mul(halves(dest(t)), src, HD ** -0.5)
        if t == T_MISC:
            return act.copy(halves(dest(t)[0:M_W]), src[0:M_W])
        return act.copy(halves(dest(t)), src)

    def evac_dve(dve, t, src, s):
        return dve.tensor_copy(halves(dest(t)), src)

    def sigmoid(act, s):
        act.wait_ge(s.taken_dve, 2)
        act.wait_ge(s.taken_act, 2)
        act.activation(S.HC[:, 2:4, :], S.HC[:, 2:4, :], ACT.Sigmoid).then_inc(s.sigmoid, 1)

    def short_swish(j):
        def run(act, s):
            act.wait_ge(s.g_conv, j + 1)
            act.wait_ge(s.g_kept, 3 * j + 3)
            act.activation(dest(T_GDN + j), S.HC[:, j % 4, :], ACT.Silu).then_inc(s.g_swish, 1)
        return run

    def vector(dve, s):
        glu_and_taps(S, dve, s)
        short_conv(S, dve, s)

    def gpsimd(pool, s):
        window_sums(S, pool, s)
        keep_tails(S, pool, s)

    more = {"vector": vector, "gpsimd": gpsimd, T_GLU + 1: sigmoid}
    for j in range(6):
        more[T_GDN + j + 1] = short_swish(j)

    def keep_window(act, sem):
        for b in range(NB):
            act.dma_start(layer(io.sample_win, l)[b, 0:512 - NT].rearrange("w c k d -> w (c k d)"),
                          layer(io.cache_win_kv, l)[b, NT:].rearrange("w c k d -> w (c k d)")).then_inc(sem, 16)
        return NB

    dense(S, "proj", (3, 2, load, lambda g: 4 if g == 3 else (0 if g == 11 else 1)), KT, lambda k: S.xT[:, k, :],
          lhsT, N_IN, evac_act, evac_dve, beside=keep_window, ready=1, on_dve=on_dve, more=more,
          more_names=("sigmoid", "placed", "taps", "moved", "packed", "psteps", "pooled", "g_taps", "g_conv", "g_kept", "g_swish"))


def page_numbers(S, engine, b, first, n):
    where = S.pages[0:1, ds(b * NPG + first, n)]
    _, values = S.nc.values_load_multi_w_load_instructions(where, engines=[engine], min_val=0, max_val=S.io.n_pool - 1,
                                                           skip_runtime_bounds_check_because="each DMA checks its own bounds")
    return values


def conv_buffers(S, ctx):
    sb = S.sb
    S.vrow = sb("vrow", [35, 256], ctx=ctx)
    S.cols = sb("cols", [P, 2, 35], ctx=ctx)
    S.u = sb("u", [P, 2, CW - 1 + SEQ], ctx=ctx)
    S.us = sb("us", [P, 2, NB, CW - 1 + NT], ctx=ctx)
    S.v = sb("v", [P, 2, PBUF + SEQ], ctx=ctx)
    S.vs = sb("vs", [P, 2, NB, PBUF + NT], ctx=ctx)
    S.poolw = sb("poolw", [P, 2, P], ctx=ctx)
    S.pw = sb("pw", [P, 2, 256], ctx=ctx)
    S.pack = sb("pack", [P, 2, 3 * 120], ctx=ctx)
    S.acc = sb("acc", [P, 2, TOK], ctx=ctx)
    S.sums = [sb(f"sum{w}", [P, 2, PBUF + SEQ], ctx=ctx) for w in (2, 4, 8, 16)]
    S.sums_s = [sb(f"sums{w}", [P, 2, NB, PBUF + NT], ctx=ctx) for w in (2, 4, 8, 16)]
    S.pd = sb("pd", [P, 2, TOK], ctx=ctx)


def glu_and_taps(S, dve, s):
    HC, u, us, acc, cols = S.HC, S.u, S.us, S.acc, S.cols
    dve.wait_ge(s.sigmoid, 1)
    dve.wait_ge(s.taken_dve, 1)
    dve.tensor_tensor(u[:, :, CW - 1:], HC[:, 0:2, 0:SEQ], HC[:, 2:4, 0:SEQ], ALU.mult).then_inc(s.placed, 1)
    for c in range(2):
        dve.tensor_tensor(us[:, c, :, CW - 1:], HC[:, c, SEQ:].rearrange("p (b t) -> p b t", b=NB),
                          HC[:, 2 + c, SEQ:].rearrange("p (b t) -> p b t", b=NB), ALU.mult).then_inc(s.placed, 1)
    dve.wait_ge(s.placed, 3)

    def tap(n, w, c, out, src):
        if n >= 4:
            dve.wait_ge(s.taps, n - 3)
        if w == 0:
            dve.tensor_scalar(out, src, cols[:, c, 0:1], cols[:, c, 31:32], ALU.mult, ALU.add).then_inc(s.taps, 1)
        else:
            dve.scalar_tensor_tensor(out, src, cols[:, c, w:w + 1], out, ALU.mult, ALU.add).then_inc(s.taps, 1)

    for w in range(CW):
        for c in range(2):
            tap(4 * w + 2 * c, w, c, acc[:, c, 0:SEQ], u[:, c, w:w + SEQ])
            tap(4 * w + 2 * c + 1, w, c, acc[:, c, SEQ:].rearrange("p (b t) -> p b t", b=NB), us[:, c, :, w:w + NT])


def short_conv(S, dve, s):
    taps, us = S.gtaps, S.gus
    for j in range(6):
        x, out = S.HT[:, T_GDN + j - 6, :], S.HC[:, j % 4, :]
        outs = out[:, SEQ:].rearrange("p (b t) -> p b t", b=NB)
        dve.wait_ge(s.taken_act, T_GDN + j - 2)
        dve.wait_ge(s.g_kept, 3 * j + 1)
        if j >= 4:
            dve.wait_ge(s.g_swish, j - 3)
        dve.tensor_scalar(out[:, 0:SEQ], x[:, 0:SEQ], taps[:, j, 3:4], None, ALU.mult).then_inc(s.g_taps, 1)
        dve.tensor_scalar(outs, us[:, j, :, 3:3 + NT], taps[:, j, 3:4], None, ALU.mult).then_inc(s.g_taps, 1)
        for w in (2, 1, 0):
            d = 3 - w
            dve.wait_ge(s.g_taps, 8 * j + 2 * d)
            dve.scalar_tensor_tensor(out[:, d:SEQ], x[:, 0:SEQ - d], taps[:, j, w:w + 1], out[:, d:SEQ], ALU.mult, ALU.add).then_inc(s.g_taps, 1)
            last = dve.scalar_tensor_tensor(outs, us[:, j, :, w:w + NT], taps[:, j, w:w + 1], outs, ALU.mult, ALU.add)
            last.then_inc(s.g_taps, 1)
        dve.wait_ge(s.g_taps, 8 * j + 8)
        dve.engine_nop().then_inc(s.g_conv, 1)


def keep_tails(S, pool, s):
    for j in range(6):
        h = S.HT[:, T_GDN + j - 6, :]
        x = h[:, SEQ:].rearrange("p (b t) -> p b t", b=NB)
        pool.wait_ge(s.taken_act, T_GDN + j - 2)
        pool.tensor_copy(S.gus[:, j, :, GC - 1:], x).then_inc(s.g_kept, 1)
        pool.tensor_copy(S.gtail[:, j, GC - 1:].rearrange("p (b t) -> p b t", b=NB), x[:, :, 1:]).then_inc(s.g_kept, 1)
        pool.tensor_copy(S.gtail[:, j, 0:GC - 1], h[:, SEQ - GC + 1:SEQ]).then_inc(s.g_kept, 1)


def window_sums(S, pool, s):
    HC, v, vs, us, pack, pd, sums, sums_s, C = S.HC, S.v, S.vs, S.us, S.pack, S.pd, S.sums, S.sums_s, S.C
    pool.wait_ge(s.taken_dve, 3)
    pool.wait_ge(s.taken_act, 3)
    pool.tensor_copy(v[:, :, PBUF:], HC[:, 4:6, 0:SEQ]).then_inc(s.moved, 1)
    for c in range(2):
        pool.tensor_copy(vs[:, c, :, PBUF:], HC[:, 4 + c, SEQ:].rearrange("p (b t) -> p b t", b=NB)).then_inc(s.moved, 1)
    pool.wait_ge(s.moved, 3)
    pool.wait_ge(s.placed, 3)
    for c in range(2):
        for h in range(2):
            pool.tensor_copy(pack[:, c, h * 120:h * 120 + 120].rearrange("p (b w) -> p b w", b=4),
                             us[:, c, 4 * h:4 * h + 4, NT:]).then_inc(s.packed, 1)
        pool.tensor_copy(pack[:, c, 240:360].rearrange("p (b w) -> p b w", b=NB), vs[:, c, :, NT:]).then_inc(s.packed, 1)
    step = Serial(pool, s.psteps)
    a, b = v, vs
    for i, w in enumerate((2, 4, 8, 16)):
        h = w // 2
        step(pool.tensor_tensor(sums[i][:, :, w - 1:], a[:, :, w - 1:], a[:, :, w - 1 - h:PBUF + SEQ - h], ALU.add))
        for c in range(2):
            step(pool.tensor_tensor(sums_s[i][:, c, :, w - 1:], b[:, c, :, w - 1:], b[:, c, :, w - 1 - h:PBUF + NT - h], ALU.add))
        a, b = sums[i], sums_s[i]
    for i in range(4):
        c, r = i // 2, slice(64 * (i % 2), 64 * (i % 2) + 64)
        inv = C["pool_inv"][r, c:c + 1]
        pool.tensor_scalar(pd[r, c, 16:SEQ], sums[i][r, c, PBUF + 16:], inv, None, ALU.mult)
        pool.tensor_tensor(pd[r, c, 0:16], sums[i][r, c, PBUF:PBUF + 16], C["pool_first"][r, 16 * c:16 * c + 16], ALU.mult)
        step(pool.tensor_scalar(pd[r, c, SEQ:].rearrange("p (b t) -> p b t", b=NB), sums_s[i][r, c, :, PBUF:], inv, None, ALU.mult))
    pool.tensor_tensor(pd[:, :, :], pd[:, :, :], HC[:, 4:6, :], ALU.subtract).then_inc(s.pooled, 1)


def conv_and_pool(S, l, ctx):
    nc, io, sb, psum, C = S.nc, S.io, S.sb, S.psum, S.C
    u, v, pack, acc, pd, cols, poolw, pw = S.u, S.v, S.pack, S.acc, S.pd, S.cols, S.poolw, S.pw
    nat = sb("nat", [120, 5, 256], ctx=ctx)
    sq = sb("sq", [P, 2, TOK], ctx=ctx)
    rstd = sb("rstd", [P, TOK], ctx=ctx)
    names = ("turned", "copied", "stored", "mean", "centred", "squared", "var", "ln", "rstd", "normed", "swish", "linear",
             "scaled", "pointwise", "out", "zero", "misc", "cmp")
    with stage(nc, "conv", *names) as (block, s):
        @block.gpsimd
        def _(pool):
            pool.memset(S.W2[:, :, :], 0.0).then_inc(s.zero, 1)
            pool.memset(S.misc_n[:, QT, :], 0.0).then_inc(s.misc, 1)

        @block.vector
        def _(dve):
            dve.wait_ge(s.mean, 1)
            for c in range(2):
                dve.tensor_tensor(halves(acc[:, c, :]), halves(acc[:, c, :]), psum[:, 6:8, 0:HALF], ALU.subtract).then_inc(s.centred, 1)
            dve.wait_ge(s.rstd, 1)
            for c in range(2):
                dve.wait_ge(s.centred, 2)
                dve.tensor_tensor(acc[:, c, :], acc[:, c, :], rstd[:, :], ALU.mult).then_inc(s.normed, 1)
            for c in range(2):
                dve.wait_ge(s.pointwise, c + 1)
                dve.tensor_copy(halves(S.yT[:, c, :]), psum[:, 2 * c:2 * c + 2, 0:HALF]).then_inc(s.out, 1)

        @block.tensor
        def _(pe):
            for h in range(2):
                for c in range(2):
                    last = pe.matmul(psum[:, 6 + h, 0:HALF], C["mean_c"], acc[:, c, h * HALF:(h + 1) * HALF], start=(c == 0), stop=(c == 1))
            last.then_inc(s.mean, 1)
            for c in range(2):
                srcs = (u[:, c, SEQ:], v[:, c, SEQ:], pack[:, c, 0:120], pack[:, c, 120:240], pack[:, c, 240:360])
                for j, src in enumerate(srcs):
                    pe.transpose(psum[0:src.shape[1], j, c * P:c * P + P], src, C["ident"]).then_inc(s.turned, 1)
            pe.wait_ge(s.copied, 5)
            for c in range(2):
                for h in range(2):
                    last = pe.matmul(psum[:, 2 * c + h, 0:HALF], poolw[:, c, :], pd[:, c, h * HALF:(h + 1) * HALF], start=True, stop=True)
                last.then_inc(s.linear, 1)
            pe.wait_ge(s.squared, 1)
            for h in range(2):
                for c in range(2):
                    last = pe.matmul(psum[:, 6 + h, 0:HALF], C["mean_c"], sq[:, c, h * HALF:(h + 1) * HALF], start=(c == 0), stop=(c == 1))
            last.then_inc(s.var, 1)
            pe.wait_ge(s.swish, 2)
            pe.wait_ge(s.scaled, 2)
            for c in range(2):
                for k in range(2):
                    for h in range(2):
                        last = pe.matmul(psum[:, 2 * c + h, 0:HALF], pw[:, k, c * P:c * P + P], acc[:, k, h * HALF:(h + 1) * HALF],
                                         start=(k == 0), stop=(k == 1))
                last.then_inc(s.pointwise, 1)

        @block.scalar
        def _(act):
            act.wait_ge(s.turned, 10)
            for j, n in enumerate((CW - 1, PBUF, 120, 120, 120)):
                act.copy(nat[0:n, j, :], psum[0:n, j, 0:256]).then_inc(s.copied, 1)
            for c in range(2):
                act.wait_ge(s.linear, c + 1)
                act.mul(halves(S.yT[:, 2 + c, :]), psum[:, 2 * c:2 * c + 2, 0:HALF], cols[:, c, 34:35]).then_inc(s.scaled, 1)
            act.wait_ge(s.centred, 2)
            act.activation(sq[:, :, :], acc[:, :, :], ACT.Square).then_inc(s.squared, 1)
            act.wait_ge(s.var, 1)
            act.activation(halves(rstd[:, :]), psum[:, 6:8, 0:HALF], ACT.Ln, bias=C["eps"][:, 0:1]).then_inc(s.ln, 1)
            act.wait_ge(s.ln, 1)
            act.activation(rstd[:, :], rstd[:, :], ACT.Exp, scale=-0.5).then_inc(s.rstd, 1)
            for c in range(2):
                act.wait_ge(s.normed, c + 1)
                act.activation(acc[:, c, :], acc[:, c, :], ACT.Silu, bias=cols[:, c, 33:34], scale=cols[:, c, 32:33]).then_inc(s.swish, 1)

        @block.sync
        def _(sp):
            compression_loads(S, l, sp, s)
            sp.wait_ge(s.copied, 5)
            sp.dma_start(layer(io.prompt_conv, l)[0], nat[0:CW - 1, 0, :]).then_inc(s.stored, 16)
            sp.dma_start(layer(io.prompt_pool, l)[0], nat[0:PBUF, 1, :]).then_inc(s.stored, 16)
            for h in range(2):
                sp.dma_start(layer(io.sample_conv, l)[4 * h:4 * h + 4].rearrange("b w c -> (b w) c"), nat[:, 2 + h, :]).then_inc(s.stored, 16)
            sp.dma_start(layer(io.sample_pool, l).rearrange("b w c -> (b w) c"), nat[:, 4, :]).then_inc(s.stored, 16)
            sp.wait_ge(s.stored, 80)
            sp.wait_ge(s.cmp, 16 * 9)


def attention_buffers(S, ctx):
    sb = S.sb
    S.st_sel = sb("st_sel", [P, NPG, P], ctx=ctx)
    S.st_win = sb("st_win", [P, 4, P], ctx=ctx)
    S.vc = sb("vc_s", [P, 2, NB, P], ctx=ctx)
    S.kv_s = sb("kv_s", [NS, 6 * P], ctx=ctx)
    S.pt_cmp = sb("pt_cmp", [P, 2, P], ctx=ctx)
    S.pt_new = sb("pt_new", [NS, 2, P], ctx=ctx)
    S.kvn = sb("kvn", [P, QT, 6 * P], ctx=ctx)
    S.kc_p = sb("kc", [P, 31], ctx=ctx)
    S.vc_p = sb("vc", [31, P], ctx=ctx)


def compression_buffers(S, ctx):
    sb = S.sb
    S.W1 = sb("W1", [P, 2, 8, P], ctx=ctx)
    S.W2 = sb("W2", [P, 2, P], ctx=ctx)
    S.pe_h = sb("pe_h", [P, 2], ctx=ctx)
    S.pe_n = sb("pe_n", [32, P], ctx=ctx)


def compression_loads(S, l, sp, s):
    io = S.io
    sp.dma_start(S.pe_n[:, :], layer(io.cmp_pe, l).rearrange("c (h j t) d -> (c h j) (t d)", h=2, j=8)).then_inc(s.cmp, 16)
    for c in range(2):
        for h in range(2):
            src = layer(io.cmp_w1, l)[c, 1024 * h:1024 * h + 1024].rearrange("(j q) e -> q j e", q=P)
            sp.dma_start(S.W1[:, c, :, HD * h:HD * h + HD], src).then_inc(s.cmp, 16)
    sp.wait_ge(s.zero, 1)
    for c in range(2):
        for k in range(KVH):
            r = slice(64 * k, 64 * k + 64)
            sp.dma_start(S.W2[r, c, r], layer(io.cmp_w2, l)[c]).then_inc(s.cmp, 16)


def natural_keys(S, l, ctx):
    nc, io, sb, psum, C = S.nc, S.io, S.sb, S.psum, S.C
    H = lambda t: S.HT[:, t - 6, :]
    kvn, kc, vc = S.kvn, S.kc_p, S.vc_p
    tok = sb("tok", [P, 2, KVH, SEQ // 2], ctx=ctx)
    hb = sb("hb_p", [HD, 2, KVH, 31], ctx=ctx)
    hc = sb("hc", [P, 2, 31], ctx=ctx)
    pe_t = sb("pe_t", [P, 2, 2, 8], ctx=ctx)
    pe_b = sb("pe_b", [HD, 2], ctx=ctx)
    with stage(nc, "nat", "turned", "copied_act", "copied_dve", "gates", "stored", "paired", "summed",
               "half", "added", "swish", "second", "kept", "pe_turned", "pe_copied", "pe_product", "pe_half", "pe_out") as (block, s):
        def by_head(ap):
            return ap.rearrange("p (k n) -> p k n", k=KVH)

        @block.gpsimd
        def _(pool):
            for c in range(2):
                for k in range(KVH):
                    for i in range(2):
                        pool.tensor_copy(tok[HD * i:HD * i + HD, c, k, :],
                                         H(T_KV + c)[HD * k:HD * k + HD, i:SEQ:2]).then_inc(s.paired, 1)

        @block.tensor
        def _(pe):
            pe.transpose(psum[:, 6, 0:32], S.pe_n[:, :], C["ident"][0:32, 0:32]).then_inc(s.pe_turned, 1)
            for q in range(QT + 1):
                n = P if q < QT else NS
                a = 2 * (q % 2)
                if q >= 2:
                    pe.wait_ge(s.copied_act, q - 1)
                    pe.wait_ge(s.copied_dve, q - 1)
                for c in range(6):
                    pe.transpose(psum[0:n, a + c // 4, (c % 4) * P:(c % 4) * P + P], H(T_KV + c)[:, q * P:q * P + n], C["ident"])
                pe.transpose(psum[0:n, a + 1, 2 * P:2 * P + M_W], H(T_MISC)[0:M_W, q * P:q * P + n],
                             C["ident"][0:M_W, 0:M_W]).then_inc(s.turned, 1)
            pe.wait_ge(s.pe_copied, 1)
            for c in range(2):
                for j in range(8):
                    last = pe.matmul(psum[:, 7, 2 * c:2 * c + 2], S.W1[:, c, j, :], pe_t[:, c, :, j],
                                     start=(j == 0), stop=(j == 7))
            last.then_inc(s.pe_product, 1)
            pe.wait_ge(s.paired, 8)
            for c in range(2):
                for j in range(8):
                    last = pe.matmul(psum[:, 4 + c, 0:64], S.W1[:, c, j, :], tok[:, c, :, j::8], start=(j == 0), stop=(j == 7))
                last.then_inc(s.summed, 1)
            pe.wait_ge(s.swish, 2)
            pe.matmul(psum[:, 6, 0:31], S.W2[:, 0, :], hc[:, 0, :], start=True, stop=True).then_inc(s.second, 1)
            pe.matmul(psum[0:31, 7, 0:P], hc[:, 1, :], S.W2[:, 1, :], start=True, stop=True).then_inc(s.second, 1)

        @block.scalar
        def _(act):
            for q in range(QT + 1):
                n = P if q < QT else NS
                dst = kvn[:, q, 0:512] if q < QT else S.kv_s[:, 0:512]
                act.wait_ge(s.turned, q + 1)
                act.copy(dst, psum[0:n, 2 * (q % 2), :]).then_inc(s.copied_act, 1)
            for c in range(2):
                act.wait_ge(s.summed, c + 1)
                act.copy(hb[:, c, :, :], by_head(psum[HD:P, 4 + c, 0:64])[:, :, 1:32]).then_inc(s.half, 1)
            act.wait_ge(s.pe_out, 2)
            for c in range(2):
                act.wait_ge(s.added, 2 * c + 2)
                act.activation(hc[:, c, :], hc[:, c, :], ACT.Silu, bias=S.pe_h[:, c:c + 1]).then_inc(s.swish, 1)
            act.wait_ge(s.copied_dve, QT + 1)
            act.activation(S.gates[:, 0:QT, :], S.misc_n[:, 0:QT, M_GATE:M_GATE + 12], ACT.Sigmoid).then_inc(s.gates, 1)
            act.activation(S.gates[0:NS, QT, :], S.misc_n[0:NS, QT, M_GATE:M_GATE + 12], ACT.Sigmoid).then_inc(s.gates, 1)

        @block.vector
        def _(dve):
            dve.wait_ge(s.pe_turned, 1)
            dve.tensor_copy(pe_t[:, :, :, :].rearrange("p c h j -> p (c h j)"), psum[:, 6, 0:32]).then_inc(s.pe_copied, 1)
            for q in range(QT + 1):
                n = P if q < QT else NS
                dst = kvn[:, q, 512:768] if q < QT else S.kv_s[:, 512:768]
                dve.wait_ge(s.turned, q + 1)
                dve.tensor_copy(dst, psum[0:n, 2 * (q % 2) + 1, 0:256])
                dve.tensor_copy(S.misc_n[0:n, q, :], psum[0:n, 2 * (q % 2) + 1, 256:256 + M_W]).then_inc(s.copied_dve, 1)
            dve.wait_ge(s.pe_product, 1)
            sums = psum[:, 7, 0:4].rearrange("p (c h) -> p c h", c=2)
            dve.tensor_copy(pe_b[:, :], sums[HD:P, :, 1]).then_inc(s.pe_half, 1)
            dve.wait_ge(s.pe_half, 1)
            for k in range(KVH):
                dve.tensor_tensor(S.pe_h[HD * k:HD * k + HD, :], sums[0:HD, :, 0], pe_b[:, :], ALU.add).then_inc(s.pe_out, 1)
            for c in range(2):
                dve.wait_ge(s.half, c + 1)
                for k in range(KVH):
                    dve.tensor_tensor(hc[HD * k:HD * k + HD, c, :], by_head(psum[0:HD, 4 + c, 0:64])[:, k, 0:31], hb[:, c, k, :],
                                      ALU.add).then_inc(s.added, 1)
            dve.wait_ge(s.second, 2)
            dve.tensor_copy(kc[:, :], psum[:, 6, 0:31]).then_inc(s.kept, 1)
            dve.tensor_copy(vc[:, :], psum[0:31, 7, 0:P]).then_inc(s.kept, 1)

        @block.sync
        def _(sp):
            sp.wait_ge(s.copied_act, QT + 1)
            sp.wait_ge(s.copied_dve, QT + 1)
            sp.dma_start(layer(io.prompt_nsa, l).rearrange("g t c k d -> t g (c k d)"), kvn[:, :, 0:512]).then_inc(s.stored, 16)
            sp.dma_start(layer(io.prompt_win, l).rearrange("a (q p) c k d -> p (a q) (c k d)", p=P), kvn[:, :, 512:768]).then_inc(s.stored, 16)
            sp.dma_start(layer(io.sample_nsa, l).rearrange("b t c k d -> (b t) (c k d)"), S.kv_s[:, 0:512]).then_inc(s.stored, 16)
            for b in range(NB):
                sp.dma_start(layer(io.sample_win, l)[b, 512 - NT:].rearrange("t c k d -> t (c k d)"),
                             S.kv_s[b * NT:b * NT + NT, 512:768]).then_inc(s.stored, 16)
            sp.wait_ge(s.stored, 16 * (3 + NB))


def sample_scores(S, l, ctx):
    nc, io, sb, psum, C = S.nc, S.io, S.sb, S.psum, S.C
    H = lambda t: S.HT[:, t - 6, :]
    S.q_rows = sb("q_rows", [P, P], ctx=ctx)
    S.st_cmp = sb("st_cmp", [P, 2, P], ctx=ctx)
    with stage(nc, "q", "zero", "placed") as (block, s):
        @block.vector
        def _(dve):
            dve.memset(S.q_rows[:, :], 0.0).then_inc(s.zero, 1)
            dve.wait_ge(s.zero, 1)
            rows = S.q_rows[:, :].rearrange("p (b k g t) -> p b k g t", b=NB, k=KVH, g=GRP)
            for k in range(KVH):
                r = slice(64 * k, 64 * k + 64)
                for g in range(GRP):
                    dve.tensor_copy(rows[r, :, k, g, :], H(T_Q + g)[r, SEQ:].rearrange("p (b t) -> p b t", b=NB)).then_inc(s.placed, 1)

    with ExitStack() as c:
        slots, gp = 4, 4
        NG = NPG // gp
        cache = sb("cache", [P, slots, gp, 3 * P], ctx=c)
        chunks = sb("chunks", [P, 2, KVH, 8, NCH], ctx=c)
        kt = sb("kt", [P, 2, gp * P], ctx=c)
        hb = sb("hb", [HD, 2, KVH, NCB], ctx=c)
        hid = sb("hid", [P, 2, NCB], ctx=c)
        kc = sb("kc_s", [P, NCB], ctx=c)
        wk = S.yT[:, 4, 0:4 * P].rearrange("p (j n) -> p j n", n=P)
        wkt = S.yT[:, 5, 0:4 * P]
        names = ("turned", "k_copied", "v_copied", "sel_act", "sel_dve", "scored", "sc_copied", "summed", "half", "added", "swish",
                 "second", "kc_copied", "vc_copied", "cmp_scored", "cmp_copied", "w_turned", "w_copied", "w_scored", "w_sc_copied",
                 "w_loaded", "loaded0", "loaded1", "loaded2", "loaded3")
        with stage(nc, "scores", *names) as (block, s):
            loaded = [s.loaded0, s.loaded1, s.loaded2, s.loaded3]
            hidden_bank = (7, 0)

            def cols(b):
                return ds(b * 16, 16)

            def pairs(bank, k, i):
                return psum[HD * k:HD * k + HD, bank, :].rearrange("p (n j i) -> p i j n", j=8, i=2)[:, i]

            def pairs_to(c, k, i, g):
                return chunks[HD * i:HD * i + HD, c, k, :, g * 32:g * 32 + 32]

            @block.sync
            def _(sp):
                def sequence(b, first):
                    for g in range(NG):
                        if not first or g >= slots:
                            sp.wait_ge(s.turned, b * NG + (g - slots + 1))
                        if g % 2 == 0:
                            numbers = page_numbers(S, mybir.EngineType.SP, b, g * gp, 2 * gp)
                        for j in range(gp):
                            page = numbers[(g % 2) * gp + j]
                            src = layer(io.cache_nsa_kv, l)[ds(page, 1)].rearrange("a t c k d -> (a t) (c k d)")
                            sp.dma_start(cache[:, g % slots, j, :], src[:, 0:3 * P]).then_inc(loaded[g % slots], 16)
                        if g == 0:
                            if not first:
                                sp.wait_ge(s.w_turned, b)
                            src = layer(io.cache_win_kv, l)[ds(b, 1)].rearrange("a (j p) c k d -> p (a j) c (k d)", p=P)
                            sp.dma_start(wk[:, :, :], src[:, :, 0, :]).then_inc(s.w_loaded, 16)

                sequence(0, True)
                with sp.Fori(0, NB - 1) as i:
                    sequence(i + 1, False)

            @block.tensor
            def _(pe):
                def turn(b, g, first):
                    pe.wait_ge(loaded[g % slots], b * (16 * gp * NG // slots) + 16 * gp * (g // slots + 1))
                    if not first or g >= 2:
                        pe.wait_ge(s.k_copied, b * NG + (g - 1))
                        pe.wait_ge(s.v_copied, b * NG + (g - 1))
                        pe.wait_ge(s.sel_dve if g % 2 else s.sel_act, b * (NG // 2) + g // 2)
                    if not first and g == 0:
                        pe.wait_ge(s.added, b * 4 - 2)
                    for c in (2, 0, 1):
                        for j in range(gp):
                            last = pe.transpose(psum[:, 3 * (g % 2) + c, j * P:j * P + P],
                                                cache[:, g % slots, j, c * P:c * P + P], C["ident"])
                    last.then_inc(s.turned, 1)

                def score(b, g, first):
                    if not first and g == 0:
                        pe.wait_ge(s.sc_copied, b)
                    pe.wait_ge(s.sel_dve if g % 2 else s.sel_act, b * (NG // 2) + (g // 2 + 1))
                    for j in range(gp):
                        t = g * gp + j
                        last = pe.matmul(psum[:, 6, t * 16:t * 16 + 16], kt[:, g % 2, j * P:j * P + P], S.q_rows[:, cols(b)],
                                         start=True, stop=True)
                    last.then_inc(s.scored, 1)

                def hidden(b):
                    pe.wait_ge(s.k_copied, b * NG + NG)
                    pe.wait_ge(s.v_copied, b * NG + NG)
                    for c in (1, 0):
                        if c == 0:
                            pe.wait_ge(s.w_sc_copied, b + 1)
                        for j in range(8):
                            last = pe.matmul(psum[:, hidden_bank[c], :], S.W1[:, c, j, :], chunks[:, c, :, j, :],
                                             start=(j == 0), stop=(j == 7))
                        last.then_inc(s.summed, 1)

                def window_turn(b, first):
                    pe.wait_ge(s.w_loaded, b * 16 + 16)
                    if not first:
                        pe.wait_ge(s.cmp_copied, b * 2)
                    for j in range(4):
                        last = pe.transpose(psum[:, 7, j * P:j * P + P], wk[:, j, :], C["ident"])
                    last.then_inc(s.w_turned, 1)

                def window_score(b):
                    pe.wait_ge(s.w_copied, b + 1)
                    for j in range(4):
                        last = pe.matmul(psum[:, 7, j * 16:j * 16 + 16], wkt[:, j * P:j * P + P], S.q_rows[:, cols(b)],
                                         start=True, stop=True)
                    last.then_inc(s.w_scored, 1)

                def second_layer(b):
                    pe.wait_ge(s.swish, b * 2 + 2)
                    pe.matmul(psum[:, 7, 0:NCB], S.W2[:, 0, :], hid[:, 0, :], start=True, stop=True)
                    for j in range(2):
                        m = P - j
                        last = pe.matmul(psum[0:m, 7, (2 + j) * P:(3 + j) * P], hid[:, 1, j * P:j * P + m], S.W2[:, 1, :], start=True, stop=True)
                    last.then_inc(s.second, 1)

                def cmp_score(b):
                    pe.wait_ge(s.kc_copied, b + 1)
                    pe.wait_ge(s.vc_copied, b * 2 + 2)
                    for j in range(2):
                        m = P - j
                        last = pe.matmul(psum[0:m, 7, j * 16:j * 16 + 16], kc[:, j * P:j * P + m], S.q_rows[:, cols(b)],
                                         start=True, stop=True)
                    last.then_inc(s.cmp_scored, 1)

                def sequence(b, before):
                    first = before is None
                    for g in range(NG):
                        turn(b, g, first)
                        if g >= 1:
                            score(b, g - 1, first)
                        if g == 1 and not first:
                            second_layer(before)
                        if g == 2 and not first:
                            cmp_score(before)
                        if g == 3:
                            window_turn(b, first)
                        if g == 4:
                            window_score(b)
                    score(b, NG - 1, first)
                    hidden(b)

                sequence(0, None)
                with pe.Fori(0, NB - 1) as i:
                    sequence(i + 1, i)
                second_layer(NB - 1)
                cmp_score(NB - 1)

            @block.scalar
            def _(act):
                def vc_out(b):
                    act.wait_ge(s.second, b + 1)
                    act.wait_ge(s.kc_copied, b + 1)
                    for j in range(2):
                        m = P - j
                        act.copy(S.vc[0:m, j, ds(b, 1), :].rearrange("p a n -> p (a n)"),
                                 psum[0:m, 7, (2 + j) * P:(3 + j) * P]).then_inc(s.vc_copied, 1)

                def sequence(b, before):
                    first = before is None
                    for g in range(NG):
                        act.wait_ge(s.turned, b * NG + (g + 1))
                        if g % 2 == 0:
                            if not first or g >= 2:
                                act.wait_ge(s.scored, b * NG + (g - 1))
                            act.copy(kt[:, 0, :], psum[:, 2, :]).then_inc(s.sel_act, 1)
                        if not first and g == 0:
                            act.wait_ge(s.summed, b * 2)
                        for k in range(KVH):
                            for i in range(2):
                                last = act.copy(pairs_to(0, k, i, g), pairs(3 * (g % 2), k, i))
                        last.then_inc(s.k_copied, 1)
                        if g == 1 and not first:
                            vc_out(before)
                    for n, c in enumerate((1, 0)):
                        act.wait_ge(s.summed, b * 2 + (n + 1))
                        src = psum[HD:P, hidden_bank[c], :].rearrange("p (k n) -> p k n", k=KVH)[:, :, 1:NCH]
                        act.copy(hb[:, c, :, :], src).then_inc(s.half, 1)
                    for n, c in enumerate((1, 0)):
                        act.wait_ge(s.added, b * 4 + (2 * n + 2))
                        act.activation(hid[:, c, :], hid[:, c, :], ACT.Silu, bias=S.pe_h[:, c:c + 1]).then_inc(s.swish, 1)

                sequence(0, None)
                with act.Fori(0, NB - 1) as i:
                    sequence(i + 1, i)
                vc_out(NB - 1)

            @block.vector
            def _(dve):
                def kc_out(b):
                    dve.wait_ge(s.second, b + 1)
                    dve.tensor_copy(kc[:, :], psum[:, 7, 0:NCB]).then_inc(s.kc_copied, 1)

                def cmp_out(b):
                    dve.wait_ge(s.cmp_scored, b + 1)
                    for j in range(2):
                        m = P - j
                        dve.tensor_copy(S.st_cmp[0:m, j, cols(b)], psum[0:m, 7, j * 16:j * 16 + 16]).then_inc(s.cmp_copied, 1)

                def sequence(b, before):
                    first = before is None
                    for g in range(NG):
                        dve.wait_ge(s.turned, b * NG + (g + 1))
                        if g % 2 == 1:
                            if not first or g >= 2:
                                dve.wait_ge(s.scored, b * NG + (g - 1))
                            dve.tensor_copy(kt[:, 1, :], psum[:, 5, :]).then_inc(s.sel_dve, 1)
                        if not first and g == 0:
                            dve.wait_ge(s.summed, b * 2)
                        for k in range(KVH):
                            for i in range(2):
                                last = dve.tensor_copy(pairs_to(1, k, i, g), pairs(3 * (g % 2) + 1, k, i))
                        last.then_inc(s.v_copied, 1)
                        if g == 1 and not first:
                            kc_out(before)
                        if g == 2 and not first:
                            cmp_out(before)
                        if g == 3:
                            dve.wait_ge(s.w_turned, b + 1)
                            dve.tensor_copy(wkt, psum[:, 7, :]).then_inc(s.w_copied, 1)
                        if g == 4:
                            dve.wait_ge(s.w_scored, b + 1)
                            dve.tensor_copy(S.st_win[:, :, cols(b)], psum[:, 7, 0:64].rearrange("p (t r) -> p t r", r=16)).then_inc(s.w_sc_copied, 1)
                    dve.wait_ge(s.scored, b * NG + NG)
                    dve.tensor_copy(S.st_sel[:, :, cols(b)], psum[:, 6, :].rearrange("p (t r) -> p t r", r=16)).then_inc(s.sc_copied, 1)
                    for n, c in enumerate((1, 0)):
                        dve.wait_ge(s.half, b * 2 + (n + 1))
                        for k in range(KVH):
                            dve.tensor_tensor(hid[HD * k:HD * k + HD, c, :], psum[0:HD, hidden_bank[c], k * NCH:k * NCH + NCB],
                                              hb[:, c, k, :], ALU.add).then_inc(s.added, 1)

                sequence(0, None)
                with dve.Fori(0, NB - 1) as i:
                    sequence(i + 1, i)
                kc_out(NB - 1)
                cmp_out(NB - 1)


def sample_softmax(S, l, ctx):
    nc, io, sb, psum, C = S.nc, S.io, S.sb, S.psum, S.C
    H = lambda t: S.HT[:, t - 6, :]
    NSC = PAST + NS
    near, new, cmp_bias, far = S.sbias[:, 0:128], S.sbias[:, 128:160], S.sbias[:, 160:160 + NCB], S.sbias[:, 415:416]
    by_head = sb("by_head", [P, 3, HEADS], ctx=ctx)
    gate = sb("gate", [P, 3], ctx=ctx)
    stat = sb("stat", [P, 3, 3], ctx=ctx)
    pc = sb("pc", [P, 264], ctx=ctx)
    imp = sb("imp", [P, 2, NBLK + 1], ctx=ctx)
    score = sb("score", [P, 3, NBLK + 1], ctx=ctx)
    top = sb("top", [P, 2, 8], ctx=ctx)
    block_bias = sb("block_bias", [P, NBLK + 1], ctx=ctx)
    diag = sb("diag", [P, 3, P], ctx=ctx)
    pt_cmp, pt_new = S.pt_cmp, S.pt_new
    p_sel = sb("p_sel", [P, NSC], ctx=ctx)
    p_win = sb("p_win", [P, 512 + NS], ctx=ctx)
    pt_sel, pt_win = S.st_sel, S.st_win

    with stage(nc, "top", "g_prod", "g_step", "st_turned", "step", "zero", "added", "maxed", "exped", "pc", "imp", "imp2",
               "bb", "diag", "c_turned", "pt_copied") as (block, s):
        @block.tensor
        def _(pe):
            pe.matmul(psum[:, 0, 0:12], C["s_row"], S.gates[0:NS, QT, :], start=True, stop=True).then_inc(s.g_prod, 1)
            for j in range(2):
                m = P - j
                pe.transpose(psum[:, 1, j * P:j * P + m], S.st_cmp[0:m, j, :], C["ident"][0:m, 0:m]).then_inc(s.st_turned, 1)
            pe.wait_ge(s.imp, 1)
            pe.matmul(psum[:, 2, 0:NBLK + 1], C["pair"], imp[:, 1, :], start=True, stop=True).then_inc(s.imp2, 1)
            pe.wait_ge(s.diag, 1)
            for j in range(2):
                m = P - j
                pe.matmul(psum[0:m, 3, j * P:j * P + P], pc[:, 4 + j * P:4 + j * P + m], diag[:, 0, :], start=True, stop=True).then_inc(s.c_turned, 1)

        @block.scalar
        def _(act):
            act.wait_ge(s.maxed, 1)
            act.activation(pc[:, 4:4 + NCB], pc[:, 4:4 + NCB], ACT.Exp, bias=stat[:, 0, 0:1], accum_out=stat[:, 0, 1:2]).then_inc(s.exped, 1)
            act.wait_ge(s.c_turned, 2)
            for j in range(2):
                m = P - j
                act.copy(pt_cmp[0:m, j, :], psum[0:m, 3, j * P:j * P + P]).then_inc(s.pt_copied, 1)

        @block.vector
        def _(dve):
            step = Serial(dve, s.step)
            dve.memset(pc[:, :], 0.0).then_inc(s.zero, 1)
            dve.wait_ge(s.g_prod, 1)
            heads = bass.AP(C["row_head"].tensor, C["row_head"].offset, [list(C["row_head"].ap[0]), [0, 3], [1, HEADS]])
            step(dve.tensor_tensor(by_head[:, :, :], psum[:, 0, 0:12].rearrange("p (c h) -> p c h", c=3), heads, ALU.mult))
            dve.tensor_reduce(gate[:, :], by_head[:, :, :], AX.X, ALU.add).then_inc(s.g_step, 1)
            dve.wait_ge(s.st_turned, 2)
            dve.wait_ge(s.zero, 1)
            step(dve.tensor_tensor(pc[:, 4:4 + NCB], psum[:, 1, 0:NCB], cmp_bias, ALU.add), s.added)
            dve.tensor_reduce(stat[:, 0, 0:1], pc[:, 4:4 + NCB], AX.X, ALU.max, negate=True).then_inc(s.maxed, 1)
            dve.wait_ge(s.exped, 1)
            step(dve.reciprocal(stat[:, 0, 2:3], stat[:, 0, 1:2]))
            step(dve.tensor_scalar(pc[:, 4:4 + NCB], pc[:, 4:4 + NCB], stat[:, 0, 2:3], None, ALU.mult), s.pc)
            dve.wait_ge(s.g_step, 1)
            dve.tensor_scalar(diag[:, 0, :], C["ident"], gate[:, 0:1], None, ALU.mult).then_inc(s.diag, 1)
            step(dve.tensor_reduce(imp[:, 0, :], pc[:, 4:264].rearrange("p (j n) -> p j n", n=4), AX.X, ALU.add))
            dve.tensor_tensor(imp[:, 1, :], imp[:, 0, :], pc[:, 3:3 + 4 * NBLK + 1:4], ALU.add).then_inc(s.imp, 1)
            dve.wait_ge(s.imp2, 1)
            step(dve.tensor_tensor(score[:, 0, :], psum[:, 2, 0:NBLK + 1], C["force"], ALU.add))
            for r in range(2):
                step(dve.max(top[:, r, :], score[:, r, :]))
                step(dve.match_replace(score[:, r + 1, :], top[:, r, :], score[:, r, :], NEG))
            step(dve.tensor_scalar(block_bias[:, :], score[:, 2, :], 0.1 * NEG, NEG, ALU.is_gt, ALU.mult))
            dve.tensor_scalar(block_bias[:, :], block_bias[:, :], far, None, ALU.add).then_inc(s.bb, 1)

    NQ = NPG // 4
    with stage(nc, "soft", "turned", "added", "new_scored", "new_added", "w_step", "maxed", "exped", "step", "diag", "pt_turned",
               "pt_copied") as (block, s):
        @block.tensor
        def _(pe):
            for q in range(NQ + 1):
                if q >= 4:
                    pe.wait_ge(s.added, q - 3)
                src = S.st_sel if q < NQ else S.st_win
                for j in range(4):
                    last = pe.transpose(psum[:, q % 4, j * P:j * P + P], src[:, (4 * q + j) if q < NQ else j, :], C["ident"])
                last.then_inc(s.turned, 1)
            pe.matmul(psum[:, 4, 0:NS], S.q_rows[:, :], H(T_KV + 2)[:, SEQ:], start=True, stop=True).then_inc(s.new_scored, 1)
            pe.matmul(psum[:, 5, 0:NS], S.q_rows[:, :], H(T_KV + 4)[:, SEQ:], start=True, stop=True).then_inc(s.new_scored, 1)
            pe.wait_ge(s.added, NQ + 1)
            for q in range(NQ + 2):
                if q >= 4:
                    pe.wait_ge(s.pt_copied, q - 3)
                br = 1 if q == NQ else 0
                pe.wait_ge(s.diag, 2 if q >= NQ else 1)
                if q <= NQ:
                    for j in range(4):
                        x = p_sel[:, (4 * q + j) * P:(4 * q + j + 1) * P] if q < NQ else p_win[:, j * P:j * P + P]
                        last = pe.matmul(psum[:, q % 4, j * P:j * P + P], x, diag[:, 1 + br, :], start=True, stop=True)
                else:
                    pe.matmul(psum[0:NS, q % 4, 0:P], p_sel[:, PAST:], diag[:, 1, :], start=True, stop=True)
                    last = pe.matmul(psum[0:NS, q % 4, P:2 * P], p_win[:, 512:], diag[:, 2, :], start=True, stop=True)
                last.then_inc(s.pt_turned, 1)

        @block.vector
        def _(dve):
            step = Serial(dve, s.step)
            for q in range(NQ):
                dve.wait_ge(s.turned, q + 1)
                dve.tensor_tensor(p_sel[:, 512 * q:512 * q + 512].rearrange("p (j n) -> p j n", n=64),
                                  psum[:, q % 4, :].rearrange("p (j n) -> p j n", n=64), bc(block_bias[:, 8 * q:8 * q + 8], 64),
                                  ALU.add).then_inc(s.added, 1)
            dve.wait_ge(s.turned, NQ + 1)
            dve.tensor_scalar(p_win[:, 0:512], psum[:, NQ % 4, :], far, None, ALU.add).then_inc(s.added, 1)
            dve.wait_ge(s.new_scored, 2)
            dve.tensor_tensor(p_sel[:, PAST:], psum[:, 4, 0:NS], new, ALU.add).then_inc(s.new_added, 1)
            dve.tensor_tensor(p_win[:, 512:], psum[:, 5, 0:NS], new, ALU.add).then_inc(s.new_added, 1)
            dve.wait_ge(s.added, NQ + 1)
            dve.tensor_tensor(p_sel[:, PAST - P:PAST], p_sel[:, PAST - P:PAST], near, ALU.add).then_inc(s.new_added, 1)
            dve.tensor_tensor(p_win[:, 384:512], p_win[:, 384:512], near, ALU.add).then_inc(s.new_added, 1)
            dve.tensor_tensor(p_win[:, 0:NT], p_win[:, 0:NT], C["win_old"], ALU.add).then_inc(s.new_added, 1)
            dve.wait_ge(s.new_added, 5)
            dve.tensor_reduce(stat[:, 1, 0:1], p_sel[:, :], AX.X, ALU.max, negate=True).then_inc(s.maxed, 1)
            dve.tensor_reduce(stat[:, 2, 0:1], p_win[:, :], AX.X, ALU.max, negate=True).then_inc(s.maxed, 1)
            for br in (1, 2):
                dve.wait_ge(s.exped, br)
                step(dve.reciprocal(stat[:, br, 2:3], stat[:, br, 1:2]))
                step(dve.tensor_tensor(stat[:, br, 2:3], stat[:, br, 2:3], gate[:, br:br + 1], ALU.mult))
                dve.tensor_scalar(diag[:, br, :], C["ident"], stat[:, br, 2:3], None, ALU.mult).then_inc(s.diag, 1)
            for q in range(1, NQ + 2, 2):
                dve.wait_ge(s.pt_turned, q + 1)
                dst = pt_sel[:, 4 * q:4 * q + 4, :] if q < NQ else pt_new[:, :, :]
                src = psum[:, q % 4, :] if q < NQ else psum[0:NS, q % 4, 0:2 * P]
                dve.wait_ge(s.pt_copied, q)
                dve.tensor_copy(dst, src.rearrange("p (t n) -> p t n", n=P)).then_inc(s.pt_copied, 1)

        @block.scalar
        def _(act):
            act.wait_ge(s.maxed, 1)
            act.activation(p_sel[:, :], p_sel[:, :], ACT.Exp, bias=stat[:, 1, 0:1], accum_out=stat[:, 1, 1:2]).then_inc(s.exped, 1)
            act.wait_ge(s.maxed, 2)
            act.activation(p_win[:, :], p_win[:, :], ACT.Exp, bias=stat[:, 2, 0:1], accum_out=stat[:, 2, 1:2]).then_inc(s.exped, 1)
            for q in range(0, NQ + 1, 2):
                act.wait_ge(s.pt_turned, q + 1)
                if q:
                    act.wait_ge(s.pt_copied, q)
                dst = pt_sel[:, 4 * q:4 * q + 4, :] if q < NQ else pt_win[:, :, :]
                act.copy(dst, psum[:, q % 4, :].rearrange("p (t n) -> p t n", n=P)).then_inc(s.pt_copied, 1)


def attention_outputs(S, l, ctx):
    nc, io, sb, psum, C = S.nc, S.io, S.sb, S.psum, S.C
    H = lambda t: S.HT[:, t - 6, :]
    kvn, kc, vc = S.kvn, S.kc_p, S.vc_p
    strip = sb("strip", [P, HEADS, STRIP], ctx=ctx)
    half = NPG // 2
    vsel = sb("vsel", [P, 2, half, P], ctx=ctx)
    vwin = sb("vwin", [P, 4, P], ctx=ctx)
    o_s = sb("o_s", [16, NB, P], ctx=ctx)
    units = [(i, h, br) for i in range(QT) for h in range(HEADS) for br in range(3)]
    N = len(units)
    sc = sb("sc", [P, 3, 512], ctx=ctx)
    pt = sb("pt", [P, 3, 512], ctx=ctx)
    nmax = sb("nmax", [P, N], ctx=ctx)
    esum = sb("esum", [P, N], ctx=ctx)
    coef = sb("coef", [P, N], ctx=ctx)
    o = sb("o", [P, QT, 256], ctx=ctx)
    names = ("scored", "added", "step", "maxed", "exped", "turned", "pt_copied", "pv", "summed", "coef", "o_turned", "o_copied",
             "strip", "pages0", "pages1", "pages_act0", "pages_act1", "window", "part", "s_copied", "s_turned", "placed")
    with stage(nc, "att", *names) as (block, s):
        pages, pages_act = (s.pages0, s.pages1), (s.pages_act0, s.pages_act1)
        by_sp = 12
        lag = 4

        def width(n):
            i, h, br = units[n]
            return 31 if br == 0 else P * (i + 1)

        def fetch(eng, kind, b, h, first_page, loaded):
            for j, page in enumerate(page_numbers(S, kind, b, half * h + first_page, 4)):
                src = layer(io.cache_nsa_kv, l)[ds(page, 1)].rearrange("a t c k d -> (a t) (c k d)")
                eng.dma_start(vsel[:, h, first_page + j, :], src[:, 3 * P:4 * P]).then_inc(loaded, 16)

        @block.sync
        def _(sp):
            def sequence(b, first):
                for h in range(2):
                    if not first:
                        sp.wait_ge(s.part, b * 2 + (h - 1))
                    if h == 0:
                        src = layer(io.cache_win_kv, l)[ds(b, 1)].rearrange("a (j p) c k d -> p (a j) c (k d)", p=P)
                        sp.dma_start(vwin[:, :, :], src[:, :, 1, :]).then_inc(s.window, 16)
                    for first_page in range(0, by_sp, 4):
                        fetch(sp, mybir.EngineType.SP, b, h, first_page, pages[h])

            src = bass.AP(io.line_dram.tensor, 127, [[LINE - 1, P], [P * LINE, HEADS], [1, STRIP]])
            sp.dma_start(strip[:, :, :], src).then_inc(s.strip, 16)
            sequence(0, True)
            with sp.Fori(0, NB - 1) as i:
                sequence(i + 1, False)

        @block.tensor
        def _(pe):
            def sample_third(n):
                part, third = n // 3, n % 3
                b, h = part // 2, part % 2
                cols = slice(16 * b, 16 * b + 16)
                o = psum[0:16, 6 + b % 2, 0:P]
                if h == 0 and third == 0:
                    if b >= 2:
                        pe.wait_ge(s.s_copied, b - 1)
                    pe.matmul(o, S.pt_new[:, 0, cols], S.kv_s[:, 3 * P:4 * P], start=True, stop=False)
                    pe.matmul(o, S.pt_new[:, 1, cols], S.kv_s[:, 5 * P:6 * P], start=False, stop=False)
                    for j in range(2):
                        m = P - j
                        pe.matmul(o, S.pt_cmp[0:m, j, cols], S.vc[0:m, j, b, :], start=False, stop=False)
                    pe.wait_ge(s.window, 16 * b + 16)
                    for j in range(4):
                        pe.matmul(o, S.st_win[:, j, cols], vwin[:, j, :], start=False, stop=False)
                if third == 0:
                    pe.wait_ge(pages[h], 16 * by_sp * (b + 1))
                    pe.wait_ge(pages_act[h], 16 * (half - by_sp) * (b + 1))
                for t in range(half * third // 3, half * (third + 1) // 3):
                    last = pe.matmul(o, S.st_sel[:, half * h + t, cols], vsel[:, h, t, :], start=False, stop=(h == 1 and t == half - 1))
                if third == 2:
                    last.then_inc(s.part, 1)

            def scores(n):
                i, h, br = units[n]
                r = slice(64 * (h // GRP), 64 * (h // GRP) + 64)
                keys = kc[r, :] if br == 0 else H(T_KV + 2 * br)[r, 0:P * (i + 1)]
                if n >= 2:
                    pe.wait_ge(s.added, n - 1)
                pe.matmul(psum[:, n % 2, 0:width(n)], H(T_Q + h % GRP)[r, i * P:i * P + P], keys,
                          start=True, stop=True).then_inc(s.scored, 1)

            def turn(n):
                pe.wait_ge(s.exped, n + 1)
                if n >= 2:
                    pe.wait_ge(s.pt_copied, n - 1)
                w = width(n)
                for j in range(0, w, P):
                    m = min(P, w - j)
                    last = pe.transpose(psum[0:m, 2 + n % 2, j:j + P], sc[:, n % 3, j:j + m], C["ident"])
                last.then_inc(s.turned, 1)

            def values(n):
                i, h, br = units[n]
                k = 64 * (h // GRP)
                pe.wait_ge(s.pt_copied, n + 1)
                if n >= 2:
                    pe.wait_ge(s.summed, n - 1)
                if br == 0:
                    last = pe.matmul(psum[:, 4 + n % 2, 0:HD], pt[0:31, n % 3, 0:P], vc[:, k:k + HD], start=True, stop=True)
                else:
                    for j in range(i + 1):
                        c = (2 * br + 1) * P + k
                        last = pe.matmul(psum[:, 4 + n % 2, 0:HD], pt[:, n % 3, j * P:j * P + P], kvn[:, j, c:c + HD],
                                         start=(j == 0), stop=(j == i))
                last.then_inc(s.pv, 1)

            for n in range(N + 2):
                if n < N:
                    scores(n)
                if 1 <= n <= N:
                    if n > lag:
                        sample_third(n - 1 - lag)
                    turn(n - 1)
                if n >= 2:
                    values(n - 2)
            for n in range(N - lag, N):
                sample_third(n)
            pe.wait_ge(s.summed, N)
            pe.wait_ge(s.s_copied, NB)
            for b in range(NB):
                last = pe.transpose(psum[:, 7, 16 * b:16 * b + 16], o_s[:, b, :], C["ident"][0:16, 0:16])
            last.then_inc(s.s_turned, 1)
            for i in range(QT):
                for c in range(2):
                    last = pe.transpose(psum[:, (6, 0)[c], i * P:i * P + P], o[:, i, c * P:c * P + P], C["ident"])
            last.then_inc(s.o_turned, 1)

        @block.scalar
        def _(act):
            def copy_out(b):
                act.wait_ge(s.part, 2 * b + 2)
                act.copy(o_s[:, b, :], psum[0:16, 6 + b % 2, 0:P]).then_inc(s.s_copied, 1)

            def fetch_rest(part):
                if part >= 2:
                    act.wait_ge(s.part, part - 1)
                fetch(act, mybir.EngineType.Activation, part // 2, part % 2, by_sp, pages_act[part % 2])

            fetch_rest(0)
            fetch_rest(1)
            for n in range(N + 1):
                if n - lag + 1 in range(6, 6 * NB, 3):
                    fetch_rest((n - lag + 1) // 3)
                if n < N:
                    act.wait_ge(s.maxed, n + 1)
                    x = sc[:, n % 3, 0:width(n)]
                    act.activation(x, x, ACT.Exp, bias=nmax[:, n:n + 1], accum_out=esum[:, n:n + 1]).then_inc(s.exped, 1)
                if n - lag - 2 in range(6, 6 * NB, 6):
                    copy_out((n - lag - 2) // 6 - 1)
                if n >= 1:
                    m = n - 1
                    act.wait_ge(s.turned, m + 1)
                    if m >= 3:
                        act.wait_ge(s.pv, m - 2)
                    w = 31 if width(m) == 31 else P
                    x = slice(0, P if w == 31 else width(m))
                    act.copy(pt[0:w, m % 3, x], psum[0:w, 2 + m % 2, x]).then_inc(s.pt_copied, 1)
            for b in range((N - lag - 2) // 6, NB):
                copy_out(b)
            act.wait_ge(s.o_turned, 1)
            for c in range(2):
                act.copy(S.yT[:, 4 + c, 0:SEQ], psum[:, (6, 0)[c], :]).then_inc(s.o_copied, 1)

        @block.vector
        def _(dve):
            step = Serial(dve, s.step)
            dve.wait_ge(s.strip, 16)
            for n in range(N + 2):
                if n < N:
                    i, h, br = units[n]
                    w = width(n)
                    x0 = 415 - P * i if br == 0 else 384 - P * i
                    bias = strip[:, h, x0:x0 + 481:16] if br == 0 else strip[:, h, x0:512]
                    x = sc[:, n % 3, 0:w]
                    dve.wait_ge(s.scored, n + 1)
                    if n >= 3:
                        dve.wait_ge(s.turned, n - 2)
                    step(dve.tensor_tensor(x, psum[:, n % 2, 0:w], bias, ALU.add), s.added)
                    step(dve.tensor_reduce(nmax[:, n:n + 1], x, AX.X, ALU.max, negate=True))
                    dve.tensor_scalar(nmax[:, n:n + 1], nmax[:, n:n + 1], -0.01 * NEG, None, ALU.min).then_inc(s.maxed, 1)
                if 1 <= n <= N:
                    m = n - 1
                    c = coef[:, m:m + 1]
                    dve.wait_ge(s.exped, m + 1)
                    step(dve.tensor_scalar(c, esum[:, m:m + 1], 1e-30, None, ALU.max))
                    step(dve.reciprocal(c, c))
                    i, h, br = units[m]
                    step(dve.tensor_tensor(c, c, S.gates[:, i, 4 * br + h:4 * br + h + 1], ALU.mult))
                if n >= 2:
                    m = n - 2
                    i, h, br = units[m]
                    out, src = o[:, i, h * HD:h * HD + HD], psum[:, 4 + m % 2, 0:HD]
                    dve.wait_ge(s.pv, m + 1)
                    if br == 0:
                        dve.tensor_scalar(out, src, coef[:, m:m + 1], None, ALU.mult).then_inc(s.summed, 1)
                    else:
                        dve.wait_ge(s.summed, m)
                        dve.scalar_tensor_tensor(out, src, coef[:, m:m + 1], out, ALU.mult, ALU.add).then_inc(s.summed, 1)
            dve.wait_ge(s.s_turned, 1)
            rows = psum[:, 7, 0:P].rearrange("p (b k g t) -> p b k g t", b=NB, k=KVH, g=GRP)
            for k in range(KVH):
                for g in range(GRP):
                    dve.tensor_copy(S.yT[64 * g:64 * g + 64, 4 + k, SEQ:].rearrange("p (b t) -> p b t", b=NB),
                                    rows[64 * k:64 * k + 64, :, k, g, :]).then_inc(s.placed, 1)


def gated_delta(S, l, ctx):
    nc, io, sb, psum, C = S.nc, S.io, S.sb, S.psum, S.C
    H = lambda t: S.HT[:, t - 6, :]
    ident = C["ident"]
    NQ = QT + 1
    rows = [P] * QT + [NS]
    upto = [C["upto"]] * QT + [C["s_upto"]]
    total = [C["ones"]] * QT + [C["s_ones"]]
    after = [C["after"]] * QT + [C["s_after"]]
    a_b = sb("a_log_b", [P, HEADS], ctx=ctx)
    dt_b = sb("dt_bias_b", [P, HEADS], ctx=ctx)
    taps = S.gtaps
    nat = sb("gnat", [P, NQ, 768], ctx=ctx)
    g = sb("g", [P, NQ, HEADS], ctx=ctx)
    beta = sb("beta", [P, NQ, HEADS], ctx=ctx)
    with ExitStack() as c:
        stp = sb("stp", [GC - 1, 768], ctx=c)
        sts = sb("sts", [24, 768], ctx=c)
        sq = sb("gsq", [P, NQ, 512], ctx=c)
        rn = sb("rn", [P, NQ, 8], ctx=c)
        sp_ = sb("softplus", [P, 3, NQ, HEADS], ctx=c)
        names = ("loaded", "turned", "copied", "stored", "n_turned", "n_act", "n_dve", "squared",
                 "rsum", "rn", "a_sum", "act_step", "soft", "beta", "step", "normed")
        with stage(nc, "gnorm", *names) as (block, s):
            @block.sync
            def _(sp):
                for dst, src in ((a_b, io.gdn_a_log), (dt_b, io.gdn_dt_bias)):
                    row = src[ds(l, 1)]
                    sp.dma_start(dst[:, :], bass.AP(row.tensor, row.offset, [[0, P], [1, HEADS]])).then_inc(s.loaded, 16)
                sp.wait_ge(s.copied, 2)
                sp.dma_start(layer(io.prompt_gconv, l)[0], stp[:, :]).then_inc(s.stored, 16)
                sp.dma_start(layer(io.sample_gconv, l).rearrange("b w c -> (b w) c"), sts[:, :]).then_inc(s.stored, 16)
                sp.wait_ge(s.stored, 32)

            @block.tensor
            def _(pe):
                for j in range(6):
                    at = slice(P * (j % 4), P * (j % 4) + P)
                    pe.transpose(psum[0:GC - 1, 4 + j // 4, at], S.gtail[:, j, 0:GC - 1], ident)
                    last = pe.transpose(psum[0:24, 6 + j // 4, at], S.gtail[:, j, GC - 1:], ident)
                last.then_inc(s.turned, 1)
                for q in range(NQ):
                    n, a = rows[q], 2 * (q % 2)
                    if q >= 2:
                        pe.wait_ge(s.n_act, q - 1)
                        pe.wait_ge(s.n_dve, q - 1)
                    for j in range(6):
                        last = pe.transpose(psum[0:n, a + j // 4, (j % 4) * P:(j % 4) * P + P], H(T_GDN + j)[:, q * P:q * P + n], ident)
                    last.then_inc(s.n_turned, 1)

            @block.scalar
            def _(act):
                step = Serial(act, s.act_step)
                act.wait_ge(s.a_sum, 1)
                step(act.activation(sp_[:, 1, :, :], sp_[:, 0, :, :], ACT.Abs))
                step(act.activation(sp_[:, 1, :, :], sp_[:, 1, :, :], ACT.Exp, scale=-1.0))
                step(act.activation(a_b[:, :], a_b[:, :], ACT.Exp))
                act.activation(sp_[:, 1, :, :], sp_[:, 1, :, :], ACT.Ln, bias=C["ones"][:, 0:1]).then_inc(s.soft, 1)
                act.activation(beta[:, :, :], S.misc_n[:, :, M_B:M_B + 4], ACT.Sigmoid).then_inc(s.beta, 1)
                for j in range(2):
                    act.activation(H(T_Z + j), H(T_Z + j), ACT.Silu).then_inc(s.beta, 1)
                for q in range(NQ):
                    n = rows[q]
                    act.wait_ge(s.n_turned, q + 1)
                    act.copy(nat[0:n, q, 0:512], psum[0:n, 2 * (q % 2), :]).then_inc(s.n_act, 1)
                    act.wait_ge(s.n_act, q + 1)
                    act.activation(sq[0:n, q, :], nat[0:n, q, 0:512], ACT.Square).then_inc(s.squared, 1)
                act.wait_ge(s.turned, 1)
                act.copy(stp[:, 0:512], psum[0:GC - 1, 4, :])
                act.copy(stp[:, 512:768], psum[0:GC - 1, 5, 0:256]).then_inc(s.copied, 1)
                act.copy(sts[:, 0:512], psum[0:24, 6, :])
                act.copy(sts[:, 512:768], psum[0:24, 7, 0:256]).then_inc(s.copied, 1)
                act.wait_ge(s.rsum, 2)
                step(act.activation(rn[:, :, :], rn[:, :, :], ACT.Ln, bias=C["eps"][:, 1:2]))
                act.activation(rn[:, :, :], rn[:, :, :], ACT.Exp, scale=-0.5).then_inc(s.rn, 1)

            @block.vector
            def _(dve):
                step = Serial(dve, s.step)
                dve.wait_ge(s.loaded, 32)
                dve.tensor_tensor(sp_[:, 0, :, :], S.misc_n[:, :, M_A:M_A + 4], bc_mid(dt_b[:, :], NQ), ALU.add).then_inc(s.a_sum, 1)
                dve.wait_ge(s.soft, 1)
                step(dve.tensor_scalar(sp_[:, 0, :, :], sp_[:, 0, :, :], 0.0, None, ALU.max))
                step(dve.tensor_tensor(sp_[:, 0, :, :], sp_[:, 0, :, :], sp_[:, 1, :, :], ALU.add))
                step(dve.tensor_tensor(sp_[:, 0, :, :], sp_[:, 0, :, :], bc_mid(a_b[:, :], NQ), ALU.mult))
                step(dve.tensor_scalar(g[:, :, :], sp_[:, 0, :, :], -1.0, None, ALU.mult))
                dve.memset(rn[:, QT, :], 1.0).then_inc(s.rsum, 1)
                for q in range(NQ):
                    n = rows[q]
                    dve.wait_ge(s.n_turned, q + 1)
                    dve.tensor_copy(nat[0:n, q, 512:768], psum[0:n, 2 * (q % 2) + 1, 0:256]).then_inc(s.n_dve, 1)
                for q in range(NQ):
                    n = rows[q]
                    dve.wait_ge(s.squared, q + 1)
                    dve.wait_ge(s.rsum, 1)
                    last = dve.tensor_reduce(rn[0:n, q, :], sq[0:n, q, :].rearrange("p (j n) -> p j n", n=HD), AX.X, ALU.add)
                last.then_inc(s.rsum, 1)
                dve.wait_ge(s.rn, 1)
                step(dve.tensor_scalar(rn[:, :, 0:4], rn[:, :, 0:4], HD ** -0.5, None, ALU.mult))
                for q in range(NQ):
                    n = rows[q]
                    x = nat[0:n, q, 0:512].rearrange("p (j n) -> p j n", n=HD)
                    dve.tensor_tensor(x, x, bc(rn[0:n, q, :], HD), ALU.mult).then_inc(s.normed, 1)

    DTs = lambda t, q: t[0:rows[q], q, :, 0:rows[q]]
    lt = sb("lt", [P, NQ, HEADS, P], ctx=ctx)
    qk = sb("qk", [P, NQ, HEADS, P], ctx=ctx)
    inv_t = sb("inv_t", [P, NQ, HEADS, P], ctx=ctx)
    inv = sb("inv", [P, NQ, HEADS, P], ctx=ctx)
    uw = sb("uw", [P, NQ, HEADS, P], ctx=ctx)
    kl = sb("kl", [P, NQ, HEADS, HD], ctx=ctx)
    qs = sb("qs", [HD, NQ, HEADS, P], ctx=ctx)
    glast = sb("glast", [HD, HEADS, QT + NB], ctx=ctx)
    with ExitStack() as c:
        gb = sb("gb", [P, NQ, HEADS, P], ctx=c)
        egb = sb("egb", [HD, HEADS, P], ctx=c)
        dec = sb("dec", [P, HEADS, P], ctx=c)
        kT = sb("kT", [HD, HEADS, P], ctx=c)
        kbT = sb("kbT", [HD, HEADS, P], ctx=c)
        qT = sb("qT", [HD, HEADS, P], ctx=c)
        kb = sb("kb", [P, NQ, HEADS, HD], ctx=c)
        gc = sb("gc", [P, NQ, 5, HEADS], ctx=c)
        names = ("gb", "cum", "cumb", "gcum", "rest", "neg", "exp", "egb", "dec0", "dec", "dstep", "kb", "nats", "turned", "t_copied",
                 "qt", "qs", "products", "lt", "qk")
        with stage(nc, "gmat", *names) as (block, s):
            @block.tensor
            def _(pe):
                def decays(q):
                    n = rows[q]
                    pe.wait_ge(s.gb, q + 1)
                    if q:
                        pe.wait_ge(s.gcum, q)
                    if q >= 2:
                        pe.wait_ge(s.dec0, q - 1)
                        pe.wait_ge(s.egb, q - 1)
                    pe.matmul(psum[0:n, 0, 0:4], upto[q], g[0:n, q, :], start=True, stop=True)
                    pe.matmul(psum[0:n, 0, 4:8], total[q], g[0:n, q, :], start=True, stop=True).then_inc(s.cum, 1)
                    for h in range(HEADS):
                        last = pe.matmul(psum[:, (1, 7)[q % 2], h * P:h * P + n], gb[0:n, q, h, :], upto[q], start=True, stop=True)
                    last.then_inc(s.cumb, 1)

                def turn(q):
                    n = rows[q]
                    pe.wait_ge(s.kb, q + 1)
                    if q:
                        pe.wait_ge(s.t_copied, 3 * q)
                    for i, src in enumerate((lambda h: nat[0:n, q, 256 + h * HD:320 + h * HD], lambda h: kb[0:n, q, h, :],
                                             lambda h: nat[0:n, q, h * HD:h * HD + HD])):
                        for h in range(HEADS):
                            last = pe.transpose(psum[0:HD, 2 + i, h * P:h * P + n], src(h), ident[0:n, 0:n])
                        last.then_inc(s.turned, 1)

                def products(q):
                    n = rows[q]
                    pe.wait_ge(s.t_copied, 3 * q + 3)
                    if q:
                        pe.wait_ge(s.qk, q)
                    for h in range(HEADS):
                        pe.matmul(psum[0:n, 5, h * P:h * P + n], kT[:, h, 0:n], kbT[:, h, 0:n], start=True, stop=True)
                        last = pe.matmul(psum[0:n, 6, h * P:h * P + n], kT[:, h, 0:n], qT[:, h, 0:n], start=True, stop=True)
                    last.then_inc(s.products, 1)

                decays(0)
                turn(0)
                for q in range(NQ):
                    if q + 1 < NQ:
                        decays(q + 1)
                    products(q)
                    if q + 1 < NQ:
                        turn(q + 1)

            def heads(bank, n, m):
                return psum[0:n, bank, :].rearrange("p (h m) -> p h m", h=HEADS)[:, :, 0:m]

            @block.scalar
            def _(act):
                for q in range(NQ):
                    n = rows[q]
                    act.wait_ge(s.rest, q + 1)
                    act.activation(gc[0:n, q, 3:5, :], gc[0:n, q, 3:5, :], ACT.Exp).then_inc(s.exp, 1)
                    act.wait_ge(s.dec0, q + 1)
                    if q:
                        act.wait_ge(s.qs, q)
                    act.activation(egb[:, :, 0:n], heads((1, 7)[q % 2], HD, n), ACT.Exp).then_inc(s.egb, 1)
                    for h in range(HEADS):
                        last = act.activation(dec[0:n, h, 0:n], dec[0:n, h, 0:n], ACT.Exp, bias=gc[0:n, q, 2, h:h + 1])
                    last.then_inc(s.dec, 1)
                    for i, dst in enumerate((kT, kbT, qT)):
                        act.wait_ge(s.turned, 3 * q + i + 1)
                        if q and i == 0:
                            act.wait_ge(s.products, q)
                            act.wait_ge(s.qs, q)
                        act.copy(dst[:, :, 0:n], heads(2 + i, HD, n)).then_inc(s.t_copied, 1)

            @block.vector
            def _(dve):
                def spread(q):
                    n = rows[q]
                    dve.tensor_copy(gb[0:n, q, :, :], bc(g[0:n, q, :], P)).then_inc(s.gb, 1)
                    k = nat[0:n, q, 256:512].rearrange("p (h d) -> p h d", h=HEADS)
                    dve.tensor_tensor(kb[0:n, q, :, :], k, bc(beta[0:n, q, :], HD), ALU.mult).then_inc(s.kb, 1)

                def sums(q):
                    n = rows[q]
                    dve.wait_ge(s.cum, q + 1)
                    dve.tensor_copy(gc[0:n, q, 0:2, :], psum[0:n, 0, 0:8].rearrange("p (c h) -> p c h", c=2)).then_inc(s.gcum, 1)
                    dve.wait_ge(s.gcum, q + 1)
                    dve.tensor_copy(gc[0:n, q, 3, :], gc[0:n, q, 0, :])
                    dve.tensor_scalar(gc[0:n, q, 2, :], gc[0:n, q, 0, :], -1.0, None, ALU.mult)
                    dve.tensor_tensor(gc[0:n, q, 4, :], gc[0:n, q, 1, :], gc[0:n, q, 0, :], ALU.subtract).then_inc(s.rest, 1)

                for q in range(NQ):
                    n = rows[q]
                    k = nat[0:n, q, 256:512].rearrange("p (h d) -> p h d", h=HEADS)
                    v = nat[0:n, q, 512:768].rearrange("p (h d) -> p h d", h=HEADS)
                    if q == 0:
                        spread(0)
                    if q + 1 < NQ:
                        spread(q + 1)
                    dve.tensor_tensor(uw[0:n, q, :, 0:HD], v, bc(beta[0:n, q, :], HD), ALU.mult).then_inc(s.nats, 1)
                    if q == 0:
                        sums(0)
                    dve.wait_ge(s.cumb, q + 1)
                    if q:
                        dve.wait_ge(s.qk, q)
                    dve.tensor_tensor(dec[0:n, :, 0:n], heads((1, 7)[q % 2], n, n), bc_mid(after[q], HEADS), ALU.add).then_inc(s.dec0, 1)
                    if q + 1 < NQ:
                        sums(q + 1)
                    dve.wait_ge(s.exp, q + 1)
                    dve.wait_ge(s.kb, q + 1)
                    dve.tensor_tensor(uw[0:n, q, :, HD:], kb[0:n, q, :, :], bc(gc[0:n, q, 3, :], HD), ALU.mult).then_inc(s.nats, 1)
                    dve.tensor_tensor(kl[0:n, q, :, :], k, bc(gc[0:n, q, 4, :], HD), ALU.mult).then_inc(s.nats, 1)
                    dve.wait_ge(s.egb, q + 1)
                    if q < QT:
                        dve.tensor_copy(glast[:, :, q], egb[:, :, P - 1])
                    else:
                        dve.tensor_copy(glast[:, :, QT:], egb[:, :, NT - 1:NS:NT])
                    dve.wait_ge(s.t_copied, 3 * q + 3)
                    dve.tensor_tensor(qs[:, q, :, 0:n], qT[:, :, 0:n], egb[:, :, 0:n], ALU.mult).then_inc(s.qs, 1)
                    dve.wait_ge(s.products, q + 1)
                    dve.wait_ge(s.dec, q + 1)
                    dve.tensor_tensor(DTs(lt, q), heads(5, n, n), dec[0:n, :, 0:n], ALU.mult).then_inc(s.lt, 1)
                    dve.tensor_tensor(DTs(qk, q), heads(6, n, n), dec[0:n, :, 0:n], ALU.mult).then_inc(s.qk, 1)

    with ExitStack() as c:
        lm = sb("lm", [P, 2, HEADS, P], ctx=c)
        y = sb("y", [P, 2, HEADS, P], ctx=c)
        units = [(v, q) for v in range(1, 7) for q in range(NQ) if q < QT or v < 2]
        N = len(units)
        at = {u: n for n, u in enumerate(units)}
        with stage(nc, "ginv", "first", "first_t", "turned", "t_copied", "lm", "y", "y_copied", "delta", "updated", "step") as (block, s):
            def bank(b, q):
                return psum[0:rows[q], b, :].rearrange("p (h m) -> p h m", h=HEADS)[:, :, 0:rows[q]]

            @block.tensor
            def _(pe):
                for q in range(NQ):
                    n = rows[q]
                    pe.wait_ge(s.first_t, q + 1)
                    if q >= 2:
                        pe.wait_ge(s.t_copied, q - 1)
                    for h in range(HEADS):
                        last = pe.transpose(psum[0:n, 6 + q % 2, h * P:h * P + n], inv_t[0:n, q, h, 0:n], ident[0:n, 0:n])
                    last.then_inc(s.turned, 1)

                def lower(m):
                    v, q = units[m]
                    n = rows[q]
                    pe.wait_ge(s.lm, m + 1)
                    if v == 1:
                        pe.wait_ge(s.t_copied, q + 1)
                    else:
                        pe.wait_ge(s.updated, at[(v - 1, q)] + 1)
                    if m >= 2:
                        pe.wait_ge(s.y_copied, m - 1)
                    for h in range(HEADS):
                        last = pe.matmul(psum[0:n, m % 2, h * P:h * P + n], lm[0:n, m % 2, h, 0:n], inv[0:n, q, h, 0:n], start=True, stop=True)
                    last.then_inc(s.y, 1)

                def delta(m):
                    v, q = units[m]
                    n = rows[q]
                    pe.wait_ge(s.y_copied, m + 1)
                    if m >= 2:
                        pe.wait_ge(s.updated, m - 1)
                    for h in range(HEADS):
                        if (v + 1, q) in at:
                            pe.matmul(psum[0:n, 2 + m % 2, h * P:h * P + n], inv_t[0:n, q, h, 0:n], y[0:n, m % 2, h, 0:n], start=True, stop=True)
                        last = pe.matmul(psum[0:n, 4 + m % 2, h * P:h * P + n], y[0:n, m % 2, h, 0:n], inv_t[0:n, q, h, 0:n], start=True, stop=True)
                    last.then_inc(s.delta, 1)

                for m in range(N + 1):
                    if m < N:
                        lower(m)
                    if m:
                        delta(m - 1)

            @block.gpsimd
            def _(pool):
                for m, (v, q) in enumerate(units):
                    n = rows[q]
                    if m >= 2:
                        pool.wait_ge(s.y, m - 1)
                    pool.tensor_tensor(lm[0:n, m % 2, :, 0:n], DTs(lt, q), bc_mid(C[f"level{v}"][0:n, 0:n], HEADS), ALU.mult).then_inc(s.lm, 1)

            @block.scalar
            def _(act):
                for q in range(NQ):
                    act.wait_ge(s.turned, q + 1)
                    act.copy(DTs(inv, q), bank(6 + q % 2, q)).then_inc(s.t_copied, 1)
                for m, (v, q) in enumerate(units):
                    n = rows[q]
                    act.wait_ge(s.y, m + 1)
                    if m >= 2:
                        act.wait_ge(s.delta, m - 1)
                    act.copy(y[0:n, m % 2, :, 0:n], bank(m % 2, q)).then_inc(s.y_copied, 1)

            @block.vector
            def _(dve):
                for q in range(NQ):
                    n = rows[q]
                    dve.tensor_tensor(DTs(inv_t, q), DTs(lt, q), bc_mid(C["level0"][0:n, 0:n], HEADS), ALU.mult).then_inc(s.first, 1)
                    dve.wait_ge(s.first, q + 1)
                    dve.tensor_tensor(DTs(inv_t, q), bc_mid(ident[0:n, 0:n], HEADS), DTs(inv_t, q), ALU.subtract).then_inc(s.first_t, 1)
                for m, (v, q) in enumerate(units):
                    dve.wait_ge(s.delta, m + 1)
                    if (v + 1, q) in at:
                        dve.tensor_tensor(DTs(inv, q), DTs(inv, q), bank(2 + m % 2, q), ALU.subtract)
                    dve.tensor_tensor(DTs(inv_t, q), DTs(inv_t, q), bank(4 + m % 2, q), ALU.subtract).then_inc(s.updated, 1)

    wT = sb("wT", [HD, NQ, HEADS, P], ctx=ctx)
    state = sb("state", [HD, HEADS, HD], ctx=ctx)
    fade = sb("fade", [HD, HEADS, HD], ctx=ctx)
    vnew = sb("vnew", [P, HEADS, HD], ctx=ctx)
    st_s = sb("st_s", [HD, HEADS, NB, HD], ctx=ctx)
    fade_s = sb("fade_s", [HD, NB, HD], ctx=ctx)
    own = sb("own", [NS, NB, HD], ctx=ctx)
    ws = sb("ws", [NS, 2, HEADS, HD], ctx=ctx)
    vb = sb("vb", [NS, HEADS, NB, HD], ctx=ctx)
    rr = sb("rr", [P, NQ, HEADS], ctx=ctx)
    o = lambda q: nat[0:rows[q], q, 0:256].rearrange("p (h d) -> p h d", h=HEADS)
    uv = lambda q: nat[0:rows[q], q, 256:512].rearrange("p (h d) -> p h d", h=HEADS)
    with stage(nc, "guv", "w_out", "loaded", "uv", "uv_copied", "wt_copied") as (block, s):
        @block.sync
        def _(sp):
            for h in range(HEADS):
                sp.dma_start(st_s[:, h, :, :], layer(io.state_gdn, l)[:, h].rearrange("b k v -> k b v")).then_inc(s.loaded, 16)
            load_out(S, l, sp, 0, 0, s.w_out)
            sp.wait_ge(s.loaded, 64)
            sp.wait_ge(s.w_out, 16)

        @block.tensor
        def _(pe):
            for q in range(NQ):
                n = rows[q]
                if q >= 2:
                    pe.wait_ge(s.uv_copied, q - 1)
                    pe.wait_ge(s.wt_copied, q - 1)
                for h in range(HEADS):
                    pe.matmul(psum[0:n, 2 * (q % 2), h * HD:h * HD + HD], inv_t[0:n, q, h, 0:n], uw[0:n, q, h, 0:HD], start=True, stop=True)
                    last = pe.matmul(psum[0:HD, 2 * (q % 2) + 1, h * P:h * P + n], uw[0:n, q, h, HD:], inv_t[0:n, q, h, 0:n], start=True, stop=True)
                last.then_inc(s.uv, 1)

        @block.vector
        def _(dve):
            for q in range(NQ):
                dve.wait_ge(s.uv, q + 1)
                dve.tensor_copy(uv(q), psum[0:rows[q], 2 * (q % 2), 0:256].rearrange("p (h d) -> p h d", h=HEADS)).then_inc(s.uv_copied, 1)

        @block.scalar
        def _(act):
            for q in range(NQ):
                act.wait_ge(s.uv, q + 1)
                src = psum[0:HD, 2 * (q % 2) + 1, :].rearrange("p (h m) -> p h m", h=HEADS)[:, :, 0:rows[q]]
                act.copy(wT[:, q, :, 0:rows[q]], src).then_inc(s.wt_copied, 1)

    names = ("ws", "vnew", "out", "o_copied", "kv", "fade", "state", "s_w", "s_own", "s_ws", "s_vnew", "s_vb", "s_fade", "s_out",
             "s_kv", "s_state", "s_o", "o_done", "stored", "squared", "rsum", "astep", "rr", "normed", "turned", "yt", "zero", "ystep")
    with stage(nc, "gscan", *names) as (block, s):
        def squares(q):
            return uw[0:rows[q], q, 0:2, :].rearrange("p a b -> p (a b)")

        bank4 = lambda b, n: psum[0:n, b, 0:256].rearrange("p (h d) -> p h d", h=HEADS)

        @block.tensor
        def _(pe):
            for q in range(QT):
                pe.wait_ge(s.zero if q == 0 else s.state, max(q, 1))
                if q:
                    pe.wait_ge(s.o_copied, q)
                for h in range(HEADS):
                    last = pe.matmul(psum[:, 0, h * HD:h * HD + HD], wT[:, q, h, :], state[:, h, :], start=True, stop=True)
                last.then_inc(s.ws, 1)
                for n in (2 * q, 2 * q + 1):
                    left, h = (wT, qs)[n // HEADS], n % HEADS
                    if n >= 2:
                        pe.wait_ge(s.s_own, n - 1)
                    pe.matmul(psum[0:NS, 3 + n % 2, :], left[:, QT, h, 0:NS], st_s[:, h, :, :].rearrange("p b v -> p (b v)"),
                              start=True, stop=True).then_inc(s.s_w, 1)
                pe.wait_ge(s.vnew, q + 1)
                for h in range(HEADS):
                    last = pe.matmul(psum[0:HD, 2, h * HD:h * HD + HD], kl[:, q, h, :], vnew[:, h, :], start=True, stop=True)
                last.then_inc(s.kv, 1)
                for h in range(HEADS):
                    out = psum[:, 1, h * HD:h * HD + HD]
                    pe.matmul(out, qs[:, q, h, :], state[:, h, :], start=True, stop=False)
                    last = pe.matmul(out, qk[:, q, h, :], vnew[:, h, :], start=False, stop=True)
                last.then_inc(s.out, 1)
            pe.wait_ge(s.s_vnew, 1)
            for h in range(HEADS):
                last = pe.matmul(psum[0:NS, 5, h * HD:h * HD + HD], qk[0:NS, QT, h, 0:NS], vnew[0:NS, h, :], start=True, stop=True)
            last.then_inc(s.s_out, 1)
            for h in range(HEADS):
                pe.wait_ge(s.s_vb, h + 1)
                if h >= 2:
                    pe.wait_ge(s.s_state, h - 1)
                pe.matmul(psum[0:HD, 6 + h % 2, :], kl[0:NS, QT, h, :], vb[:, h, :, :].rearrange("p b v -> p (b v)"),
                          start=True, stop=True).then_inc(s.s_kv, 1)
            pe.wait_ge(s.normed, NQ)
            pe.wait_ge(s.o_copied, QT)
            for q in range(NQ):
                n = rows[q]
                for c in range(2):
                    bankc = (0 if q < QT else 2) + c
                    last = pe.transpose(psum[:, bankc, (q % 4) * P:(q % 4) * P + n], nat[0:n, q, c * P:c * P + P], ident[0:n, 0:n])
            last.then_inc(s.turned, 1)

        @block.gpsimd
        def _(pool):
            pool.memset(state[:, :, :], 0.0).then_inc(s.zero, 1)

        @block.scalar
        def _(act):
            for q in range(QT):
                act.wait_ge(s.out, q + 1)
                act.copy(o(q), bank4(1, P)).then_inc(s.o_copied, 1)
            act.wait_ge(s.o_copied, QT)
            for q in range(QT):
                act.activation(squares(q), nat[:, q, 0:256], ACT.Square).then_inc(s.squared, 1)
            act.wait_ge(s.s_o, 1)
            act.activation(squares(QT), nat[0:NS, QT, 0:256], ACT.Square).then_inc(s.squared, 1)
            act.wait_ge(s.rsum, 2)
            act.activation(rr[:, :, :], rr[:, :, :], ACT.Ln, bias=C["eps"][:, 0:1], scale=1 / HD).then_inc(s.astep, 1)
            act.wait_ge(s.astep, 1)
            act.activation(rr[:, :, :], rr[:, :, :], ACT.Exp, scale=-0.5).then_inc(s.rr, 1)

        @block.vector
        def _(dve):
            def keep_own(n):
                dve.wait_ge(s.s_w, n + 1)
                if n:
                    dve.wait_ge(s.s_ws, n)
                dve.tensor_tensor(own[:, :, :], psum[0:NS, 3 + n % 2, :].rearrange("p (b v) -> p b v", b=NB), bc(C["s_batch"], HD),
                                  ALU.mult).then_inc(s.s_own, 1)
                dve.wait_ge(s.s_own, n + 1)
                dve.tensor_reduce(ws[:, n // HEADS, n % HEADS, :], own[:, :, :].rearrange("p b v -> p v b"), AX.X, ALU.add).then_inc(s.s_ws, 1)

            for q in range(QT):
                dve.wait_ge(s.ws, q + 1)
                dve.tensor_tensor(vnew[:, :, :], uv(q), bank4(0, P), ALU.subtract).then_inc(s.vnew, 1)
                dve.wait_ge(s.zero if q == 0 else s.state, max(q, 1))
                dve.tensor_tensor(fade[:, :, :], state[:, :, :], bc(glast[:, :, q], HD), ALU.mult).then_inc(s.fade, 1)
                for n in (2 * q, 2 * q + 1):
                    keep_own(n)
                dve.wait_ge(s.fade, q + 1)
                dve.wait_ge(s.out, q + 1)
                dve.tensor_tensor(state[:, :, :], fade[:, :, :], bank4(2, HD), ALU.add).then_inc(s.state, 1)
            dve.wait_ge(s.s_ws, 2 * HEADS)
            dve.tensor_tensor(vnew[0:NS, :, :], uv(QT), ws[:, 0, :, :], ALU.subtract).then_inc(s.s_vnew, 1)
            dve.wait_ge(s.s_vnew, 1)
            for h in range(HEADS):
                v = vnew[0:NS, h, :].unsqueeze(1).broadcast_to([NS, NB, HD])
                dve.tensor_tensor(vb[:, h, :, :], v, bc(C["s_batch"], HD), ALU.mult).then_inc(s.s_vb, 1)
            dve.wait_ge(s.s_out, 1)
            dve.wait_ge(s.s_ws, 8)
            dve.tensor_tensor(o(QT), bank4(5, NS), ws[:, 1, :, :], ALU.add).then_inc(s.s_o, 1)
            for h in range(HEADS):
                if h:
                    dve.wait_ge(s.s_state, h)
                dve.wait_ge(s.s_w, 8)
                dve.tensor_tensor(fade_s[:, :, :], st_s[:, h, :, :], bc(glast[:, h, QT:], HD), ALU.mult).then_inc(s.s_fade, 1)
                dve.wait_ge(s.s_fade, h + 1)
                dve.wait_ge(s.s_kv, h + 1)
                dve.tensor_tensor(st_s[:, h, :, :], fade_s[:, :, :], psum[0:HD, 6 + h % 2, :].rearrange("p (b v) -> p b v", b=NB),
                                  ALU.add).then_inc(s.s_state, 1)
            dve.memset(rr[:, QT, :], 1.0).then_inc(s.rsum, 1)
            dve.wait_ge(s.rsum, 1)
            for q in range(NQ):
                dve.wait_ge(s.squared, q + 1)
                last = dve.tensor_reduce(rr[0:rows[q], q, :], squares(q).rearrange("p (h d) -> p h d", h=HEADS), AX.X, ALU.add)
            last.then_inc(s.rsum, 1)
            dve.wait_ge(s.rr, 1)
            for q in range(NQ):
                dve.tensor_tensor(o(q), o(q), bc(rr[0:rows[q], q, :], HD), ALU.mult).then_inc(s.normed, 1)
            dve.wait_ge(s.turned, 1)
            for c in range(2):
                for b, t in ((c, slice(0, SEQ)), (2 + c, slice(SEQ, TOK))):
                    n = t.stop - t.start
                    dve.scalar_tensor_tensor(S.yT[:, 6 + c, t], psum[:, b, 0:n], taps[:, 0, 4:5], H(T_Z + c)[:, t],
                                             ALU.mult, ALU.mult).then_inc(s.yt, 1)

        @block.sync
        def _(sp):
            sp.wait_ge(s.state, QT)
            sp.dma_start(layer(io.prompt_gdn, l)[0].rearrange("h k v -> k h v"), state[:, :, :]).then_inc(s.stored, 16)
            sp.wait_ge(s.s_state, HEADS)
            for h in range(HEADS):
                sp.dma_start(layer(io.sample_gdn, l)[:, h].rearrange("b k v -> k b v"), st_s[:, h, :, :]).then_inc(s.stored, 16)
            sp.wait_ge(s.stored, 80)


def layer_norm(S, l, ctx, gain, bias, name, preload=None):
    nc, sb, psum, C, xT = S.nc, S.sb, S.psum, S.C, S.xT
    row = sb(name + "_row", [2, D], ctx=ctx)
    col = sb(name + "_col", [P, KT, 2], ctx=ctx)
    sq = sb(name + "_sq", [P, KT, TOK], ctx=ctx)
    rstd = sb(name + "_rstd", [P, TOK], ctx=ctx)
    with stage(nc, "ln", "next", "summed_pool", "summed_dve", "loaded", "turned", "copied", "mean", "centred", "squared", "var", "ln", "rstd", "normed", "done") as (block, s):
        @block.sync
        def _(sp):
            sp.dma_start(row[0:1, :], gain[ds(l, 1)]).then_inc(s.loaded, 16)
            sp.dma_start(row[1:2, :], bias[ds(l, 1)]).then_inc(s.loaded, 16)
            if preload:
                preload(sp, s.next)
                sp.wait_ge(s.next, 16)

        @block.gpsimd
        def _(pool):
            for k in range(1, KT // 2):
                pool.wait_ge(s.squared, k + 1)
                if k > 1:
                    pool.wait_ge(s.summed_pool, k - 1)
                pool.tensor_tensor(sq[:, 0, :], sq[:, 0, :], sq[:, k, :], ALU.add).then_inc(s.summed_pool, 1)

        @block.tensor
        def _(pe):
            for h in range(2):
                last = pe.matmul(psum[:, h, 0:HALF], C["mean_d"], S.xsum[:, h * HALF:(h + 1) * HALF], start=True, stop=True)
            last.then_inc(s.mean, 1)
            pe.wait_ge(s.loaded, 32)
            for k in range(KT):
                last = pe.transpose(psum[:, 4, 2 * k:2 * k + 2], row[:, k * P:k * P + P], C["ident"][0:2, 0:2])
            last.then_inc(s.turned, 1)
            pe.wait_ge(s.summed_dve, KT // 2)
            for h in range(2):
                last = pe.matmul(psum[:, 2 + h, 0:HALF], C["mean_d"], sq[:, KT // 2, h * HALF:(h + 1) * HALF], start=True, stop=True)
            last.then_inc(s.var, 1)

        @block.vector
        def _(dve):
            dve.wait_ge(s.mean, 1)
            for k in range(KT):
                dve.tensor_tensor(halves(xT[:, k, :]), halves(xT[:, k, :]), psum[:, 0:2, 0:HALF], ALU.subtract).then_inc(s.centred, 1)
            half = KT // 2
            for k in range(half + 1, KT):
                dve.wait_ge(s.squared, k + 1)
                if k > half + 1:
                    dve.wait_ge(s.summed_dve, k - half - 1)
                dve.tensor_tensor(sq[:, half, :], sq[:, half, :], sq[:, k, :], ALU.add).then_inc(s.summed_dve, 1)
            dve.wait_ge(s.summed_dve, half - 1)
            dve.wait_ge(s.summed_pool, half - 1)
            dve.tensor_tensor(sq[:, half, :], sq[:, half, :], sq[:, 0, :], ALU.add).then_inc(s.summed_dve, 1)
            dve.wait_ge(s.centred, KT)
            dve.wait_ge(s.rstd, 1)
            for k in range(KT):
                dve.tensor_tensor(xT[:, k, :], xT[:, k, :], rstd[:, :], ALU.mult).then_inc(s.normed, 1)

        @block.scalar
        def _(act):
            for k in range(KT):
                act.wait_ge(s.centred, k + 1)
                act.activation(sq[:, k, :], xT[:, k, :], ACT.Square).then_inc(s.squared, 1)
            act.wait_ge(s.turned, 1)
            act.copy(col[:, :, :], psum[:, 4, 0:2 * KT].rearrange("p (k n) -> p k n", n=2)).then_inc(s.copied, 1)
            act.wait_ge(s.var, 1)
            act.activation(halves(rstd[:, :]), psum[:, 2:4, 0:HALF], ACT.Ln, bias=C["eps"][:, 0:1]).then_inc(s.ln, 1)
            act.wait_ge(s.ln, 1)
            act.activation(rstd[:, :], rstd[:, :], ACT.Exp, scale=-0.5).then_inc(s.rstd, 1)
            act.wait_ge(s.copied, 1)
            for k in range(KT):
                act.wait_ge(s.normed, k + 1)
                act.activation(xT[:, k, :], xT[:, k, :], ACT.Identity, bias=col[:, k, 1:2], scale=col[:, k, 0:1]).then_inc(s.done, 1)


def sum_tiles(S, pool, s):
    for t in range(KT):
        pool.wait_ge(s.taken_dve, t + 1)
        if t == 1:
            pool.tensor_tensor(S.xsum[:, :], S.xT[:, 0, :], S.xT[:, 1, :], ALU.add).then_inc(s.added, 1)
        elif t:
            pool.wait_ge(s.added, t - 1)
            pool.tensor_tensor(S.xsum[:, :], S.xsum[:, :], S.xT[:, t, :], ALU.add).then_inc(s.added, 1)


def add_residual(S):
    def evac(dve, t, src, s):
        return dve.scalar_tensor_tensor(halves(S.xT[:, t, :]), halves(S.xT[:, t, :]), ALPHA, src, ALU.mult, ALU.add)
    return evac


def out_ring(S):
    return S.HT[:, :, :].rearrange("p a b -> p (a b)")[:, 0:3 * KT * 256].rearrange("p (s k n) -> p s k n", s=3, k=KT)


def load_out(S, l, sp, g, slot, sem):
    w_out = layer(S.io.w_out, l).rearrange("(k p) n -> p k n", p=P)
    sp.dma_start(out_ring(S)[:, slot, :, :], w_out[:, :, g * 256:g * 256 + 256]).then_inc(sem, 16)


def project_out(S, l, ctx):
    ring = out_ring(S)
    w_up = layer(S.io.w_up, l).rearrange("(k p) n -> p k n", p=P)

    def load(sp, g, slot, sem):
        load_out(S, l, sp, g, slot, sem)

    def first_up(sp, sem):
        sp.dma_start(S.up_ring[:, 0, :, :], w_up[:, :, 0:256]).then_inc(sem, 16)

    dense(S, "out", (3, 2, load, lambda g: 1), KT, lambda k: S.yT[:, k, :],
          lambda t, k: ring[:, (t // 2) % 3, k, (t % 2) * P:(t % 2) * P + P], KT, None, add_residual(S), ready=1,
          more={"gpsimd": lambda pool, s: sum_tiles(S, pool, s)}, more_names=("added",))
    layer_norm(S, l, ctx, S.io.ln1_g, S.io.ln1_b, "ln1", first_up)


def feed_forward(S, l, ctx):
    sb, io, xT = S.sb, S.io, S.xT
    FT = DFF // P
    w_up = layer(io.w_up, l).rearrange("(k p) n -> p k n", p=P)
    w_down = layer(io.w_down, l).rearrange("(k p) n -> p k n", p=P)
    with ExitStack() as c:
        f = sb("ff", [P, FT, TOK], ctx=c)
        n = FT * P
        ht, yt = (x[:, :, :].rearrange("p a b -> p (a b)") for x in (S.HT, S.yT))
        down = [x.rearrange("p (k n) -> p k n", k=FT) for x in (ht[:, 0:n], ht[:, n:2 * n], yt[:, 0:n])]

        def first_down(act, sem):
            act.dma_start(down[0], w_down[:, :, 0:P]).then_inc(sem, 16)
            return 1

        with ExitStack() as c2:
            ring = S.up_ring
            pos = sb("pos", [P, TOK], ctx=c2)

            def load_up(sp, g, slot, sem):
                sp.dma_start(ring[:, slot, :, :], w_up[:, :, g * 256:g * 256 + 256]).then_inc(sem, 16)

            def squared_dve(dve, t, src, s):
                dve.tensor_scalar(halves(f[:, t, :]), src, 0.0, None, ALU.max).then_inc(s.rect_dve, 1)
                dve.wait_ge(s.rect_dve, t // 2 + 1)
                return dve.tensor_tensor(f[:, t, :], f[:, t, :], f[:, t, :], ALU.mult)

            def squared_act(act, t, src, s):
                if t > 1:
                    act.wait_ge(s.taken_act, t // 2)
                act.activation(halves(pos[:, :]), src, ACT.Relu).then_inc(s.rect_act, 1)
                act.wait_ge(s.rect_act, t // 2 + 1)
                return act.activation(f[:, t, :], pos[:, :], ACT.Square)

            dense(S, "up", (3, 2, load_up, lambda g: 1), KT, lambda k: xT[:, k, :],
                  lambda t, k: ring[:, (t // 2) % 3, k, (t % 2) * P:(t % 2) * P + P], FT, squared_act, squared_dve, beside=first_down, ready=1)

        def load_down(sp, g, slot, sem):
            sp.dma_start(down[slot], w_down[:, :, g * P:g * P + P]).then_inc(sem, 16)

        dense(S, "down", (3, 1, load_down, lambda g: 1), FT, lambda k: f[:, k, :],
              lambda t, k: down[t % 3][:, k, :], KT, None, add_residual(S), ready=1,
          more={"gpsimd": lambda pool, s: sum_tiles(S, pool, s)}, more_names=("added",))
    layer_norm(S, l, ctx, io.ln2_g, io.ln2_b, "ln2")


def store_outputs(S):
    nc, io = S.nc, S.io
    with ExitStack() as c:
        y = S.sb("y_out", [P, QT + 1, D], ctx=c)
        with stage(nc, "y", "turned", "copied", "stored") as (block, s):
            @block.tensor
            def _(pe):
                for q in range(QT + 1):
                    n = P if q < QT else NS
                    if q >= 4:
                        pe.wait_ge(s.copied, q - 3)
                    for k in range(KT):
                        last = pe.transpose(S.psum[0:n, 2 * (q % 4) + k // 4, (k % 4) * P:(k % 4) * P + P],
                                            S.xT[:, k, q * P:q * P + n], S.C["ident"])
                    last.then_inc(s.turned, 1)

            @block.vector
            def _(dve):
                for q in range(QT + 1):
                    n = P if q < QT else NS
                    dve.wait_ge(s.turned, q + 1)
                    dve.tensor_copy(y[0:n, q, :].rearrange("p (b n) -> p b n", b=2),
                                    S.psum[0:n, 2 * (q % 4):2 * (q % 4) + 2, :]).then_inc(s.copied, 1)

            @block.sync
            def _(sp):
                for q in range(QT + 1):
                    sp.wait_ge(s.copied, q + 1)
                    dst = io.y_prompt[0, q * P:q * P + P, :] if q < QT else io.y_sample.rearrange("b t n -> (b t) n")
                    sp.dma_start(dst, y[0:P if q < QT else NS, q, :]).then_inc(s.stored, 16)
                sp.wait_ge(s.stored, 16 * (QT + 1))


OUTS = [("y_prompt", (1, SEQ, D)), ("y_sample", (NB, NT, D)),
        ("prompt_nsa", (DEPTH, SEQ // PAGE, PAGE, 4, KVH, HD)), ("prompt_win", (DEPTH, 1, SEQ, 2, KVH, HD)),
        ("prompt_conv", (DEPTH, 1, CW - 1, 256)), ("prompt_pool", (DEPTH, 1, PBUF, 256)),
        ("prompt_gconv", (DEPTH, 1, GC - 1, 768)), ("prompt_gdn", (DEPTH, 1, HEADS, HD, HD)),
        ("sample_nsa", (DEPTH, NB, NT, 4, KVH, HD)), ("sample_win", (DEPTH, NB, 512, 2, KVH, HD)),
        ("sample_conv", (DEPTH, NB, CW - 1, 256)), ("sample_pool", (DEPTH, NB, PBUF, 256)),
        ("sample_gconv", (DEPTH, NB, GC - 1, 768)), ("sample_gdn", (DEPTH, NB, HEADS, HD, HD))]


def kernel(**inputs):
    import concourse.bacc as bacc
    from concourse.bass_utils import run_bass_kernel_spmd

    nc = bacc.Bacc("TRN2", target_bir_lowering=False, num_devices=1)
    arrays, args = {}, {}
    io = Named(args)
    args["n_pool"] = inputs["cache_nsa_kv"].shape[1]
    table, where = pack_tables()
    for name, a in list(inputs.items()) + [("cst", table)]:
        a = np.ascontiguousarray(a)
        arrays[f"in_{name}"] = a
        args[name] = nc.dram_tensor(f"in_{name}", a.shape, mybir.dt.from_np(a.dtype), kind="ExternalInput").ap()
    for name, shape in OUTS:
        args[name] = nc.dram_tensor(f"out_{name}", shape, F32, kind="ExternalOutput").ap()
    args["line_dram"] = nc.dram_tensor("line_dram", (HEADS, P, LINE), F32, kind="Internal").ap()
    build(nc, io, where)
    r = run_bass_kernel_spmd(nc, [arrays], core_ids=[0])
    return tuple(r.results[0][f"out_{name}"] for name, _ in OUTS)
```
